# Optimizing a Trainium2 kernel written in Bass

```python
import math
import jax, jax.numpy as jnp
from jax import lax
import numpy as np

D_MODEL = 1024
BATCH = 1
SEQ = 512
DEPTH = 1
DEC_BATCH = 8
DEC_SEQ = 4
PAST_LEN = 2048
PAGE_SIZE = 128

HEAD_DIM = 64
D_ATT = D_MODEL
N_ATT_HEADS = D_ATT // HEAD_DIM
D_SSM = D_MODEL
N_SSM_HEADS = D_SSM // HEAD_DIM
N_SSM_GROUPS = 2
D_STATE = 128
CONV_WIDTH = 4
CONV_DIM = D_SSM + 2 * N_SSM_GROUPS * D_STATE
SSD_CHUNK = 128
D_MIX = D_ATT + D_SSM
DILATED_CONFIGS = ((128, 1), (512, 4), (2048, 16))
MAX_WINDOW = 2048
ATT_BLOCK = 128
PEER_HEADS = 8
PEER_NKEYS = 128
PEER_EXPERTS = PEER_NKEYS * PEER_NKEYS
PEER_TOPK = 16
PEER_DKEY = 256
PEER_BLOCK = 128
LN_EPS = 1e-5
RMS_EPS = 1e-5
ALPHA = (2 * DEPTH) ** 0.25
BETA = (8 * DEPTH) ** -0.25
Q_OFF = 0
K_OFF = D_ATT
V_OFF = 2 * D_ATT
Z_OFF = 3 * D_ATT
XBC_OFF = Z_OFF + D_SSM
DT_OFF = XBC_OFF + CONV_DIM
N_IN = DT_OFF + N_SSM_HEADS

kernel_name = 'hybrid_ssd_dilated_peer_step'

def layer_norm(x, g, b):
    xf = x.astype(jnp.float32)
    mu = xf.mean(-1, keepdims=True)
    var = jnp.square(xf - mu).mean(-1, keepdims=True)
    return ((xf - mu) * lax.rsqrt(var + LN_EPS) * g.astype(jnp.float32) + b.astype(jnp.float32)).astype(x.dtype)

def alibi_slopes():
    return 2.0 ** (-8.0 * jnp.arange(1, N_ATT_HEADS + 1, dtype=jnp.float32) / N_ATT_HEADS)

def dilated_band_attention(q, k, v, window, dil, slopes):
    b, s, h, e = q.shape
    span = window // dil
    unit = dil * ATT_BLOCK
    s_pad = -(-s // unit) * unit
    nblk = s_pad // unit

    def to_blocks(a):
        a = jnp.pad(a, ((0, 0), (0, s_pad - s), (0, 0), (0, 0)))
        return a.reshape(b, nblk, ATT_BLOCK, dil, h, e)

    def with_prev(a):
        prev = jnp.concatenate([jnp.zeros_like(a[:, :1]), a[:, :-1]], axis=1)
        return jnp.concatenate([prev, a], axis=2)

    qb, kb, vb = to_blocks(q), to_blocks(k), to_blocks(v)
    kc, vc = with_prev(kb), with_prev(vb)
    sc = jnp.einsum('bnirhe,bnjrhe->bnrhij', qb, kc).astype(jnp.float32) * (e ** -0.5)
    qi = jnp.arange(ATT_BLOCK)[:, None]
    kj = jnp.arange(2 * ATT_BLOCK)[None, :]
    back = ATT_BLOCK + qi - kj
    key_m = jnp.arange(nblk)[:, None, None] * ATT_BLOCK + kj[None] - ATT_BLOCK
    valid = (back >= 0) & (back <= span) & (key_m >= 0)
    bias = -slopes[:, None, None] * (back * dil).astype(jnp.float32)
    sc = jnp.where(valid[:, None, None], sc + bias, -jnp.inf)
    lse = jax.nn.logsumexp(sc, axis=-1)
    p = jnp.exp(sc - lse[..., None]).astype(v.dtype)
    o = jnp.einsum('bnrhij,bnjrhe->bnirhe', p, vc).reshape(b, s_pad, h, e)[:, :s]
    lse = lse.transpose(0, 1, 4, 2, 3).reshape(b, s_pad, h)[:, :s]
    return o, lse

def dilated_gather_attention(q, k_all, v_all, window, dil, slopes):
    b, t, h, e = q.shape
    past = k_all.shape[1] - t
    span = window // dil
    steps = jnp.arange(span + 1)
    idx = past + jnp.arange(t)[:, None] - steps[None, :] * dil
    valid = idx >= 0
    idx = jnp.maximum(idx, 0)
    kg = k_all[:, idx]
    vg = v_all[:, idx]
    sc = jnp.einsum('bthe,btjhe->bhtj', q, kg).astype(jnp.float32) * (e ** -0.5)
    sc = sc - slopes[:, None, None] * (steps * dil).astype(jnp.float32)
    sc = jnp.where(valid, sc, -jnp.inf)
    lse = jax.nn.logsumexp(sc, axis=-1)
    p = jnp.exp(sc - lse[..., None]).astype(v_all.dtype)
    o = jnp.einsum('bhtj,btjhe->bthe', p, vg)
    return o, lse.transpose(0, 2, 1)

def mix_dilations(results):
    dtype = results[0][0].dtype
    outs = jnp.stack([o for o, _ in results]).astype(jnp.float32)
    lses = jnp.stack([l for _, l in results])
    wts = jax.nn.softmax(lses, axis=0)
    o = jnp.einsum('cblh,cblhe->blhe', wts, outs)
    b, L, h, e = o.shape
    return o.reshape(b, L, h * e).astype(dtype)

def causal_dwconv(x_ext, w, bias):
    c = x_ext.shape[-1]
    rhs = jnp.transpose(w)[:, None, :].astype(x_ext.dtype)
    y = lax.conv_general_dilated(x_ext, rhs, (1,), 'VALID',
                                 dimension_numbers=('NWC', 'WIO', 'NWC'), feature_group_count=c)
    return y + bias

def ssd_scan(x, dt, A, Bm, Cm, D, h0, chunk):
    b, L, H, P = x.shape
    G, N = Bm.shape[2], Bm.shape[3]
    HG = H // G
    nc = L // chunk
    xc = x.astype(jnp.float32).reshape(b, nc, chunk, G, HG, P)
    dtc = dt.astype(jnp.float32).reshape(b, nc, chunk, G, HG)
    Bc = Bm.astype(jnp.float32).reshape(b, nc, chunk, G, N)
    Cc = Cm.astype(jnp.float32).reshape(b, nc, chunk, G, N)
    acs = jnp.cumsum(dtc * A.reshape(G, HG), axis=2)
    causal = jnp.tril(jnp.ones((chunk, chunk), dtype=bool))
    seg = acs[:, :, :, None] - acs[:, :, None, :]
    decay = jnp.exp(jnp.where(causal[:, :, None, None], seg, -jnp.inf))
    cb = jnp.einsum('bcign,bcjgn->bcijg', Cc, Bc)
    y = jnp.einsum('bcijgh,bcjghp->bcighp', cb[..., None] * decay * dtc[:, :, None], xc)
    to_end = jnp.exp(acs[:, :, -1:] - acs) * dtc
    states = jnp.einsum('bclgn,bclghp->bcghpn', Bc, xc * to_end[..., None])
    chunk_decay = jnp.exp(acs[:, :, -1])

    def step(hc, inp):
        st, dec = inp
        return hc * dec[..., None, None] + st, hc

    h_last, h_in = lax.scan(step, h0.astype(jnp.float32).reshape(b, G, HG, P, N),
                            (jnp.moveaxis(states, 1, 0), jnp.moveaxis(chunk_decay, 1, 0)))
    h_in = jnp.moveaxis(h_in, 0, 1)
    y = y + jnp.einsum('bclgn,bcghpn->bclghp', Cc, h_in) * jnp.exp(acs)[..., None]
    y = y + xc * D.astype(jnp.float32).reshape(G, HG)[:, :, None]
    return y.reshape(b, L, H, P), h_last.reshape(b, H, P, N)

def gated_rmsnorm(y, z, g):
    b, L = z.shape[:2]
    gs = D_SSM // N_SSM_GROUPS
    u = y.reshape(b, L, N_SSM_GROUPS, gs) * jax.nn.silu(z.astype(jnp.float32)).reshape(b, L, N_SSM_GROUPS, gs)
    u = u * lax.rsqrt(jnp.mean(u * u, axis=-1, keepdims=True) + RMS_EPS)
    return (u.reshape(b, L, D_SSM) * g.astype(jnp.float32)).astype(z.dtype)

def hybrid_mixer(h, w_in, conv_w, conv_b, dt_bias, a_log, d_skip, ssm_norm_g, w_out, slopes, hist):
    bsz, L, _ = h.shape
    proj = h @ w_in
    q = proj[..., Q_OFF:K_OFF].reshape(bsz, L, N_ATT_HEADS, HEAD_DIM)
    k = proj[..., K_OFF:V_OFF].reshape(bsz, L, N_ATT_HEADS, HEAD_DIM)
    v = proj[..., V_OFF:Z_OFF].reshape(bsz, L, N_ATT_HEADS, HEAD_DIM)
    z = proj[..., Z_OFF:XBC_OFF]
    xbc = proj[..., XBC_OFF:DT_OFF]
    dt_raw = proj[..., DT_OFF:N_IN]
    if hist is None:
        k_all, v_all = k, v
        conv_ext = jnp.pad(xbc, ((0, 0), (CONV_WIDTH - 1, 0), (0, 0)))
        h0 = jnp.zeros((bsz, N_SSM_HEADS, HEAD_DIM, D_STATE), jnp.float32)
        chunk = SSD_CHUNK
        att = [dilated_band_attention(q, k, v, w, d, slopes) for w, d in DILATED_CONFIGS]
    else:
        k_buf, v_buf, conv_buf, h0 = hist
        k_all = jnp.concatenate([k_buf, k], axis=1)
        v_all = jnp.concatenate([v_buf, v], axis=1)
        conv_ext = jnp.concatenate([conv_buf, xbc], axis=1)
        chunk = L
        att = [dilated_gather_attention(q, k_all, v_all, w, d, slopes) for w, d in DILATED_CONFIGS]
    att_out = mix_dilations(att)
    xbc_c = jax.nn.silu(causal_dwconv(conv_ext, conv_w, conv_b))
    gn = N_SSM_GROUPS * D_STATE
    xs = xbc_c[..., :D_SSM].reshape(bsz, L, N_SSM_HEADS, HEAD_DIM)
    Bm = xbc_c[..., D_SSM:D_SSM + gn].reshape(bsz, L, N_SSM_GROUPS, D_STATE)
    Cm = xbc_c[..., D_SSM + gn:].reshape(bsz, L, N_SSM_GROUPS, D_STATE)
    dt = jax.nn.softplus(dt_raw.astype(jnp.float32) + dt_bias.astype(jnp.float32))
    A = -jnp.exp(a_log.astype(jnp.float32))
    y, h_last = ssd_scan(xs, dt, A, Bm, Cm, d_skip, h0, chunk)
    ssm_out = gated_rmsnorm(y, z, ssm_norm_g)
    out = jnp.concatenate([att_out, ssm_out], axis=-1) @ w_out
    keep = max(0, k_all.shape[1] - MAX_WINDOW)
    new_state = (k_all[:, keep:], v_all[:, keep:], conv_ext[:, -(CONV_WIDTH - 1):], h_last.astype(h.dtype))
    return out, new_state

def peer_ffn(h, w_q, sub_keys, u_tab, v_tab):
    b, L, d = h.shape
    tok = h.reshape(b * L, d)
    n = tok.shape[0]
    q = (tok @ w_q).astype(jnp.float32).reshape(n, PEER_HEADS, 2, PEER_DKEY // 2)
    sk = sub_keys.astype(jnp.float32)
    s1 = jnp.einsum('nhk,ek->nhe', q[:, :, 0], sk[0])
    s2 = jnp.einsum('nhk,ek->nhe', q[:, :, 1], sk[1])
    v1, i1 = lax.top_k(s1, PEER_TOPK)
    v2, i2 = lax.top_k(s2, PEER_TOPK)
    cand = (v1[..., :, None] + v2[..., None, :]).reshape(n, PEER_HEADS, PEER_TOPK * PEER_TOPK)
    cidx = (i1[..., :, None] * PEER_NKEYS + i2[..., None, :]).reshape(n, PEER_HEADS, PEER_TOPK * PEER_TOPK)
    top_s, top_i = lax.top_k(cand, PEER_TOPK)
    expert = jnp.take_along_axis(cidx, top_i, axis=-1)
    gate = jax.nn.softmax(top_s, axis=-1).astype(h.dtype)
    n_pad = -(-n // PEER_BLOCK) * PEER_BLOCK
    pad = n_pad - n
    tok_b = jnp.pad(tok, ((0, pad), (0, 0))).reshape(-1, PEER_BLOCK, d)
    gate_b = jnp.pad(gate, ((0, pad), (0, 0), (0, 0))).reshape(-1, PEER_BLOCK, PEER_HEADS, PEER_TOPK)
    exp_b = jnp.pad(expert, ((0, pad), (0, 0), (0, 0))).reshape(-1, PEER_BLOCK, PEER_HEADS, PEER_TOPK)

    def run_block(args):
        t, g, e = args
        act = jax.nn.gelu(jnp.einsum('nd,nhkd->nhk', t, u_tab[e]), approximate=False)
        return jnp.einsum('nhk,nhkd->nd', g * act, v_tab[e])

    out = lax.map(run_block, (tok_b, gate_b, exp_b))
    return out.reshape(n_pad, d)[:n].reshape(b, L, d)

def setup_inputs(seed: int = 0) -> dict:
    key = jax.random.key(seed)
    ks = jax.random.split(key, 24)
    f32 = jnp.float32
    w_buf = min(MAX_WINDOW, PAST_LEN)

    def nrm(k, shape, scale):
        return jax.random.normal(k, shape, f32) * scale

    x_prompt = nrm(ks[0], (BATCH, SEQ, D_MODEL), 1.0)
    x_sample = nrm(ks[1], (DEC_BATCH, DEC_SEQ, D_MODEL), 1.0)
    cache_k = nrm(ks[2], (DEPTH, DEC_BATCH, w_buf, N_ATT_HEADS, HEAD_DIM), 1.0)
    cache_v = nrm(ks[3], (DEPTH, DEC_BATCH, w_buf, N_ATT_HEADS, HEAD_DIM), BETA)
    state_conv = nrm(ks[4], (DEPTH, DEC_BATCH, CONV_WIDTH - 1, CONV_DIM), 1.0)
    state_ssm = nrm(ks[5], (DEPTH, DEC_BATCH, N_SSM_HEADS, HEAD_DIM, D_STATE), 0.1)
    w_in = nrm(ks[6], (DEPTH, D_MODEL, N_IN), D_MODEL ** -0.5)
    w_in = w_in.at[:, :, V_OFF:Z_OFF].multiply(BETA)
    conv_w = nrm(ks[7], (DEPTH, CONV_DIM, CONV_WIDTH), CONV_WIDTH ** -0.5)
    conv_b = nrm(ks[8], (DEPTH, CONV_DIM), 0.02)
    dt0 = jnp.exp(jax.random.uniform(ks[9], (DEPTH, N_SSM_HEADS), f32, math.log(1e-3), math.log(1e-1)))
    dt_bias = dt0 + jnp.log(-jnp.expm1(-dt0))
    a_log = jnp.log(jax.random.uniform(ks[10], (DEPTH, N_SSM_HEADS), f32, 1.0, 16.0))
    d_skip = 1.0 + nrm(ks[11], (DEPTH, N_SSM_HEADS), 0.02)
    ssm_norm_g = 1.0 + nrm(ks[12], (DEPTH, D_SSM), 0.02)
    w_out = nrm(ks[13], (DEPTH, D_MIX, D_MODEL), D_MIX ** -0.5 * BETA)
    ln1_g = 1.0 + nrm(ks[14], (DEPTH, D_MODEL), 0.02)
    ln1_b = nrm(ks[15], (DEPTH, D_MODEL), 0.02)
    peer_wq = nrm(ks[16], (DEPTH, D_MODEL, PEER_HEADS * PEER_DKEY), D_MODEL ** -0.5)
    peer_keys = nrm(ks[17], (DEPTH, 2, PEER_NKEYS, PEER_DKEY // 2), (PEER_DKEY // 2) ** -0.5)
    peer_u = nrm(ks[18], (DEPTH, PEER_EXPERTS, D_MODEL), D_MODEL ** -0.5)
    peer_v = nrm(ks[19], (DEPTH, PEER_EXPERTS, D_MODEL), BETA * PEER_HEADS ** -0.5)
    ln2_g = 1.0 + nrm(ks[20], (DEPTH, D_MODEL), 0.02)
    ln2_b = nrm(ks[21], (DEPTH, D_MODEL), 0.02)
    return {'x_prompt': x_prompt, 'x_sample': x_sample, 'cache_k': cache_k, 'cache_v': cache_v,
            'state_conv': state_conv, 'state_ssm': state_ssm, 'w_in': w_in, 'conv_w': conv_w,
            'conv_b': conv_b, 'dt_bias': dt_bias, 'a_log': a_log, 'd_skip': d_skip,
            'ssm_norm_g': ssm_norm_g, 'w_out': w_out, 'ln1_g': ln1_g, 'ln1_b': ln1_b,
            'peer_wq': peer_wq, 'peer_keys': peer_keys, 'peer_u': peer_u, 'peer_v': peer_v,
            'ln2_g': ln2_g, 'ln2_b': ln2_b}

def reference(x_prompt, x_sample, cache_k, cache_v, state_conv, state_ssm, w_in, conv_w, conv_b,
              dt_bias, a_log, d_skip, ssm_norm_g, w_out, ln1_g, ln1_b, peer_wq, peer_keys,
              peer_u, peer_v, ln2_g, ln2_b):
    slopes = alibi_slopes()
    hp, hs = x_prompt, x_sample
    pk, pv, pc, ps = [], [], [], []
    sk, sv, sc, ss = [], [], [], []
    for l in range(DEPTH):
        mw = (w_in[l], conv_w[l], conv_b[l], dt_bias[l], a_log[l], d_skip[l], ssm_norm_g[l], w_out[l], slopes)
        mix_p, st_p = hybrid_mixer(hp, *mw, None)
        mix_s, st_s = hybrid_mixer(hs, *mw, (cache_k[l], cache_v[l], state_conv[l], state_ssm[l]))
        hp = layer_norm(ALPHA * hp + mix_p, ln1_g[l], ln1_b[l])
        hs = layer_norm(ALPHA * hs + mix_s, ln1_g[l], ln1_b[l])
        pw = (peer_wq[l], peer_keys[l], peer_u[l], peer_v[l])
        hp = layer_norm(ALPHA * hp + peer_ffn(hp, *pw), ln2_g[l], ln2_b[l])
        hs = layer_norm(ALPHA * hs + peer_ffn(hs, *pw), ln2_g[l], ln2_b[l])
        pk.append(st_p[0]); pv.append(st_p[1]); pc.append(st_p[2]); ps.append(st_p[3])
        sk.append(st_s[0]); sv.append(st_s[1]); sc.append(st_s[2]); ss.append(st_s[3])
    return (hp, hs, jnp.stack(pk), jnp.stack(pv), jnp.stack(pc), jnp.stack(ps),
            jnp.stack(sk), jnp.stack(sv), jnp.stack(sc), jnp.stack(ss))


_drawn_inputs = setup_inputs


def setup_inputs(seed=0):
    import zlib

    import numpy as np

    out = dict(_drawn_inputs(seed))
    spreads = {}
    factors = {'d_skip': 6.087, 'ssm_norm_g': 5.705, 'ln2_g': 2.945, 'ln2_b': 2.748}
    for name, (base, spread) in spreads.items():
        noise = np.random.default_rng([zlib.crc32(name.encode()), seed]).standard_normal(out[name].shape)
        drawn = base * np.exp(spread * noise) if base else spread * noise
        out[name] = __import__('jax').numpy.asarray(drawn.astype(out[name].dtype))
    for name, factor in factors.items():
        out[name] = (out[name] * factor).astype(out[name].dtype)
    return out
```

```python
import math
from contextlib import ExitStack

import numpy as np
import concourse.bass as bass
from concourse import mybir

F32 = mybir.dt.float32
U32 = mybir.dt.uint32
F32R = mybir.dt.float32r
I32 = mybir.dt.int32
ALU = mybir.AluOpType
ACT = mybir.ActivationFunctionType
AX = mybir.AxisListType

P = 128
D = 1024
DC = D // P
SEQ, NB, NT = 512, 8, 4
NS = NB * NT
TOK = SEQ + NS
HALF = TOK // 2
QT = SEQ // P
TILES = QT + 1
H, E = 16, 64
GR, N = 2, 128
CW = 4
XF = 12
PAST, WIN = 2048, 2048
BLOCK = 128
DILATIONS = ((128, 1), (512, 4), (2048, 16))
KOLD = 96
KEYS = 512 + KOLD * NT
KB = KEYS // P
KALL = KEYS + NT
PH, PK, TOPK = 8, 128, 16
SLOTS = PH * TOPK
EPS = 1e-5
ALPHA = 2.0 ** 0.25
NEG = -1.0e30
SLAB = 32
GRP = 4


def rows(i):
    return P if i < QT else NS


def sees(dist):
    n = np.zeros(dist.shape, np.int64)
    for window, dil in DILATIONS:
        n += (dist >= 0) & (dist <= window) & (dist % dil == 0)
    return n


def penalty(dist, head):
    slope = 2.0 ** (-8.0 * (head + 1) / H)
    n = sees(dist)
    return np.where(n > 0, -slope * dist + np.log(np.maximum(n, 1)), NEG).astype(np.float32)


def sample_positions():
    old = (np.arange(KOLD)[:, None] * 16 + np.arange(NT)[None, :]).ravel()
    return np.concatenate([old, np.arange(PAST - 512, PAST)])


def constants():
    p, c = np.arange(P)[:, None], np.arange(SEQ)[None, :]
    dist = (SEQ - P) + p - c
    prompt_bias = np.stack([penalty(dist, h) for h in range(H)], 0)
    pos = np.concatenate([sample_positions(), PAST + np.arange(NT)])
    sample_bias = np.concatenate([penalty(PAST + t - pos[None, :], h) for h in range(H) for t in range(NT)], 0)
    l, i = np.arange(P)[:, None], np.arange(P)[None, :]
    same = (l // NT == i // NT) & (l < NS) & (i < NS)
    tri = (l <= i).astype(np.float32)
    tri_s = (tri * same).astype(np.float32)
    seq_of = ((l // NT) == np.arange(NB)[None, :]) & (l < NS)
    cols = {
        "ident": np.eye(P, dtype=np.float32),
        "ones": np.ones((P, P), np.float32),
        "tri": tri, "ntri": -tri, "hide": np.where(l <= i, 0.0, NEG).astype(np.float32),
        "tri_s": tri_s, "ntri_s": -tri_s, "same_s": same.astype(np.float32),
        "hide_s": np.where((l <= i) & same, 0.0, NEG).astype(np.float32),
        "iota": np.broadcast_to(np.arange(P, dtype=np.float32), (P, P)),
        "seqrow": seq_of.astype(np.float32),
        "seqcol": np.broadcast_to((np.arange(NS)[None, :] // NT == np.arange(NB)[:, None]).reshape(1, -1), (P, NB * NS)),
    }
    at, parts = {}, []
    n = 0
    for name, a in cols.items():
        at[name] = (n, a.shape[1])
        parts.append(a)
        n += a.shape[1]
    return at, np.ascontiguousarray(np.concatenate(parts, 1).astype(np.float32)), prompt_bias, np.ascontiguousarray(sample_bias)


CONST_AT, CONST_TABLE, PROMPT_BIAS, SAMPLE_BIAS = constants()
CONST_W = CONST_TABLE.shape[1]


class Steps:

    def __init__(self, sem):
        self.sem, self.base, self.n = sem, 0, 0

    def __call__(self, instruction):
        instruction.then_inc(self.sem, 1)
        self.n += 1
        return self.base + self.n

    def wait(self, eng):
        eng.wait_ge(self.sem, self.base + self.n)

    def enter(self, i, per):
        self.outer, self.per = self.base + self.n, per
        self.base, self.n = self.outer + i * per, 0

    def leave(self, count):
        assert self.n == self.per, (self.n, self.per)
        self.base, self.n = self.outer + count * self.per, 0


def layer(nc, t):
    ctx = ExitStack()
    with ctx:
        def sem(name):
            return ctx.enter_context(nc.semaphore(name))

        KW = 256
        overlays = []

        def overlay(at, *dims, kind=F32):
            n = len(overlays)
            with nc.sbuf_tensor(f"under{n}", [P, int(at * KW)], F32):
                with nc.sbuf_tensor(f"overlay{n}", [P, int(np.prod(dims))], kind) as tensor:
                    overlays.append((tensor, dims))
            return shaped(tensor[:, :], dims)

        with nc.sbuf_tensor("arena", [P, 206 * KW], F32) as arena:
            pass

        def shaped(v, dims):
            if len(dims) == 2:
                v = v.rearrange("p (a b) -> p a b", b=dims[1])
            elif len(dims) == 3:
                v = v.rearrange("p (a b c) -> p a b c", b=dims[1], c=dims[2])
            return v

        def cut(at, *dims):
            n = int(np.prod(dims))
            assert at * KW + n <= 206 * KW, (at, dims)
            return shaped(arena[:, int(at * KW):int(at * KW) + n], dims)

        def product(pe, out, lhs, rhs, start, stop):
            pe.matmul(out, lhs[0], rhs[0], start=start, stop=False)
            pe.matmul(out, lhs[0], rhs[1], start=False, stop=False)
            return pe.matmul(out, lhs[1], rhs[0], start=False, stop=stop)

        consts = cut(0, CONST_W)
        def const(name):
            at, w = CONST_AT[name]
            return consts[:, at:at + w]
        ident, ones = const("ident"), const("ones")
        small = lambda at, *dims: cut(6.25 + at / KW, *dims)
        qk = cut(10, 16, TOK)
        vz = cut(44, TILES, 2 * D)
        mixT = cut(84, 16, TOK)
        att = cut(101, QT, D)
        xbc = cut(118, XF, 3 + TOK)
        xT = cut(153, DC, TOK)
        wslot = cut(170, 8, DC, P)
        xc = cut(153, XF, TOK)
        ext = cut(144, XF, NB * 7)
        qst, kst = cut(179, 2, SEQ), cut(183, 2, SEQ)
        bst, sst, pst, ptst = cut(187, 2, SEQ), cut(191, 2, SEQ), cut(195, 2, SEQ), cut(199, 2, SEQ)
        kring = cut(118, 4, KALL)
        vring = cut(179, 6, D)
        vring2 = cut(101, 1, D)
        vnew = cut(105, D)
        sdec, pdec = cut(109, KALL), cut(113, KALL)
        ptdec, ptnew = cut(133, KB, 64), cut(135, 64)
        qdiag = cut(136, 2, DC, 64)
        sbias = cut(140, KALL)
        ksam = cut(147, D)

        convw = small(0, XF, CW)
        convb = small(48, XF)
        dtb, alog, dskip = small(60, H), small(76, H), small(92, H)
        dt, dA = small(108, TILES, H), small(188, TILES, H)
        tmpa, tmpb = small(268, TILES, H), small(348, TILES, H)
        nmax, den, rden = small(428, 4), small(432, 4), small(436, 4)
        negA = small(440, H)
        eacs, wend, etot = small(456, H), small(472, H), small(488, H)
        wsum = small(504, H)
        stat = small(520, 8)
        dAm, decs = small(528, NB * H), small(656, NB * H)

        bank = ctx.enter_context(nc.psum_tensor("bank", [P, 8, 512], F32))

        consts_in, x_in, dtw_in = sem("consts_in"), sem("x_in"), sem("dtw_in")
        w_in_slot = [sem(f"w_in_slot{s}") for s in range(4)]
        w_in_half = [sem(f"w_in_half{s}") for s in range(2)]
        feat_ready, feat_kept = sem("feat_ready"), sem("feat_kept")
        rows_ready, rows_kept = sem("rows_ready"), sem("rows_kept")
        dt_ready, dt_made = sem("dt_ready"), sem("dt_made")
        zeroed = sem("zeroed")
        stored, xbc_stored, vs_stored = sem("stored"), sem("xbc_stored"), sem("vs_stored")
        dve_chain = Steps(sem("dve_chain"))
        act_chain = Steps(sem("act_chain"))
        silu_done = sem("silu_done")
        staged, bias_in = sem("staged"), [sem(f"bias_in{s}") for s in range(2)]
        scores_ready, max_ready = sem("scores_ready"), sem("max_ready")
        attT_ready, attT_kept = sem("attT_ready"), sem("attT_kept")
        stores = [0]

        def store(eng, dst, src):
            eng.dma_start(dst, src).then_inc(stored, 16)
            stores[0] += 16

        block = ctx.enter_context(nc.Block())

        FT = 28

        def sp_project(sp):
            sp.dma_start(consts, t["consts"]).then_inc(consts_in, 16)
            sp.dma_start(xT, t["xT"]).then_inc(x_in, 16)
            for s in range(4):
                sp.dma_start(wslot[:, s], t["w_in"][s]).then_inc(w_in_slot[s], 16)
            for dst, name in ((convw, "conv_w"), (convb, "conv_b"), (dtb, "dt_bias"), (alog, "a_log"), (dskip, "d_skip")):
                sp.dma_start(dst, t[name]).then_inc(consts_in, 16)
            sp.dma_start(cut(147, DC, H), t["w_dt"]).then_inc(dtw_in, 16)
            sp.dma_start(cut(148.5, XF, NB * 3), t["state_conv"]).then_inc(dtw_in, 16)
            sp.dma_start(wslot[:, 4:8], t["w_in"][FT:FT + 4].rearrange("s p c f -> p s c f")).then_inc(w_in_half[1], 16)
            with sp.Fori(1, FT // 4) as jj:
                for s in range(4):
                    sp.wait_ge(feat_ready, jj * 4 + (s - 3))
                    sp.dma_start(wslot[:, s], t["w_in"][bass.ds(jj * 4 + s, 1)].rearrange("s p c f -> p (s c) f"))\
                        .then_inc(w_in_slot[s], 16)
            for g in range(1, 4):
                if g == 1:
                    sp.wait_ge(feat_ready, FT)
                else:
                    sp.wait_ge(rows_ready, TILES * (g - 1))
                h = (g + 1) % 2
                sp.dma_start(wslot[:, 4 * h:4 * h + 4], t["w_in"][FT + 4 * g:FT + 4 * g + 4].rearrange("s p c f -> p s c f"))\
                    .then_inc(w_in_half[h], 16)

        def pe_project(pe):
            pe.wait_ge(consts_in, 96)
            pe.wait_ge(x_in, 16)

            def tile(jj, s, first):
                j = jj * 4 + s
                pe.wait_ge(w_in_slot[s], jj * 16 + 16)
                if not (first and s < 2):
                    pe.wait_ge(feat_kept, j - 1)
                for half in range(2):
                    for c in range(DC):
                        mm = pe.matmul(bank[:, 2 * (s % 2) + half, 0:HALF], wslot[:, s, c],
                                       xT[:, c, half * HALF:(half + 1) * HALF], start=(c == 0), stop=(c == DC - 1))
                mm.then_inc(feat_ready, 1)

            for s in range(4):
                tile(0, s, True)
            with pe.Fori(1, FT // 4) as jj:
                for s in range(4):
                    tile(jj, s, False)

            for g in range(4):
                half = (g + 1) % 2
                pe.wait_ge(w_in_half[half], 16 * (g // 2 + 1))
                for i in range(TILES):
                    n = g * TILES + i
                    if n >= 2:
                        pe.wait_ge(rows_kept, n - 1)
                    for c in range(DC):
                        mm = pe.matmul(bank[0:rows(i), 4 + n % 2, :], xT[:, c, i * P:i * P + rows(i)],
                                       wslot[:, 4 * half:4 * half + 4, c], start=(c == 0), stop=(c == DC - 1))
                    mm.then_inc(rows_ready, 1)
            pe.wait_ge(dtw_in, 32)
            for i in range(TILES):
                for c in range(DC):
                    mm = pe.matmul(bank[0:rows(i), 6, i * H:(i + 1) * H], xT[:, c, i * P:i * P + rows(i)],
                                   cut(147, DC, H)[:, c], start=(c == 0), stop=(c == DC - 1))
            mm.then_inc(dt_ready, 1)

        def act_project(act):
            for name, lo, n in (("qk", 0, 16), ("xbc", 16, XF)):
                with act.Fori(0, n // 4) as jj:
                    for s in range(4):
                        act.wait_ge(feat_ready, jj * 4 + (lo + s + 1))
                        j = bass.ds(jj * 4 + s, 1)
                        dst = qk[:, j] if name == "qk" else xbc[:, j, 3:3 + TOK]
                        act.copy(dst.rearrange("p o (h n) -> p (o h) n", h=2),
                                 bank[:, 2 * (s % 2):2 * (s % 2) + 2, 0:HALF]).then_inc(feat_kept, 1)

        def dve_project(dve):
            for n in range(4 * TILES):
                g, i = divmod(n, TILES)
                dve.wait_ge(rows_ready, n + 1)
                dve.tensor_copy(vz[0:rows(i), i, g * 512:(g + 1) * 512], bank[0:rows(i), 4 + n % 2, :]).then_inc(rows_kept, 1)

        after = {}
        ratio, ratio_r = cut(150, TILES, H), cut(150.5, TILES, H)

        def dve_dt(dve):
            step = dve_chain
            dve.wait_ge(dt_ready, 1)
            dve.wait_ge(consts_in, 96)
            dve.wait_ge(zeroed, 2)
            for i in range(TILES):
                r = rows(i)
                step(dve.tensor_tensor(dt[0:r, i], bank[0:r, 6, i * H:(i + 1) * H], dtb[0:r], ALU.add))
            step.wait(dve)
            after["abs"] = step(dve.scalar_tensor_tensor(tmpa, dt, -1.0, dt, ALU.mult, ALU.max))
            dve.wait_ge(dt_made, 1)
            after["u"] = step(dve.tensor_scalar(tmpb, tmpa, 1.0, None, ALU.add))
            step.wait(dve)
            after["ratio"] = step(dve.tensor_scalar(ratio, tmpb, 1.0, 1e-30, ALU.subtract, ALU.max))
            step.wait(dve)
            step(dve.reciprocal(ratio_r, ratio))
            step.wait(dve)
            step(dve.tensor_tensor(tmpa, tmpa, ratio_r, ALU.mult))
            step.wait(dve)
            dve.wait_ge(dt_made, 3)
            step(dve.tensor_tensor(tmpb, tmpb, tmpa, ALU.mult))
            step.wait(dve)
            step(dve.scalar_tensor_tensor(dt, dt, 0.0, tmpb, ALU.max, ALU.add))
            step.wait(dve)
            after["dA"] = step(dve.scalar_tensor_tensor(
                dA, dt, -1.0, negA.unsqueeze(1).to_broadcast([P, TILES, H]), ALU.mult, ALU.mult))

        def act_dt(act):
            act.wait_ge(dve_chain.sem, after["abs"])
            act.activation(tmpa, tmpa, ACT.Exp, scale=-1.0).then_inc(dt_made, 1)
            act.activation(negA, alog, ACT.Exp).then_inc(dt_made, 1)
            act.wait_ge(dve_chain.sem, after["ratio"])
            act.activation(tmpb, tmpb, ACT.Ln).then_inc(dt_made, 1)

        def pool_zeros(pool):
            pool.memset(xbc[:, :, 0:3], 0.0).then_inc(zeroed, 1)
            pool.memset(dt, 0.0).then_inc(zeroed, 1)

        def dve_conv(dve):
            step = dve_chain
            extv = ext.rearrange("p f (b w) -> p f b w", w=7)
            dve.wait_ge(feat_kept, FT)
            dve.wait_ge(dtw_in, 32)
            dve.wait_ge(zeroed, 1)
            old = cut(148.5, XF, NB * 3)
            step(dve.tensor_copy(extv[:, :, :, 0:3], old.rearrange("p f (b w) -> p f b w", w=3)))
            after["ext"] = step(dve.tensor_copy(extv[:, :, :, 3:7], xbc[:, :, 3 + SEQ:].rearrange("p f (b w) -> p f b w", w=4)))
            step.wait(dve)
            dve.wait_ge(dt_ready, 1)
            with dve.Fori(0, XF) as f:
                step.enter(f, 2 * CW)
                o = bass.ds(f, 1)
                out = xc[:, o].rearrange("p o n -> p (o n)")
                outs = out[:, SEQ:].rearrange("p (b w) -> p b w", w=NT)
                for k in range(CW):
                    w = convw[:, o, k:k + 1].rearrange("p o k -> p (o k)")
                    a = xbc[:, o, k:k + SEQ].rearrange("p o n -> p (o n)")
                    b = extv[:, o, :, k:k + NT].rearrange("p o b w -> p (o b) w")
                    if k == 0:
                        step(dve.tensor_scalar(out[:, 0:SEQ], a, w, convb[:, o], ALU.mult, ALU.add))
                        step(dve.tensor_scalar(outs, b, w, convb[:, o], ALU.mult, ALU.add))
                    else:
                        dve.wait_ge(step.sem, step.base + step.n - 1)
                        step(dve.scalar_tensor_tensor(out[:, 0:SEQ], a, w, out[:, 0:SEQ], ALU.mult, ALU.add))
                        dve.wait_ge(step.sem, step.base + step.n - 1)
                        step(dve.scalar_tensor_tensor(outs, b, w, outs, ALU.mult, ALU.add))
                after["conv0"] = step.outer
            step.leave(XF)
            after["conv"] = step.base

        def act_conv(act):
            with act.Fori(0, XF) as f:
                act.wait_ge(dve_chain.sem, f * (2 * CW) + (after["conv0"] + 2 * CW))
                v = xc[:, bass.ds(f, 1)]
                act.activation(v, v, ACT.Silu).then_inc(silu_done, 1)

        def sp_states(sp):
            sp.wait_ge(feat_kept, FT)
            store(sp, t["o_kT"], qk[:, 8:16])
            sp.dma_start(t["o_conv"], xbc[:, :, SEQ:SEQ + 3]).then_inc(xbc_stored, 16)
            sp.wait_ge(dve_chain.sem, after["ext"])
            store(sp, t["o_ext"], ext)
            sp.wait_ge(rows_kept, 2 * TILES)
            store(sp, t["o_v"].rearrange("(i p) n -> p i n", p=P), vz[:, 0:QT, 0:D])
            sp.dma_start(t["o_vs"], vz[0:NS, QT, 0:D]).then_inc(vs_stored, 16)

        UNITS = H * QT
        s_free, exp_done, turned, pt_kept, pv_done, att_kept = (
            sem(n) for n in ("s_free", "exp_done", "turned", "pt_kept", "pv_done", "att_kept"))

        def units(pp):
            for n in range(16):
                yield n, n // 8, (n // 4) % 2, n % 4, pp * 16 + n

        def sp_bias(sp):
            sp.wait_ge(dt_ready, 1)
            for s in range(2):
                sp.dma_start(bst[:, s], t["prompt_bias"][s]).then_inc(bias_in[s], 16)
            with sp.Fori(1, H // 2) as k:
                for s in range(2):
                    sp.wait_ge(s_free, k * 8 + (4 * s - 4 + 2))
                    sp.dma_start(bst[:, s], t["prompt_bias"][bass.ds(k * 2 + s, 1)].rearrange("h p n -> p (h n)"))\
                        .then_inc(bias_in[s], 16)

        def pool_stage(pool):
            pool.wait_ge(dt_ready, 1)

            def pair(p, s):
                for dst, lo in ((qst, 0), (kst, 8)):
                    pool.tensor_copy(dst[:, s], qk[:, bass.ds(p + lo, 1), 0:SEQ].rearrange("p o n -> p (o n)")).then_inc(staged, 1)

            pool.wait_ge(feat_kept, 16)
            for s in range(2):
                pair(s, s)
            with pool.Fori(1, H // 4) as k:
                for s in range(2):
                    pool.wait_ge(scores_ready, k * 16 + (8 * s - 8))
                    pair(k * 2 + s, s)

        def pe_attend(pe):
            pe.sem_inc(turned, 2)
            pe.sem_inc(pv_done, 2)
            pe.wait_ge(feat_kept, FT)
            pe.wait_ge(rows_kept, 4 * TILES)
            pe.wait_ge(dve_chain.sem, after["dA"])

            def scores(n, s, r, i, u):
                if i == 0 and r == 0:
                    pe.wait_ge(staged, pp * 4 + (2 * s + 2))
                pe.wait_ge(s_free, u + 1)
                k = (i + 1) * P
                pe.matmul(bank[:, n % 2, 0:k], qst[E * r:E * r + E, s, i * P:(i + 1) * P], kst[E * r:E * r + E, s, 0:k],
                          start=True, stop=True).then_inc(scores_ready, 1)

            def turn(n, s, r, i, u):
                pe.wait_ge(exp_done, u + 3)
                pe.wait_ge(pt_kept, u + 1)
                for kt in range(i + 1):
                    mm = pe.transpose(bank[:, 2 + n % 2, kt * P:(kt + 1) * P], pst[:, n % 2, kt * P:(kt + 1) * P], ident)
                mm.then_inc(turned, 1)

            def values(n, s, r, i, u):
                pe.wait_ge(pt_kept, u + 3)
                pe.wait_ge(att_kept, u + 1)
                for kt in range(i + 1):
                    mm = pe.matmul(bank[:, 4 + n % 2, 0:E], ptst[:, n % 2, kt * P:(kt + 1) * P],
                                   vz[:, kt, bass.ds(pp * (4 * E) + (2 * s + r) * E, E)], start=(kt == 0), stop=(kt == i))
                mm.then_inc(pv_done, 1)

            with pe.Fori(0, H // 4) as pp:
                us = list(units(pp))
                for n in range(16 + 2):
                    if n < 16:
                        scores(*us[n])
                    if 1 <= n <= 16:
                        turn(*us[n - 1])
                    if n >= 2:
                        values(*us[n - 2])
            pe.wait_ge(att_kept, UNITS + 2)
            for n in range(2 * QT):
                i, c0 = n // 2, 4 * (n % 2)
                if n >= 2:
                    pe.wait_ge(attT_kept, n - 1)
                for c in range(4):
                    mm = pe.transpose(bank[:, 6 + n % 2, c * P:(c + 1) * P], att[:, i, (c0 + c) * P:(c0 + c + 1) * P], ident)
                mm.then_inc(attT_ready, 1)

        def dve_attend(dve):
            dve.sem_inc(s_free, 2)
            dve.sem_inc(att_kept, 2)

            def bias(n, s, r, i, u):
                if i == 0:
                    dve.wait_ge(bias_in[r], pp * 32 + (16 * s + 16))
                dve.wait_ge(scores_ready, u + 1)
                dve.wait_ge(exp_done, u + 1)
                k = (i + 1) * P
                dve.scalar_tensor_tensor(sst[:, n % 2, 0:k], bank[:, n % 2, 0:k], E ** -0.5, bst[:, r, SEQ - k:SEQ],
                                         ALU.mult, ALU.add).then_inc(s_free, 1)
                dve.wait_ge(s_free, u + 3)
                dve.tensor_reduce(nmax[:, n % 4:n % 4 + 1], sst[:, n % 2, 0:k], AX.X, ALU.max, negate=True).then_inc(max_ready, 1)

            def norm(n, s, r, i, u):
                dve.wait_ge(exp_done, u + 3)
                dve_chain(dve.reciprocal(rden[:, n % 4:n % 4 + 1], den[:, n % 4:n % 4 + 1]))
                dve_chain.wait(dve)
                dve.wait_ge(pv_done, u + 3)
                dve.tensor_scalar(att[:, i, bass.ds(pp * (4 * E) + (2 * s + r) * E, E)], bank[:, 4 + n % 2, 0:E],
                                  rden[:, n % 4:n % 4 + 1], None, ALU.mult).then_inc(att_kept, 1)

            with dve.Fori(0, H // 4) as pp:
                dve_chain.enter(pp, 16)
                us = list(units(pp))
                for n in range(16 + 2):
                    if n < 16:
                        bias(*us[n])
                    if n >= 2:
                        norm(*us[n - 2])
            dve_chain.leave(H // 4)

        def act_attend(act):
            act.sem_inc(exp_done, 2)
            act.sem_inc(pt_kept, 2)

            def exp(n, s, r, i, u):
                act.wait_ge(max_ready, u + 1)
                act.wait_ge(turned, u + 1)
                k = (i + 1) * P
                act.activation(pst[:, n % 2, 0:k], sst[:, n % 2, 0:k], ACT.Exp, bias=nmax[:, n % 4:n % 4 + 1],
                               accum_out=den[:, n % 4:n % 4 + 1]).then_inc(exp_done, 1)

            def keep(n, s, r, i, u):
                act.wait_ge(turned, u + 3)
                act.wait_ge(pv_done, u + 1)
                k = (i + 1) * P
                act.copy(ptst[:, n % 2, 0:k], bank[:, 2 + n % 2, 0:k]).then_inc(pt_kept, 1)

            with act.Fori(0, H // 4) as pp:
                us = list(units(pp))
                for n in range(16 + 1):
                    if n < 16:
                        exp(*us[n])
                    if n >= 1:
                        keep(*us[n - 1])
            for n in range(2 * QT):
                i, c0 = n // 2, 4 * (n % 2)
                act.wait_ge(attT_ready, n + 1)
                act.copy(mixT[:, c0:c0 + 4, i * P:(i + 1) * P], bank[:, 6 + n % 2, :].rearrange("p (c n) -> p c n", c=4)).then_inc(attT_kept, 1)

        k_in = [sem(f"k_in{s}") for s in range(4)]
        v_in = [sem(f"v_in{s}") for s in range(KB)]
        vnew_in, qd_ready, k_used, v_used = (sem(n) for n in ("vnew_in", "qd_ready", "k_used", "v_used"))
        d_biased, d_max, d_exp, d_scaled, d_turned, d_kept, d_pv, d_out = (
            sem(n) for n in ("d_biased", "d_max", "d_exp", "d_scaled", "d_turned", "d_kept", "d_pv", "d_out"))
        sbias_in, ks_turned, ks_kept = sem("sbias_in"), sem("ks_turned"), sem("ks_kept")
        ROWS = H * NT
        vslot = [vring[:, s] for s in range(6)] + [vring2[:, 0]]
        qflat = [cut(135.25 + 2.25 * s, 9 * 64) for s in range(2)]
        KH = KEYS // 2

        def sp_samples(sp):
            sp.wait_ge(rows_kept, 2 * TILES)
            sp.wait_ge(silu_done, XF)
            sp.wait_ge(xbc_stored, 16)
            sp.dma_start(sbias[0:ROWS], t["sample_bias"]).then_inc(sbias_in, 16)

            def keys_of(b0, first):
                for c in range(DC):
                    if not (first and c < 4):
                        sp.wait_ge(k_used, b0 * DC + (c - 3 + 2 * DC))
                    sp.dma_start(kring[:, c % 4, 0:KEYS], t["cache_kT"][bass.ds(b0, 1), c].rearrange("b p n -> p (b n)"))\
                        .then_inc(k_in[c % 4], 16)

            keys_of(0, True)
            sp.wait_ge(ks_kept, 1)
            sp.wait_ge(vs_stored, 16)
            for b in range(NB):
                store(sp, t["o_ks"][b, WIN - NT:], ksam[b * NT:(b + 1) * NT])
                store(sp, t["o_vsall"][b, WIN - NT:], vz[b * NT:(b + 1) * NT, QT, 0:D])
            with sp.Fori(1, NB) as b:
                keys_of(b, False)

        def pool_values(pool):
            def values_of(b0, first):
                for kb in range(KB):
                    if not first:
                        pool.wait_ge(v_used, b0 * KB + (kb + 1 - KB))
                    pool.dma_start(vslot[kb], t["cache_v"][bass.ds(b0, 1), kb].rearrange("b p n -> p (b n)")).then_inc(v_in[kb], 16)
                if not first:
                    pool.wait_ge(d_pv, b0 + 1)
                pool.dma_start(vnew[0:NT], t["o_vs"][bass.ds(b0 * NT, NT)]).then_inc(vnew_in, 16)

            pool.wait_ge(vs_stored, 16)
            pool.wait_ge(attT_kept, 2 * QT)
            values_of(0, True)
            with pool.Fori(1, NB) as b:
                values_of(b, False)

        def pool_qdiag0(pool):
            pool.wait_ge(silu_done, XF)
            pool.wait_ge(xbc_stored, 16)
            for s in range(2):
                pool.memset(qflat[s], 0.0).then_inc(zeroed, 1)

        def dve_samples(dve):
            dve.wait_ge(zeroed, 4)
            dve.wait_ge(sbias_in, 16)
            dve.sem_inc(d_biased, 1)
            dve.sem_inc(d_out, 3)

            def place_q(s, b):
                dve.wait_ge(k_used, b * DC + DC)
                for r in range(2):
                    dst = qflat[s].rearrange("p (c w) -> p c w", w=72)
                    dve.tensor_copy(dst[E * r:E * r + E, :, NT * r:NT * r + NT],
                                    qk[E * r:E * r + E, 0:DC, bass.ds(b * NT + SEQ, NT)]).then_inc(qd_ready, 1)

            def soft(b):
                dve.wait_ge(k_used, b * DC + 3 * DC)
                dve.wait_ge(d_exp, b + 1)
                dve_chain(dve.scalar_tensor_tensor(sdec[0:ROWS, 0:KEYS].rearrange("p (h n) -> p h n", h=2), bank[0:ROWS, 0:2, 0:KH],
                                                   E ** -0.5, sbias[0:ROWS, 0:KEYS].rearrange("p (h n) -> p h n", h=2), ALU.mult, ALU.add))
                dve.scalar_tensor_tensor(sdec[0:ROWS, KEYS:KALL], bank[0:ROWS, 2, 0:NT], E ** -0.5, sbias[0:ROWS, KEYS:KALL],
                                         ALU.mult, ALU.add).then_inc(d_biased, 1)
                dve.wait_ge(d_biased, b + 2)
                dve.tensor_reduce(nmax[0:ROWS, 0:1], sdec[0:ROWS, :], AX.X, ALU.max, negate=True).then_inc(d_max, 1)
                dve.wait_ge(d_exp, b + 2)
                dve_chain(dve.reciprocal(rden[0:ROWS, 0:1], den[0:ROWS, 0:1]))
                dve_chain.wait(dve)
                dve.tensor_scalar(pdec[0:ROWS, :], pdec[0:ROWS, :], rden[0:ROWS, 0:1], None, ALU.mult).then_inc(d_scaled, 1)

            def keep(b, s):
                dve.wait_ge(d_pv, b + 2)
                for r in range(2):
                    src = bank[:, 6 + s, 0:64].rearrange("p (c w) -> p c w", w=8)
                    dve.tensor_copy(mixT[E * r:E * r + E, 0:DC, bass.ds(b * NT + SEQ, NT)],
                                    src[E * r:E * r + E, :, NT * r:NT * r + NT]).then_inc(d_out, 1)

            with dve.Fori(0, NB // 2) as bb:
                dve_chain.enter(bb, 4)
                b0, b1 = bb * 2, bb * 2 + 1
                place_q(0, b0)
                place_q(1, b1)
                soft(b0)
                soft(b1)
                keep(b0, 0)
                keep(b1, 1)
            dve_chain.leave(NB // 2)

        def act_samples(act):
            act.sem_inc(d_exp, 1)
            act.sem_inc(d_kept, 1)

            def exp(b):
                act.wait_ge(d_max, b + 1)
                act.wait_ge(d_turned, b + 1)
                act.activation(pdec[0:ROWS, :], sdec[0:ROWS, :], ACT.Exp, bias=nmax[0:ROWS, 0:1], accum_out=den[0:ROWS, 0:1]).then_inc(d_exp, 1)

            def keep(b):
                act.wait_ge(d_turned, b + 2)
                act.wait_ge(d_pv, b + 1)
                act_chain(act.copy(ptdec, bank[:, 4, 0:KB * ROWS].rearrange("p (k n) -> p k n", n=ROWS)))
                act.copy(ptnew[0:NT], bank[0:NT, 5, 0:ROWS]).then_inc(d_kept, 1)

            act.wait_ge(ks_turned, 1)
            act.copy(ksam[0:NS].rearrange("p (b n) -> p b n", b=2), bank[0:NS, 6:8, :]).then_inc(ks_kept, 1)
            with act.Fori(0, NB) as b:
                act_chain.enter(b, 1)
                exp(b)
                keep(b)
            act_chain.leave(NB)

        def pe_samples(pe):
            pe.sem_inc(k_used, 2 * DC)
            pe.sem_inc(d_turned, 1)
            pe.sem_inc(d_pv, 1)

            def scores(b, s):
                pe.wait_ge(qd_ready, b * 2 + 2)
                pe.wait_ge(d_biased, b + 1)
                for c in range(DC):
                    pe.wait_ge(k_in[c % 4], b * 32 + 16 * (c // 4 + 1))
                    lhsT = qflat[s][:, c * 64:c * 64 + ROWS]
                    pe.matmul(bank[0:ROWS, 2, 0:NT], lhsT, qk[:, DC + c, bass.ds(b * NT + SEQ, NT)], start=(c == 0), stop=(c == DC - 1))
                    pe.matmul(bank[0:ROWS, 0, 0:KH], lhsT, kring[:, c % 4, 0:KH], start=(c == 0), stop=(c == DC - 1))
                    pe.matmul(bank[0:ROWS, 1, 0:KH], lhsT, kring[:, c % 4, KH:KEYS], start=(c == 0), stop=(c == DC - 1)).then_inc(k_used, 1)

            def tail(b, s):
                pe.wait_ge(d_scaled, b + 1)
                pe.wait_ge(d_kept, b + 1)
                for kb in range(KB):
                    turn = pe.matmul if kb == 0 else pe.transpose
                    turn(bank[:, 4, kb * ROWS:(kb + 1) * ROWS], pdec[0:ROWS, kb * P:(kb + 1) * P], ident[0:ROWS, 0:ROWS])
                pe.transpose(bank[0:NT, 5, 0:ROWS], pdec[0:ROWS, KEYS:KALL], ident[0:ROWS, 0:ROWS]).then_inc(d_turned, 1)
                pe.wait_ge(d_kept, b + 2)
                pe.wait_ge(d_out, b * 2 + 1)
                for kb in range(KB + 1):
                    if kb < KB:
                        pe.wait_ge(v_in[kb], b * 16 + 16)
                    else:
                        pe.wait_ge(vnew_in, b * 16 + 16)
                    for c in range(DC):
                        v = vslot[kb][:, c * P:(c + 1) * P] if kb < KB else vnew[0:NT, c * P:(c + 1) * P]
                        w = ptdec[:, kb, 8 * c:8 * c + 8] if kb < KB else ptnew[0:NT, 8 * c:8 * c + 8]
                        mm = pe.matmul(bank[:, 6 + s, 8 * c:8 * c + 8], v, w, start=(kb == 0 and c == 0), stop=(kb == KB and c == DC - 1),
                                       skip_group_check=True)
                    mm.then_inc(v_used, 1) if kb < KB else mm.then_inc(d_pv, 1)

            pe.wait_ge(attT_kept, 2 * QT)
            for c in range(DC):
                mm = pe.transpose(bank[0:NS, 6 + c // 4, (c % 4) * P:(c % 4 + 1) * P], qk[:, DC + c, SEQ:], ident)
            mm.then_inc(ks_turned, 1)
            pe.wait_ge(ks_kept, 1)
            with pe.Fori(0, NB // 2) as bb:
                b0, b1 = bb * 2, bb * 2 + 1
                scores(b0, 0)
                scores(b1, 1)
                tail(b0, 0)
                tail(b1, 1)
        class Events:

            def __init__(self, sem, names):
                self.sem, self.counts, n = sem, {}, 0
                for i in range(TILES):
                    for name in names(i):
                        n += 1
                        self.counts[i, name] = n
                self.seen = 0

            def count_done(self, i, name, instruction):
                self.seen += 1
                assert self.counts[i, name] == self.seen, (i, name)
                instruction.then_inc(self.sem, 1)

            def wait(self, eng, i, name):
                eng.wait_ge(self.sem, self.counts[i, name])

        heads4 = range(4)
        seqs = range(NB)
        pe_ssd = Events(sem("pe_ssd"), lambda i:
            ["x_turned", "sums", "cb", "seg0", "seg1"] + (["out_turned"] if i else []) + (["inter"] if i < QT else []) +
            ["y0", "seg2", "y1", "seg3", "y2", "y3"] + (["state"] if i < QT else [f"state{b}" for b in seqs] + ["last_turned"]))
        act_ssd = Events(sem("act_ssd"), lambda i:
            ["x_kept", "b_kept", "eacs", "etot", "cb_kept"] + (["out_kept"] if i else []) + ["wexp", "E0", "E1", "E2", "E3", "zsilu", "sq0", "sq1", "root"] +
            (["last_kept"] if i == QT else []))
        dve_ssd = Events(sem("dve_ssd"), lambda i:
            ["wdiff", "xdt", "xw"] + (["bmask"] if i == QT else []) + ["M0", "M1", "M2", "M3"] +
            ([x for b in seqs for x in (f"hd{b}", f"hn{b}")] if i == QT else ["hd", "hn"]) +
            ["t_inter", "y_add", "xD", "y_full", "u", "var", "rstd", "n0", "n1"])
        pool_ssd = Events(sem("pool_ssd"), lambda i: (["dam", "cmask0", "cmask1"] if i == QT else []) + ["X0", "X1", "X2", "X3"])
        normg_in = sem("normg_in")
        h0_in = [sem(f"h0_in{s}") for s in range(2)]
        hn_stored = [sem(f"hn_stored{s}") for s in range(2)]

        xtok, btok = cut(10, D), cut(18, GR, N)
        xdt, xw = cut(20, D), cut(24, D)
        hT = cut(28, 2, D)
        yb, yu = cut(36, D), cut(40, D)
        esb, xsb, msb = cut(118, 2, 4, P), cut(122, 2, 4, P), cut(126, 2, 4, P)
        cbs = cut(130, GR, P)
        normg, zs = cut(132, D), cut(136, D)
        yo = cut(140, D)
        h0, hn = cut(179, 2, D), cut(187, 2, D)
        cm = cut(195, GR, NB, NS)
        bm = cut(197, NB, GR * N)
        ssq = stat[:, 0:2]
        rstd = stat[:, 2:4]

        def per_head(v, r, heads=H):
            return v.unsqueeze(2).to_broadcast([r, heads, E])

        def by_head(a, r):
            return a[0:r].rearrange("p (h e) -> p h e", e=E)

        def two_banks(b, r):
            return bank[0:r, b:b + 2, :].rearrange("p b (h e) -> p (b h) e", e=E)

        def sp_ssd(sp):
            sp.wait_ge(d_out, 3 + 2 * NB)
            sp.dma_start(normg, t["ssm_norm_g"]).then_inc(normg_in, 16)
            for b in seqs:
                if b >= 2:
                    pe_ssd.wait(sp, QT, f"state{b - 2}")
                    dve_ssd.wait(sp, QT, f"hd{b - 2}")
                sp.dma_start(h0[:, b % 2], t["state_ssm"][b]).then_inc(h0_in[b % 2], 16)
            dve_ssd.wait(sp, QT - 1, "hn")
            store(sp, t["o_hp"], hT[:, QT % 2])

        def act_store_states(act, b):
            dve_ssd.wait(act, QT, f"hn{b}")
            act.dma_start(t["o_hs"][b], hn[:, b % 2]).then_inc(hn_stored[b % 2], 16)

        def pool_ssd_run(pool):
            pool.wait_ge(d_out, 3 + 2 * NB)
            pool.wait_ge(dve_chain.sem, after["dA"])
            pool.memset(hT[:, 0], 0.0).then_inc(zeroed, 1)
            for i in range(TILES):
                r, sfx = rows(i), "" if i < QT else "_s"
                if i == QT:
                    pool_ssd.count_done(i, "dam", pool.tensor_tensor(
                        dAm[0:r].rearrange("p (b h) -> p b h", h=H), dA[0:r, i].unsqueeze(1).to_broadcast([r, NB, H]),
                        const("seqrow")[0:r].unsqueeze(2).to_broadcast([r, NB, H]), ALU.mult))
                    for g in range(GR):
                        pool_ssd.count_done(i, f"cmask{g}", pool.tensor_tensor(
                            cm[:, g], xc[:, 10 + g, SEQ:].unsqueeze(1).to_broadcast([P, NB, NS]),
                            const("seqcol").rearrange("p (b n) -> p b n", n=NS), ALU.mult))
                for q in heads4:
                    if q >= 2:
                        pe_ssd.wait(pool, i, f"seg{q - 2}")
                    elif i > 0:
                        pe_ssd.wait(pool, i - 1, f"seg{q + 2}")
                    pool_ssd.count_done(i, f"X{q}", pool.tensor_tensor(
                        xsb[0:r, q % 2, :, 0:r], const("tri" + sfx)[0:r, 0:r].unsqueeze(1).to_broadcast([r, 4, r]),
                        dA[0:r, i, 4 * q:4 * q + 4].unsqueeze(2).to_broadcast([r, 4, r]), ALU.mult))

        def pe_ssd_run(pe):
            pe.wait_ge(d_out, 3 + 2 * NB)
            pe.wait_ge(silu_done, XF)
            for i in range(TILES):
                r, sfx, c0 = rows(i), "" if i < QT else "_s", i * P

                def seg(q):
                    pool_ssd.wait(pe, i, f"X{q}")
                    if q >= 2:
                        act_ssd.wait(pe, i, f"E{q - 2}")
                    o = bank[0:r, 4 + q % 2, 0:4 * r].rearrange("p (h n) -> p h n", n=r)
                    pe.matmul(o, ones[0:r, 0:r], xsb[0:r, q % 2, :, 0:r], start=True, stop=False)
                    pe.matmul(o, const("ntri" + sfx)[0:r, 0:r], dA[0:r, i, 4 * q:4 * q + 4].unsqueeze(2).to_broadcast([r, 4, r]),
                              start=False, stop=False)
                    pe_ssd.count_done(i, f"seg{q}", pe.matmul(o, ident[0:r, 0:r],
                                  const("hide" + sfx)[0:r, 0:r].unsqueeze(1).to_broadcast([r, 4, r]), start=False, stop=True))

                def intra(q):
                    dve_ssd.wait(pe, i, f"M{q}")
                    for k in range(4):
                        h = 4 * q + k
                        mm = pe.matmul(bank[0:r, 6 + h // 8, (h % 8) * E:(h % 8 + 1) * E], msb[0:r, q % 2, k, 0:r],
                                       xdt[0:r, h * E:(h + 1) * E], start=True, stop=True)
                    pe_ssd.count_done(i, f"y{q}", mm)

                def turn_out(n):
                    dve_ssd.wait(pe, n, "n1")
                    for c in range(8):
                        mm = pe.transpose(bank[:, c // 4, (c % 4) * P:(c % 4) * P + rows(n)], yo[0:rows(n), c * P:(c + 1) * P],
                                          ident[0:rows(n), 0:rows(n)])
                    return mm

                if i:
                    dve_ssd.wait(pe, i - 1, "y_add")
                    act_ssd.wait(pe, i - 1, "cb_kept")
                for c in range(8):
                    pe.transpose(bank[0:r, c // 4, (c % 4) * P:(c % 4 + 1) * P], xc[:, c, c0:c0 + r], ident)
                for g in range(GR):
                    mm = pe.transpose(bank[0:r, 2, g * N:(g + 1) * N], xc[:, 8 + g, c0:c0 + r], ident)
                pe_ssd.count_done(i, "x_turned", mm)

                if i == 0:
                    pe.wait_ge(dve_chain.sem, after["dA"])
                pe.matmul(bank[0:r, 3, 0:H], const("tri" + sfx)[0:r, 0:r], dA[0:r, i], start=True, stop=True)
                end = ones if i < QT else const("same_s")
                mm = pe.matmul(bank[0:r, 3, H:2 * H], end[0:r, 0:r], dA[0:r, i], start=True, stop=True)
                if i == QT:
                    pool_ssd.wait(pe, i, "dam")
                    mm = pe.matmul(bank[:, 3, 2 * H:2 * H + NB * H], ones[0:r, :], dAm[0:r], start=True, stop=True)
                pe_ssd.count_done(i, "sums", mm)
                act_ssd.wait(pe, i, "b_kept")
                for g in range(GR):
                    mm = pe.matmul(bank[0:r, 2, g * r:(g + 1) * r], xc[:, 8 + g, c0:c0 + r], xc[:, 10 + g, c0:c0 + r],
                                   start=True, stop=True)
                pe_ssd.count_done(i, "cb", mm)
                seg(0)
                seg(1)
                act_ssd.wait(pe, i, "x_kept")
                if i:
                    pe_ssd.count_done(i, "out_turned", turn_out(i - 1))
                    act_ssd.wait(pe, i, "out_kept")
                if i < QT:
                    if i == 0:
                        pe.wait_ge(zeroed, 5)
                    else:
                        dve_ssd.wait(pe, i - 1, "hn")
                    for g in range(GR):
                        mm = pe.matmul(bank[:, g, :], xc[:, 10 + g, c0:c0 + r], hT[:, i % 2, g * 512:(g + 1) * 512], start=True, stop=True)
                    pe_ssd.count_done(i, "inter", mm)
                intra(0)
                seg(2)
                intra(1)
                seg(3)
                intra(2)
                intra(3)
                if i < QT:
                    act_ssd.wait(pe, i, "E3")
                    for g in range(GR):
                        mm = pe.matmul(bank[:, 4 + g, :], btok[:, g], xw[:, g * 512:(g + 1) * 512], start=True, stop=True)
                    pe_ssd.count_done(i, "state", mm)
                else:
                    act_ssd.wait(pe, i, "E3")
                    for b in seqs:
                        pe.wait_ge(h0_in[b % 2], 16 * (b // 2 + 1))
                        if b:
                            dve_ssd.wait(pe, i, f"hn{b - 1}")
                        for g in range(GR):
                            pe.matmul(bank[0:r, g, :], cm[:, g, b], h0[:, b % 2, g * 512:(g + 1) * 512], start=(b == 0), stop=(b == NB - 1))
                            mm = pe.matmul(bank[:, 4 + g, :], bm[0:r, b, g * N:(g + 1) * N], xw[0:r, g * 512:(g + 1) * 512],
                                           start=True, stop=True)
                        pe_ssd.count_done(i, f"state{b}", mm)
                    pe_ssd.count_done(i, "last_turned", turn_out(QT))

        def act_ssd_run(act):
            act.wait_ge(d_out, 3 + 2 * NB)
            for i in range(TILES):
                r = rows(i)

                def keep_out(n, name):
                    act_ssd.count_done(i, name, act.copy(
                        mixT[:, 8:16, n * P:n * P + rows(n)].rearrange("p (b c) n -> p b c n", b=2),
                        bank[:, 0:2, :].rearrange("p b (c n) -> p b c n", n=P)[:, :, :, 0:rows(n)]))

                pe_ssd.wait(act, i, "x_turned")
                if i:
                    dve_ssd.wait(act, i - 1, "xD")
                    pe_ssd.wait(act, i - 1, "state")
                act_ssd.count_done(i, "x_kept", act.copy(xtok[0:r].rearrange("p (b n) -> p b n", b=2), bank[0:r, 0:2, :]))
                act_ssd.count_done(i, "b_kept", act.copy(btok[0:r], bank[0:r, 2, 0:GR * N].rearrange("p (g n) -> p g n", n=N)))
                pe_ssd.wait(act, i, "sums")
                act_ssd.count_done(i, "eacs", act.activation(eacs[0:r], bank[0:r, 3, 0:H], ACT.Exp))
                if i < QT:
                    act_ssd.count_done(i, "etot", act.activation(etot, bank[:, 3, H:2 * H], ACT.Exp))
                else:
                    act_ssd.count_done(i, "etot", act.activation(decs, bank[:, 3, 2 * H:2 * H + NB * H], ACT.Exp))
                pe_ssd.wait(act, i, "cb")
                act_ssd.count_done(i, "cb_kept", act.copy(cbs[0:r, :, 0:r], bank[0:r, 2, 0:GR * r].rearrange("p (g n) -> p g n", n=r)))
                if i:
                    pe_ssd.wait(act, i, "out_turned")
                    keep_out(i - 1, "out_kept")
                dve_ssd.wait(act, i, "wdiff")
                act_ssd.count_done(i, "wexp", act.activation(wend[0:r], wsum[0:r], ACT.Exp))
                for q in heads4:
                    pe_ssd.wait(act, i, f"seg{q}")
                    if q >= 2:
                        dve_ssd.wait(act, i, f"M{q - 2}")
                    act_ssd.count_done(i, f"E{q}", act.activation(
                        esb[0:r, q % 2, :, 0:r], bank[0:r, 4 + q % 2, 0:4 * r].rearrange("p (h n) -> p h n", n=r), ACT.Exp))
                act_ssd.count_done(i, "zsilu", act.activation(zs[0:r], vz[0:r, i, D:2 * D], ACT.Silu))
                if i == QT:
                    for b in seqs:
                        act_store_states(act, b)
                dve_ssd.wait(act, i, "u")
                for g in range(GR):
                    act_ssd.count_done(i, f"sq{g}", act.activation(yu[0:r, g * 512:(g + 1) * 512], yb[0:r, g * 512:(g + 1) * 512], ACT.Square,
                                                               accum_out=ssq[0:r, g:g + 1]))
                dve_ssd.wait(act, i, "var")
                act_ssd.count_done(i, "root", act.activation(rstd[0:r], rstd[0:r], ACT.Sqrt))
                if i == QT:
                    pe_ssd.wait(act, i, "last_turned")
                    keep_out(QT, "last_kept")

        def dve_ssd_run(dve):
            dve.wait_ge(normg_in, 16)
            dve.wait_ge(consts_in, 96)
            for i in range(TILES):
                r = rows(i)
                pe_ssd.wait(dve, i, "sums")
                act_ssd.wait(dve, i, "etot")
                dve_chain(dve.tensor_copy(tmpa[0:r, 0], bank[0:r, 3, 0:H]))
                dve_chain.wait(dve)
                if i:
                    act_ssd.wait(dve, i - 1, "wexp")
                dve_ssd.count_done(i, "wdiff", dve.tensor_tensor(wsum[0:r], bank[0:r, 3, H:2 * H], tmpa[0:r, 0], ALU.subtract))
                act_ssd.wait(dve, i, "x_kept")
                dve_ssd.count_done(i, "xdt", dve.tensor_tensor(by_head(xdt, r), by_head(xtok, r), per_head(dt[0:r, i], r), ALU.mult))
                act_ssd.wait(dve, i, "wexp")
                dve_ssd.wait(dve, i, "xdt")
                dve_ssd.count_done(i, "xw", dve.tensor_tensor(by_head(xw, r), by_head(xdt, r), per_head(wend[0:r], r), ALU.mult))
                if i == QT:
                    dve_ssd.count_done(i, "bmask", dve.tensor_tensor(
                        bm[0:r], btok[0:r].rearrange("p g n -> p (g n)").unsqueeze(1).to_broadcast([r, NB, GR * N]),
                        const("seqrow")[0:r].unsqueeze(2).to_broadcast([r, NB, GR * N]), ALU.mult))
                act_ssd.wait(dve, i, "cb_kept")
                for q in heads4:
                    act_ssd.wait(dve, i, f"E{q}")
                    if q >= 2:
                        pe_ssd.wait(dve, i, f"y{q - 2}")
                    elif i:
                        pe_ssd.wait(dve, i - 1, f"y{q + 2}")
                    dve_ssd.count_done(i, f"M{q}", dve.tensor_tensor(
                        msb[0:r, q % 2, :, 0:r], esb[0:r, q % 2, :, 0:r], cbs[0:r, q // 2, 0:r].unsqueeze(1).to_broadcast([r, 4, r]), ALU.mult))
                if i < QT:
                    if i == 0:
                        dve.wait_ge(zeroed, 5)
                    else:
                        dve_ssd.wait(dve, i - 1, "hn")
                        pe_ssd.wait(dve, i - 1, "inter")
                    dve_ssd.count_done(i, "hd", dve.tensor_tensor(by_head(hT[:, (i + 1) % 2], P), by_head(hT[:, i % 2], P), per_head(etot, P), ALU.mult))
                    pe_ssd.wait(dve, i, "state")
                    dve_ssd.wait(dve, i, "hd")
                    dve_ssd.count_done(i, "hn", dve.tensor_tensor(by_head(hT[:, (i + 1) % 2], P), by_head(hT[:, (i + 1) % 2], P), two_banks(4, P), ALU.add))
                else:
                    for b in seqs:
                        dve.wait_ge(h0_in[b % 2], 16 * (b // 2 + 1))
                        if b >= 2:
                            dve.wait_ge(hn_stored[b % 2], 16 * (b // 2))
                        dve_ssd.count_done(i, f"hd{b}", dve.tensor_tensor(by_head(hn[:, b % 2], P), by_head(h0[:, b % 2], P),
                                                                      per_head(decs[:, b * H:(b + 1) * H], P), ALU.mult))
                        pe_ssd.wait(dve, i, f"state{b}")
                        dve_ssd.wait(dve, i, f"hd{b}")
                        dve_ssd.count_done(i, f"hn{b}", dve.tensor_tensor(by_head(hn[:, b % 2], P), by_head(hn[:, b % 2], P), two_banks(4, P), ALU.add))
                pe_ssd.wait(dve, i, "inter" if i < QT else f"state{NB - 1}")
                if i:
                    act_ssd.wait(dve, i - 1, "sq1")
                dve_ssd.count_done(i, "t_inter", dve.tensor_tensor(by_head(yb, r), two_banks(0, r), per_head(eacs[0:r], r), ALU.mult))
                dve_ssd.wait(dve, i, "t_inter")
                pe_ssd.wait(dve, i, "y3")
                dve_ssd.count_done(i, "y_add", dve.tensor_tensor(by_head(yb, r), by_head(yb, r), two_banks(6, r), ALU.add))
                if i:
                    act_ssd.wait(dve, i - 1, "sq1")
                dve_ssd.count_done(i, "xD", dve.tensor_tensor(by_head(yu, r), by_head(xtok, r), per_head(dskip[0:r], r), ALU.mult))
                dve_ssd.wait(dve, i, "xD")
                dve_ssd.count_done(i, "y_full", dve.tensor_tensor(yb[0:r], yb[0:r], yu[0:r], ALU.add))
                dve_ssd.wait(dve, i, "y_full")
                act_ssd.wait(dve, i, "zsilu")
                dve_ssd.count_done(i, "u", dve.tensor_tensor(yb[0:r], yb[0:r], zs[0:r], ALU.mult))
                act_ssd.wait(dve, i, "sq1")
                dve_ssd.count_done(i, "var", dve.tensor_scalar(rstd[0:r], ssq[0:r], 1.0 / 512, EPS, ALU.mult, ALU.add))
                act_ssd.wait(dve, i, "root")
                dve_ssd.count_done(i, "rstd", dve.reciprocal(rstd[0:r], rstd[0:r]))
                dve_ssd.wait(dve, i, "rstd")
                if i:
                    act_ssd.wait(dve, i, "out_kept")
                for g in range(GR):
                    c = slice(g * 512, (g + 1) * 512)
                    dve_ssd.count_done(i, f"n{g}", dve.scalar_tensor_tensor(yo[0:r, c], yb[0:r, c], rstd[0:r, g:g + 1], normg[0:r, c], ALU.mult, ALU.mult))

        def sp_dump5(sp):
            for s in range(2):
                sp.wait_ge(hn_stored[s], 16 * (NB // 2))
        wout = cut(10, 16, D)
        h1, h1T = cut(186, TILES, D), overlay(169, DC, TOK)
        xres, lng, lnb, hpre = cut(118, 2, D), cut(126, D), cut(130, D), cut(134, 2, D)
        bst6, mv = small(784, 2, 12), small(808, 2, 2)
        LN = 8
        wout_in, ln_in, xres_in = sem("wout_in"), sem("ln_in"), [sem(f"xres_in{s}") for s in range(2)]
        mixed, ln_step, ln_root = sem("mixed"), Steps(sem("ln_step")), sem("ln_root")
        h_turned, h_keptT = sem("h_turned"), sem("h_keptT")
        lnm = {}

        def layer_norm(dve, n, i, dst, g, b, product, loaded):
            r, s, step = rows(i), n % 2, ln_step
            x, residual = hpre[0:r, s], loaded()
            step(dve.scalar_tensor_tensor(x.rearrange("p (b n) -> p b n", b=2), residual.rearrange("p (b n) -> p b n", b=2), ALPHA,
                                          product, ALU.mult, ALU.add))
            lnm["sum", n] = step.base + step.n
            step.wait(dve)
            for k in range(2):
                step(dve.bn_stats(bst6[0:r, s, 6 * k:6 * k + 6], x[:, k * 512:(k + 1) * 512]))
            step.wait(dve)
            step(dve.bn_aggr(mv[0:r, s], bst6[0:r, s]))
            step.wait(dve)
            step(dve.tensor_scalar(mv[0:r, s, 1:2], mv[0:r, s, 1:2], EPS, None, ALU.add))
            lnm["var", n] = step.base + step.n
            dve.wait_ge(ln_root, n + 1)
            step(dve.reciprocal(mv[0:r, s, 1:2], mv[0:r, s, 1:2]))
            step.wait(dve)
            step(dve.tensor_scalar(x, x, mv[0:r, s, 0:1], mv[0:r, s, 1:2], ALU.subtract, ALU.mult))
            step.wait(dve)
            step(dve.tensor_tensor(x, x, g[0:r], ALU.mult))
            step.wait(dve)
            step(dve.tensor_tensor(dst, x, b[0:r], ALU.add))
            lnm["out", n] = step.base + step.n

        def act_root(act, n, i):
            act.wait_ge(ln_step.sem, lnm["var", n])
            act.activation(mv[0:rows(i), n % 2, 1:2], mv[0:rows(i), n % 2, 1:2], ACT.Sqrt).then_inc(ln_root, 1)

        def sp_out(sp):
            act_ssd.wait(sp, QT, "last_kept")
            for g in range(4):
                sp.dma_start(wout[:, 4 * g:4 * g + 4], t["w_out"][:, 4 * g:4 * g + 4]).then_inc(wout_in, 16)
            sp.dma_start(lng, t["ln1_g"]).then_inc(ln_in, 16)
            sp.dma_start(lnb, t["ln1_b"]).then_inc(ln_in, 16)
            for i in range(TILES):
                if i >= 2:
                    sp.wait_ge(ln_step.sem, lnm["sum", i - 2])
                sp.dma_start(xres[0:rows(i), i % 2], t["x"][i * P:i * P + rows(i)]).then_inc(xres_in[i % 2], 16)

        def pe_out(pe):
            pe.wait_ge(wout_in, 64)
            act_ssd.wait(pe, QT, "last_kept")
            for i in range(TILES):
                if i >= 2:
                    pe.wait_ge(ln_step.sem, lnm["sum", i - 2])
                for half in range(2):
                    for c in range(16):
                        mm = pe.matmul(bank[0:rows(i), 2 * (i % 2) + half, :], mixT[:, c, i * P:i * P + rows(i)],
                                       wout[:, c, half * 512:(half + 1) * 512], start=(c == 0), stop=(c == 15))
                mm.then_inc(mixed, 1)
                if i:
                    turn_h(pe, i - 1)
            turn_h(pe, QT)

        def turn_h(pe, i):
            pe.wait_ge(ln_step.sem, lnm["out", i])
            if i:
                pe.wait_ge(h_keptT, 2 * i)
            for c in range(DC):
                mm = pe.transpose(bank[:, 4 + c // 4, (c % 4) * P:(c % 4) * P + rows(i)], h1[0:rows(i), i, c * P:(c + 1) * P],
                                  ident[0:rows(i), 0:rows(i)])
                if c % 4 == 3:
                    mm.then_inc(h_turned, 1)

        def dve_out(dve):
            dve.wait_ge(ln_in, 32)
            act_ssd.wait(dve, QT, "last_kept")
            for i in range(TILES):
                def loaded(i=i):
                    dve.wait_ge(xres_in[i % 2], 16 * (i // 2 + 1))
                    dve.wait_ge(mixed, i + 1)
                    return xres[0:rows(i), i % 2]
                layer_norm(dve, i, i, h1[0:rows(i), i], lng, lnb, bank[0:rows(i), 2 * (i % 2):2 * (i % 2) + 2, :], loaded)

        def act_out(act):
            for i in range(TILES):
                act_root(act, i, i)
                for k in range(2):
                    act.wait_ge(h_turned, 2 * i + k + 1)
                    act.copy(h1T[:, 4 * k:4 * k + 4, i * P:i * P + rows(i)],
                             bank[:, 4 + k, :].rearrange("p (c n) -> p c n", n=P)[:, :, 0:rows(i)]).then_inc(h_keptT, 1)

        QF = 2 * PH
        wq, qT, skT = cut(142, 4, DC, P), cut(158, 2, TOK), cut(74, 2, P)
        sall = cut(10, TILES, QF, PK)
        wq_in, skT_in = [sem(f"wq_in{s}") for s in range(4)], sem("skT_in")
        q_ready, q_kept, s_ready, s_kept = (sem(n) for n in ("q_ready", "q_kept", "s_ready", "s_kept"))
        sall_zeroed = sem("sall_zeroed")

        def sp_query(sp):
            sp.dma_start(skT, t["peer_keys"]).then_inc(skT_in, 16)
            for s in range(4):
                sp.dma_start(wq[:, s], t["peer_wq"][s]).then_inc(wq_in[s], 16)
            with sp.Fori(1, QF // 4) as k:
                for s in range(4):
                    sp.wait_ge(q_ready, k * 4 + (s - 3))
                    sp.dma_start(wq[:, s], t["peer_wq"][bass.ds(k * 4 + s, 1)].rearrange("f p c n -> p (f c) n")).then_inc(wq_in[s], 16)

        def pool_query(pool):
            pool.wait_ge(mixed, TILES)
            pool.memset(sall[:, QT], 0.0).then_inc(sall_zeroed, 1)

        def pe_query(pe):
            pe.wait_ge(h_keptT, 2 * TILES)
            pe.wait_ge(skT_in, 16)
            pe.wait_ge(ln_step.sem, lnm["out", QT])
            pe.sem_inc(s_ready, 2)

            def query(f, s):
                pe.wait_ge(wq_in[s], (f - s) * 4 + 16)
                pe.wait_ge(q_kept, f + 1)
                for half in range(2):
                    for c in range(DC):
                        mm = pe.matmul(bank[:, 2 * (s % 2) + half, 0:HALF], wq[:, s, c], h1T[:, c, half * HALF:(half + 1) * HALF],
                                       start=(c == 0), stop=(c == DC - 1))
                mm.then_inc(q_ready, 1)

            def score(f, s):
                pe.wait_ge(q_kept, f + 3)
                pe.wait_ge(s_kept, f * 2 + 2)
                for i in range(TILES):
                    mm = pe.matmul(bank[0:rows(i), 4 + 2 * (s % 2) + i // QT, (i % QT) * P:(i % QT + 1) * P],
                                   qT[:, s % 2, i * P:i * P + rows(i)], skT[:, s % 2], start=True, stop=True)
                mm.then_inc(s_ready, 1)

            with pe.Fori(0, QF // 4) as k:
                for s in range(5):
                    if s < 4:
                        query(k * 4 + s, s)
                    if s:
                        score(k * 4 + (s - 1), s - 1)

        def act_query(act):
            act.sem_inc(q_kept, 2)
            with act.Fori(0, QF // 4) as k:
                for s in range(4):
                    f = k * 4 + s
                    act.wait_ge(q_ready, f + 1)
                    act.wait_ge(s_ready, f + 1)
                    act.copy(qT[:, s % 2].rearrange("p (h n) -> p h n", h=2), bank[:, 2 * (s % 2):2 * (s % 2) + 2, 0:HALF]).then_inc(q_kept, 1)

        def dve_query(dve):
            dve.sem_inc(s_kept, 4)
            dve.wait_ge(sall_zeroed, 1)
            with dve.Fori(0, QF // 4) as k:
                for s in range(4):
                    f = k * 4 + s
                    dve.wait_ge(s_ready, f + 3)
                    dve.tensor_copy(sall[:, 0:QT, bass.ds(f, 1)].rearrange("p i o n -> p i (o n)"),
                                    bank[:, 4 + 2 * (s % 2), :].rearrange("p (i n) -> p i n", n=P)).then_inc(s_kept, 1)
                    dve.tensor_copy(sall[0:NS, QT, bass.ds(f, 1)].rearrange("p o n -> p (o n)"), bank[0:NS, 5 + 2 * (s % 2), 0:P]).then_inc(s_kept, 1)

        K8 = 8
        sc, sv = cut(75, QF, PK), cut(83, QF, TOPK)
        su = cut(84, QF, TOPK).bitcast(U32)
        si = cut(85, QF, TOPK)
        cand = cut(86, PH, TOPK, TOPK)
        cv, cu, ca = cut(94, PH, TOPK), cut(94.5, PH, TOPK).bitcast(U32), cut(95, PH, TOPK).bitcast(U32)
        caf = cut(95.5, 2, PH, TOPK)
        cb_ = cut(96.5, PH, TOPK).bitcast(U32)
        hot = cut(97, PH, TOPK, TOPK)
        chosen = cut(105, 3, PH * TOPK)
        hsum, hrec = cut(106.5, PH), cut(106.6, PH)
        slotT = cut(161.5, 3, TILES * P)
        TOP = 12 * QF // 2
        picked, gate_exp, ch_turned, ch_kept = sem("picked"), sem("gate_exp"), sem("ch_turned"), sem("ch_kept")
        topk = Steps(sem("topk"))
        PER_TILE = 1 + 5 * QF + 2 + 5 * PH + 5 + 2 * 3 + 3
        cv2 = cut(107, PH, TOPK)

        def dve_topk(dve):
            step = topk
            dve.wait_ge(s_kept, 2 * QF + 4)
            NEGBIG = -3.0e38
            fences = []
            with dve.Fori(0, TILES) as i:
                step.enter(i, PER_TILE)
                step(dve.tensor_copy(sc, sall[:, bass.ds(i, 1)].rearrange("p o f n -> p (o f) n")))
                step.wait(dve)

                def fence():
                    step.wait(dve)
                    fences.append(0)
                    dve.memset(small(900 + len(fences), 1), 0.0)

                def top16(values, width, out_v, out_i, n):
                    for k in range(2):
                        fence()
                        for f in range(n):
                            step(dve.max(out_v(f, k), values(f)))
                        fence()
                        for f in range(n):
                            step(dve.max_index(out_i(f, k), out_v(f, k), values(f)))
                        if k == 0:
                            fence()
                            for f in range(n):
                                step(dve.match_replace(values(f), out_v(f, k), values(f), NEGBIG))

                top16(lambda f: sc[:, f], PK, lambda f, k: sv[:, f, K8 * k:K8 * k + K8], lambda f, k: su[:, f, K8 * k:K8 * k + K8], QF)
                step.wait(dve)
                step(dve.tensor_copy(si, su))
                v = sv.rearrange("p (h s) k -> p h s k", s=2)
                step(dve.tensor_tensor(cand, v[:, :, 0].unsqueeze(3).to_broadcast([P, PH, TOPK, TOPK]),
                                       v[:, :, 1].unsqueeze(2).to_broadcast([P, PH, TOPK, TOPK]), ALU.add))
                step.wait(dve)
                flat = cand.rearrange("p h a b -> p h (a b)")
                top16(lambda f: flat[:, f], TOPK * TOPK, lambda f, k: cv[:, f, K8 * k:K8 * k + K8],
                      lambda f, k: cu[:, f, K8 * k:K8 * k + K8], PH)
                step.wait(dve)
                step(dve.tensor_scalar(ca, cu, 4, None, ALU.logical_shift_right))
                step(dve.tensor_scalar(cb_, cu, 15, None, ALU.bitwise_and))
                step.wait(dve)
                step(dve.tensor_copy(caf[:, 0], ca))
                step(dve.tensor_copy(caf[:, 1], cb_))
                step(dve.tensor_tensor(cv2, cv, cv[:, :, 0:1].to_broadcast([P, PH, TOPK]), ALU.subtract))
                after["shifted"] = step.outer + step.n
                step.wait(dve)
                dve.wait_ge(ch_turned, i + 1)
                iv = si.rearrange("p (h s) k -> p h s k", s=2)
                for side in range(2):
                    step(dve.tensor_tensor(hot, caf[:, side].unsqueeze(3).to_broadcast([P, PH, TOPK, TOPK]),
                                           const("iota")[:, 0:TOPK].unsqueeze(1).unsqueeze(1).to_broadcast([P, PH, TOPK, TOPK]), ALU.is_equal))
                    step.wait(dve)
                    step(dve.tensor_tensor(hot, hot, iv[:, :, side].unsqueeze(2).to_broadcast([P, PH, TOPK, TOPK]), ALU.mult))
                    step.wait(dve)
                    step(dve.tensor_reduce(chosen[:, side].rearrange("p (h k) -> p h k", k=TOPK), hot, AX.X, ALU.add))
                    step.wait(dve)
                dve.wait_ge(gate_exp, i + 1)
                step(dve.tensor_reduce(hsum, cv2, AX.X, ALU.add))
                step.wait(dve)
                step(dve.reciprocal(hrec, hsum))
                step.wait(dve)
                step(dve.tensor_tensor(chosen[:, 2].rearrange("p (h k) -> p h k", k=TOPK), cv2,
                                       hrec.unsqueeze(2).to_broadcast([P, PH, TOPK]), ALU.mult))
                step.wait(dve)
            step.leave(TILES)
        AHEAD = 12
        EARLY, SLABS = AHEAD * TILES, TOK // SLAB
        assert EARLY + SLABS * GRP == PK
        slab = [cut(10, PK, SLAB), cut(26, PK, SLAB)]
        hh = overlay(108, DC, TOK, kind=F32R), overlay(125, DC, TOK, kind=F32R)
        uraw, us = overlay(142, 4, DC, P), (overlay(50, 4, DC, P, kind=F32R), overlay(169, 4, DC, P, kind=F32R))
        aring = cut(66, 4, TOK)
        hot_a, hot_b = cut(75, 2, 4, P), cut(79, 2, 4, P)
        h_hi, h_lo = sem("h_hi"), sem("h_lo")
        u_in, a_stored = [sem(f"u_in{s}") for s in range(4)], [sem(f"a_stored{s}") for s in range(4)]
        u_hi, u_lo, u_done, gelu_done = (sem(n) for n in ("u_hi", "u_lo", "u_done", "gelu_done"))
        hot_ready, g_done, g_kept = (sem(n) for n in ("hot_ready", "g_done", "g_kept"))
        slab_stored = [sem(f"slab_stored{s}") for s in range(2)]
        GS = SLAB // 4
        GROUPS = PK // GRP

        def sp_up(sp):
            for s in range(4):
                sp.sem_inc(a_stored[s], 16)
            for s in range(2):
                sp.sem_inc(slab_stored[s], 16)

            def fetch(a, s, first=False):
                if first:
                    sp.wait_ge(q_ready, QF)
                else:
                    sp.wait_ge(u_lo, a - 3)
                sp.dma_start(uraw[:, s], t["peer_u"][bass.ds(a, 1)].rearrange("a p c n -> p (a c) n")).then_inc(u_in[s], 16)

            def keep(a, s, g):
                sp.wait_ge(gelu_done, a + 3)
                sp.dma_start(t["act"][bass.ds(g, 1), :, s].rearrange("g p n -> p (g n)"), aring[:, s]).then_inc(a_stored[s], 16)

            for s in range(4):
                fetch(s, s, True)
            with sp.Fori(0, EARLY // 4) as x:
                for s in range(4):
                    fetch(x * 4 + (s + 4), s)
                    keep(x * 4 + s, s, x)

            def keep_slab(n, s):
                sp.wait_ge(g_kept, n * GS + (GS + 2))
                sp.dma_start(t["gate"][bass.ds(n, 1)].rearrange("s p a n -> p (s a) n"), slab[s]).then_inc(slab_stored[s], 16)

            def last_rows(n, more=True):
                for s in range(4):
                    if more:
                        fetch(n * 4 + (EARLY + s + 4), s)
                    keep(n * 4 + (EARLY + s), s, n + EARLY // 4)

            last_rows(0)
            with sp.Fori(0, (SLABS - 3) // 2) as x:
                for s in range(2):
                    keep_slab(x * 2 + s, s)
                    last_rows(x * 2 + (s + 1))
            for n in range(SLABS - 3, SLABS):
                keep_slab(n, n % 2)
                if n < SLABS - 1:
                    last_rows(n + 1, n + 1 < SLABS - 1)

        def act_up(act):
            act.wait_ge(h_keptT, 2 * TILES)
            act.wait_ge(s_ready, QF + 2)
            for c in range(DC):
                act.copy(hh[0][:, c], h1T[:, c]).then_inc(h_hi, 1)
            act.sem_inc(ch_kept, 1)
            act.sem_inc(gelu_done, 2)
            act.sem_inc(g_kept, 2)

            def hi(a, s, q):
                act.wait_ge(u_in[s], q * 16 + 16)
                act.copy(us[0][:, s], uraw[:, s]).then_inc(u_hi, 1)

            def gelu(a, s, q):
                act.wait_ge(u_done, a + 1)
                act.wait_ge(a_stored[s], q * 16 + 16)
                act.activation(aring[:, s].rearrange("p (h n) -> p h n", h=2), bank[:, 2 * (s % 2):2 * (s % 2) + 2, 0:HALF],
                               ACT.Gelu).then_inc(gelu_done, 1)

            for s in range(4):
                hi(s, s, 0)
            with act.Fori(0, TILES) as i:
                for n in range(AHEAD):
                    a, q = i * AHEAD + n, i * (AHEAD // 4) + n // 4
                    gelu(a, n % 4, q)
                    hi(a + 4, n % 4, q + 1)
                    if n == AHEAD - 3:
                        act.wait_ge(topk.sem, i * PER_TILE + after["shifted"])
                        act.activation(cv2, cv2, ACT.Exp).then_inc(gate_exp, 1)
                act.wait_ge(ch_turned, i + 2)
                act.copy(slotT[:, :, bass.ds(i * P, P)], bank[:, 6, 0:3 * P].rearrange("p (j n) -> p j n", j=3)).then_inc(ch_kept, 1)

            def last_rows(n, sl, more=True):
                for s in range(4):
                    a, q = n * 4 + (EARLY + s), n + EARLY // 4
                    gelu(a, s, q)
                    if more:
                        hi(a + 4, s, q + 1)
                    for par in range(2):
                        act.wait_ge(g_done, n * GS + (2 * s + par + 3))
                        act.copy(slab[sl][:, :, 8 * s + 4 * par:8 * s + 4 * par + 4].rearrange("p a n -> p n a"),
                                 bank[:, 4 + par, :].rearrange("p (n a) -> p n a", a=P)).then_inc(g_kept, 1)

            with act.Fori(0, (SLABS - 1) // 2) as x:
                for sl in range(2):
                    act.wait_ge(slab_stored[sl], x * 16 + 16)
                    last_rows(x * 2 + sl, sl)
            act.wait_ge(slab_stored[(SLABS - 1) % 2], 16 * (SLABS // 2 + 1))
            last_rows(SLABS - 1, (SLABS - 1) % 2, False)

        def pool_up(pool):
            for c in range(DC):
                pool.wait_ge(h_hi, c + 1)
                pool.tensor_tensor(hh[1][:, c], h1T[:, c], hh[0][:, c].bitcast(F32), ALU.subtract).then_inc(h_lo, 1)
            pool.wait_ge(h_lo, DC)
            with pool.Fori(0, PK // 4) as x:
                for s in range(4):
                    pool.wait_ge(u_hi, x * 4 + (s + 1))
                    pool.tensor_tensor(us[1][:, s], uraw[:, s], us[0][:, s].bitcast(F32), ALU.subtract).then_inc(u_lo, 1)

        def pe_up(pe):
            pe.sem_inc(ch_turned, 1)
            pe.sem_inc(g_done, 2)
            pe.wait_ge(q_kept, QF + 2)
            pe.wait_ge(s_kept, 2 * QF + 4)
            pe.wait_ge(h_lo, DC)

            def up(a, s):
                pe.wait_ge(u_lo, a + 1)
                pe.wait_ge(gelu_done, a + 1)
                for half in range(2):
                    for c in range(DC):
                        mm = product(pe, bank[:, 2 * (s % 2) + half, 0:HALF], [w[:, s, c] for w in us],
                                     [h[:, c, half * HALF:(half + 1) * HALF] for h in hh], c == 0, c == DC - 1)
                mm.then_inc(u_done, 1)

            with pe.Fori(0, TILES) as i:
                for n in range(AHEAD):
                    up(i * AHEAD + n, n % 4)
                pe.wait_ge(topk.sem, i * PER_TILE + PER_TILE)
                pe.wait_ge(ch_kept, i + 1)
                for j in range(3):
                    mm = pe.transpose(bank[:, 6, j * P:(j + 1) * P], chosen[:, j], ident)
                mm.then_inc(ch_turned, 1)
            pe.wait_ge(ch_kept, TILES + 1)
            with pe.Fori(0, SLABS) as n:
                for s in range(4):
                    up(n * 4 + (EARLY + s), s)
                    for par in range(2):
                        w = n * GS + (2 * s + par)
                        pe.wait_ge(hot_ready, w + 1)
                        pe.wait_ge(g_kept, w + 1)
                        for j in range(4):
                            mm = pe.matmul(bank[:, 4 + par, j * P:(j + 1) * P], hot_b[:, par, j], hot_a[:, par, j], start=True, stop=True)
                        mm.then_inc(g_done, 1)

        def dve_onehots(dve):
            dve.wait_ge(ch_kept, TILES + 1)
            with dve.Fori(0, TOK // 8) as x:
                for par in range(2):
                    w = x * 2 + par
                    dve.wait_ge(g_done, w + 1)
                    for j in range(4):
                        at = lambda row: slotT[:, row, bass.ds(w * 4 + j, 1)]
                        dve.tensor_scalar(hot_a[:, par, j], const("iota"), at(0), None, ALU.is_equal)
                        last = dve.tensor_scalar(hot_b[:, par, j], const("iota"), at(1), at(2), ALU.is_equal, ALU.mult)
                    last.then_inc(hot_ready, 1)

        acc = cut(10, DC, TOK)
        ga = overlay(27, 8, TOK, kind=F32R), overlay(44, 8, TOK, kind=F32R)
        agrp, ggrp = cut(61, 2, GRP, TOK), cut(99, 2, GRP * TOK)
        vraw, vs = overlay(83, 4, D), (overlay(116, 8, D, kind=F32R), overlay(148, 8, D, kind=F32R))
        prod = overlay(180, 2, TOK)
        a_in, gate_in = [sem(f"a_in{s}") for s in range(2)], [sem(f"gate_in{s}") for s in range(2)]
        vraw_in = [sem(f"vraw_in{s}") for s in range(4)]
        v_hi, v_lo, ga_hi, ga_lo, weighted, vp_done, added, copied, acc_zeroed = (
            sem(n) for n in ("v_hi", "v_lo", "ga_hi", "ga_lo", "weighted", "vp_done", "added", "copied", "acc_zeroed"))
        CHUNK = (WIN - NT) * D // 16
        PIECE = CHUNK // 16

        def sp_values(sp):
            for s in range(2):
                sp.wait_ge(slab_stored[s], 16 * (1 + (SLABS + 1 - s) // 2))
            for s in range(4):
                sp.wait_ge(a_stored[s], 16 * (GROUPS + 1))

            def values(g2, par, k):
                a = g2 * 8 + (par * GRP + k)
                sp.wait_ge(v_lo, a + 1)
                sp.dma_start(vraw[:, k], t["peer_v"][bass.ds(a, 1)].rearrange("a p n -> p (a n)")).then_inc(vraw_in[k], 16)

            with sp.Fori(0, GROUPS // 2) as x:
                for par in range(2):
                    g = x * 2 + par
                    sp.wait_ge(weighted, g * GRP + 4)
                    sp.dma_start(agrp[:, par], t["act"][bass.ds(g, 1)].rearrange("g p k n -> p (g k) n")).then_inc(a_in[par], 16)
                    sp.dma_start(ggrp[:, par].rearrange("p (s a n) -> p s (a n)", a=GRP, n=SLAB),
                                 t["gate"].rearrange("s p a n -> p s (a n)")[:, :, bass.ds(g * (GRP * SLAB), GRP * SLAB)])\
                        .then_inc(gate_in[par], 16)
                    for k in range(GRP):
                        values(x, par, k)
                    src, dst = (("cache_k", "o_ks"), ("cache_vall", "o_vsall"))[par]
                    cutout = lambda ap, lo: ap.rearrange("b s d -> b (s d)")[:, bass.ds(x * CHUNK + lo, CHUNK)]\
                        .rearrange("b (s n) -> s b n", n=PIECE)
                    sp.dma_start(cutout(t[dst], 0), cutout(t[src], NT * D)).then_inc(copied, 16)
            sp.wait_ge(copied, 16 * 32)

        def pool_values_lo(pool):
            pool.sem_inc(v_lo, 4)
            pool.wait_ge(u_done, PK)
            with pool.Fori(0, PK // 8) as x:
                for j in range(8):
                    pool.wait_ge(v_hi, x * 8 + (j + 1))
                    pool.tensor_tensor(vs[1][:, j], vraw[:, j % GRP], vs[0][:, j].bitcast(F32), ALU.subtract).then_inc(v_lo, 1)

        def act_values(act):
            act.wait_ge(slab_stored[0], 16 * (2 + SLABS // 2))
            act.wait_ge(slab_stored[1], 16 * (1 + SLABS // 2))
            with act.Fori(0, GROUPS // 2) as x:
                for j in range(8):
                    par, k = j // GRP, j % GRP
                    if k == 0:
                        act.wait_ge(vp_done, x * (2 * DC) + (par * DC + DC))
                    act.wait_ge(vraw_in[k], x * 32 + (16 * par + 16))
                    act.copy(vs[0][:, j], vraw[:, k]).then_inc(v_hi, 1)
                    act.wait_ge(weighted, x * 8 + (j + 9))
                    act.copy(ga[0][:, j], prod[:, j % 2]).then_inc(ga_hi, 1)

        def pe_values(pe):
            pe.sem_inc(vp_done, 2 * DC)
            pe.wait_ge(gelu_done, PK + 2)
            pe.wait_ge(g_kept, SLABS * GS + 2)
            with pe.Fori(0, GROUPS // 2) as x:
                for par in range(2):
                    g = x * 2 + par
                    pe.wait_ge(ga_lo, g * GRP + (GRP + 2))
                    pe.wait_ge(v_lo, g * GRP + (GRP + 4))
                    for c in range(DC):
                        pe.wait_ge(added, g * DC + (c + 5))
                        for half in range(2):
                            for k in range(GRP):
                                j = par * GRP + k
                                mm = product(pe, bank[:, 2 * (c % 4) + half, 0:HALF], [v[:, j, c * P:(c + 1) * P] for v in vs],
                                             [w[:, j, half * HALF:(half + 1) * HALF] for w in ga], k == 0, k == GRP - 1)
                        mm.then_inc(vp_done, 1)

        def dve_values(dve):
            dve.sem_inc(weighted, 8)
            dve.sem_inc(added, 8)
            dve.sem_inc(ga_lo, 2)
            dve.wait_ge(slab_stored[0], 16 * (2 + SLABS // 2))
            dve.wait_ge(slab_stored[1], 16 * (1 + SLABS // 2))
            dve.wait_ge(u_done, PK)
            dve.memset(acc, 0.0).then_inc(acc_zeroed, 1)
            dve.wait_ge(acc_zeroed, 1)

            def weigh(g2, par, g):
                def times(k):
                    if k == 0:
                        dve.wait_ge(a_in[par], g2 * 16 + 16)
                        dve.wait_ge(gate_in[par], g2 * 16 + 16)
                    dve.wait_ge(ga_lo, g * GRP + (k + 1))
                    dve.tensor_tensor(prod[:, k % 2].rearrange("p (s n) -> p s n", n=SLAB),
                                      agrp[:, par, k].rearrange("p (s n) -> p s n", n=SLAB),
                                      ggrp[:, par].rearrange("p (s a n) -> p s a n", a=GRP, n=SLAB)[:, :, k], ALU.mult).then_inc(weighted, 1)

                def low(k):
                    dve.wait_ge(ga_hi, g * GRP + (k + 1))
                    j = par * GRP + k
                    dve.tensor_tensor(ga[1][:, j], prod[:, k % 2], ga[0][:, j].bitcast(F32), ALU.subtract).then_inc(ga_lo, 1)

                times(0)
                for k in range(1, GRP):
                    times(k)
                    low(k - 1)
                low(GRP - 1)

            def add(g2, par, g):
                for c in range(DC):
                    dve.wait_ge(vp_done, g * DC + (c + 17))
                    dve.wait_ge(added, g * DC + (c + 1))
                    v = acc[:, c].rearrange("p (h n) -> p h n", h=2)
                    dve.tensor_tensor(v, v, bank[:, 2 * (c % 4):2 * (c % 4) + 2, 0:HALF], ALU.add).then_inc(added, 1)

            weigh(0, 0, 0)
            with dve.Fori(0, GROUPS // 2 - 1) as x:
                weigh(x, 1, x * 2 + 1)
                add(x, 0, x * 2)
                weigh(x + 1, 0, x * 2 + 2)
                add(x, 1, x * 2 + 1)
            x = GROUPS // 2 - 1
            weigh(x, 1, 2 * x + 1)
            add(x, 0, 2 * x)
            add(x, 1, 2 * x + 1)

        ln2_in, o_turned, y_stored = sem("ln2_in"), sem("o_turned"), [sem(f"y_stored{s}") for s in range(2)]

        def sp_final(sp):
            sp.wait_ge(vp_done, (GROUPS + 2) * DC)
            sp.dma_start(lng, t["ln2_g"]).then_inc(ln2_in, 16)
            sp.dma_start(lnb, t["ln2_b"]).then_inc(ln2_in, 16)
            for i in range(TILES):
                sp.wait_ge(ln_step.sem, lnm["out", TILES + i])
                s = (TILES + i) % 2
                sp.dma_start(t["o_y"][i * P:i * P + rows(i)], xres[0:rows(i), s]).then_inc(y_stored[s], 16)
            sp.wait_ge(y_stored[1], 48)
            sp.wait_ge(y_stored[0], 32)

        def pe_final(pe):
            pe.wait_ge(added, GROUPS * DC + 8)
            for i in range(TILES):
                if i >= 2:
                    pe.wait_ge(ln_step.sem, lnm["sum", TILES + i - 2])
                for c in range(DC):
                    mm = pe.transpose(bank[0:rows(i), 2 * (i % 2) + c // 4, (c % 4) * P:(c % 4 + 1) * P], acc[:, c, i * P:i * P + rows(i)], ident)
                mm.then_inc(o_turned, 1)

        def dve_final(dve):
            dve.wait_ge(ln2_in, 32)
            for i in range(TILES):
                def loaded(i=i):
                    dve.wait_ge(o_turned, i + 1)
                    if i >= 2:
                        dve.wait_ge(y_stored[(TILES + i) % 2], 16 * (i // 2))
                    return h1[0:rows(i), i]
                layer_norm(dve, TILES + i, i, xres[0:rows(i), (TILES + i) % 2], lng, lnb, bank[0:rows(i), 2 * (i % 2):2 * (i % 2) + 2, :], loaded)

        def act_final(act):
            for i in range(TILES):
                act_root(act, TILES + i, i)
        @block.vector
        def _(dve):
            dve_project(dve)
            dve_dt(dve)
            dve_conv(dve)
            dve_attend(dve)
            dve_samples(dve)
            dve_ssd_run(dve)
            dve_out(dve)
            dve_query(dve)
            dve_topk(dve)
            dve_onehots(dve)
            dve_values(dve)
            dve_final(dve)

        @block.scalar
        def _(act):
            act_project(act)
            act_dt(act)
            act_conv(act)
            act_attend(act)
            act_samples(act)
            act_ssd_run(act)
            act_out(act)
            act_query(act)
            act_up(act)
            act_values(act)
            act_final(act)

        @block.gpsimd
        def _(pool):
            pool_zeros(pool)
            pool_stage(pool)
            pool_qdiag0(pool)
            pool_values(pool)
            pool_ssd_run(pool)
            pool_query(pool)
            pool_up(pool)
            pool_values_lo(pool)

        @block.tensor
        def _(pe):
            pe_project(pe)
            pe_attend(pe)
            pe_samples(pe)
            pe_ssd_run(pe)
            pe_out(pe)
            pe_query(pe)
            pe_up(pe)
            pe_values(pe)
            pe_final(pe)

        @block.sync
        def _(sp):
            sp_project(sp)
            sp_states(sp)
            sp_bias(sp)
            sp_samples(sp)
            sp_ssd(sp)
            sp_dump5(sp)
            sp_out(sp)
            sp_query(sp)
            sp_up(sp)
            sp_values(sp)
            sp_final(sp)
            sp.wait_ge(stored, stores[0])


def lay_out(a):
    f = {k: np.asarray(v) for k, v in a.items()}
    tok = np.concatenate([f["x_prompt"].reshape(SEQ, D), f["x_sample"].reshape(NS, D)], 0)
    w = f["w_in"][0]
    blocks = lambda m: m.reshape(DC, P, m.shape[1] // P, P).transpose(2, 1, 0, 3)
    qkv_z = np.concatenate([w[:, 0:2 * D], w[:, 4 * D:4 * D + XF * P], w[:, 2 * D:4 * D]], 1)
    across = lambda v: np.broadcast_to(v[None, :], (P, v.shape[0]))
    perseq = lambda m, n: m.transpose(2, 0, 1).reshape(n, P, -1).transpose(1, 0, 2)
    ins = {
        "consts": CONST_TABLE,
        "x": tok,
        "xT": tok.T.reshape(DC, P, TOK).transpose(1, 0, 2),
        "w_in": blocks(qkv_z),
        "w_dt": w[:, -H:].reshape(DC, P, H).transpose(1, 0, 2),
        "state_conv": perseq(f["state_conv"][0], XF),
        "conv_w": f["conv_w"][0].reshape(XF, P, CW).transpose(1, 0, 2),
        "conv_b": f["conv_b"][0].reshape(XF, P).T,
        "dt_bias": across(f["dt_bias"][0]), "a_log": across(f["a_log"][0]), "d_skip": across(f["d_skip"][0]),
        "prompt_bias": PROMPT_BIAS, "sample_bias": SAMPLE_BIAS,
        "cache_kT": f["cache_k"][0][:, sample_positions()].transpose(0, 2, 3, 1).reshape(NB, DC, P, KEYS),
        "cache_v": f["cache_v"][0][:, sample_positions()].reshape(NB, KB, P, D),
        "ssm_norm_g": across(f["ssm_norm_g"][0]),
        "state_ssm": f["state_ssm"][0].transpose(0, 3, 1, 2).reshape(NB, N, D),
        "w_out": f["w_out"][0].reshape(16, P, D).transpose(1, 0, 2),
        "ln1_g": across(f["ln1_g"][0]), "ln1_b": across(f["ln1_b"][0]),
        "peer_wq": blocks(f["peer_wq"][0]), "peer_keys": f["peer_keys"][0].transpose(2, 0, 1),
        "peer_u": f["peer_u"][0].reshape(PK, PK, DC, P).transpose(0, 3, 2, 1),
        "peer_v": f["peer_v"][0].reshape(PK, PK, D),
        "ln2_g": across(f["ln2_g"][0]), "ln2_b": across(f["ln2_b"][0]),
        "cache_k": f["cache_k"][0].reshape(NB, WIN, D), "cache_vall": f["cache_v"][0].reshape(NB, WIN, D),
    }
    return {k: np.ascontiguousarray(v) for k, v in ins.items()}


OUTS = {
    "o_kT": (P, 8, TOK), "o_conv": (P, XF, 3), "o_ext": (P, XF, NB * 7), "o_v": (SEQ, D), "o_vs": (NS, D),
    "o_hp": (N, D), "o_hs": (NB, N, D),
    "o_ks": (NB, WIN, D), "o_vsall": (NB, WIN, D), "o_y": (TOK, D),
}


def kernel(**inputs):
    import concourse.bacc as bacc
    from concourse.bass_utils import run_bass_kernel_spmd as run

    nc = bacc.Bacc("TRN2", target_bir_lowering=False, num_devices=1)
    ins = lay_out(inputs)
    t = {k: nc.dram_tensor(k, v.shape, F32, kind="ExternalInput").ap() for k, v in ins.items()}
    t.update({k: nc.dram_tensor(k, s, F32, kind="ExternalOutput").ap() for k, s in OUTS.items()})
    t["gate"] = nc.dram_tensor("gate", (TOK // SLAB, P, PK, SLAB), F32, kind="Internal").ap()
    t["act"] = nc.dram_tensor("act", (PK // GRP, P, GRP, TOK), F32, kind="Internal").ap()
    layer(nc, t)
    r = run(nc, [ins], core_ids=[0]).results[0]
    kT = r["o_kT"].transpose(2, 1, 0).reshape(TOK, H, E)
    k_prompt = kT[:SEQ][None, None]
    v_prompt = r["o_v"].reshape(1, 1, SEQ, H, E)
    conv_prompt = r["o_conv"].transpose(2, 1, 0).reshape(1, 1, 3, XF * P)
    ext = r["o_ext"].reshape(P, XF, NB, 7).transpose(2, 3, 1, 0).reshape(NB, 7, XF * P)
    conv_sample = ext[None, :, 4:]
    h_prompt = r["o_hp"].reshape(N, H, E).transpose(1, 2, 0)[None, None]
    h_sample = r["o_hs"].reshape(NB, N, H, E).transpose(0, 2, 3, 1)[None]
    y = r["o_y"]
    return (y[:SEQ].reshape(1, SEQ, D), y[SEQ:].reshape(NB, NT, D), k_prompt, v_prompt, conv_prompt, h_prompt,
            r["o_ks"].reshape(1, NB, WIN, H, E), r["o_vsall"].reshape(1, NB, WIN, H, E), conv_sample, h_sample)
```

```python
import math
from contextlib import ExitStack

import numpy as np
import concourse.bass as bass
from concourse import mybir

F32 = mybir.dt.float32
U32 = mybir.dt.uint32
F32R = mybir.dt.float32r
I32 = mybir.dt.int32
ALU = mybir.AluOpType
ACT = mybir.ActivationFunctionType
AX = mybir.AxisListType

P = 128
D = 1024
DC = D // P
SEQ, NB, NT = 512, 8, 4
NS = NB * NT
TOK = SEQ + NS
HALF = TOK // 2
QT = SEQ // P
TILES = QT + 1
H, E = 16, 64
GR, N = 2, 128
CW = 4
XF = 12
PAST, WIN = 2048, 2048
BLOCK = 128
DILATIONS = ((128, 1), (512, 4), (2048, 16))
KOLD = 96
KEYS = 512 + KOLD * NT
KB = KEYS // P
KALL = KEYS + NT
PH, PK, TOPK = 8, 128, 16
SLOTS = PH * TOPK
EPS = 1e-5
ALPHA = 2.0 ** 0.25
NEG = -1.0e30
SLAB = 32
GRP = 4


def rows(i):
    return P if i < QT else NS


def sees(dist):
    n = np.zeros(dist.shape, np.int64)
    for window, dil in DILATIONS:
        n += (dist >= 0) & (dist <= window) & (dist % dil == 0)
    return n


def penalty(dist, head):
    slope = 2.0 ** (-8.0 * (head + 1) / H)
    n = sees(dist)
    return np.where(n > 0, -slope * dist + np.log(np.maximum(n, 1)), NEG).astype(np.float32)


def sample_positions():
    old = (np.arange(KOLD)[:, None] * 16 + np.arange(NT)[None, :]).ravel()
    return np.concatenate([old, np.arange(PAST - 512, PAST)])


def constants():
    p, c = np.arange(P)[:, None], np.arange(SEQ)[None, :]
    dist = (SEQ - P) + p - c
    prompt_bias = np.stack([penalty(dist, h) for h in range(H)], 0)
    pos = np.concatenate([sample_positions(), PAST + np.arange(NT)])
    sample_bias = np.concatenate([penalty(PAST + t - pos[None, :], h) for h in range(H) for t in range(NT)], 0)
    l, i = np.arange(P)[:, None], np.arange(P)[None, :]
    same = (l // NT == i // NT) & (l < NS) & (i < NS)
    tri = (l <= i).astype(np.float32)
    tri_s = (tri * same).astype(np.float32)
    seq_of = ((l // NT) == np.arange(NB)[None, :]) & (l < NS)
    cols = {
        "ident": np.eye(P, dtype=np.float32),
        "ones": np.ones((P, P), np.float32),
        "tri": tri, "ntri": -tri, "hide": np.where(l <= i, 0.0, NEG).astype(np.float32),
        "tri_s": tri_s, "ntri_s": -tri_s, "same_s": same.astype(np.float32),
        "hide_s": np.where((l <= i) & same, 0.0, NEG).astype(np.float32),
        "iota": np.broadcast_to(np.arange(P, dtype=np.float32), (P, P)),
        "seqrow": seq_of.astype(np.float32),
        "seqcol": np.broadcast_to((np.arange(NS)[None, :] // NT == np.arange(NB)[:, None]).reshape(1, -1), (P, NB * NS)),
    }
    at, parts = {}, []
    n = 0
    for name, a in cols.items():
        at[name] = (n, a.shape[1])
        parts.append(a)
        n += a.shape[1]
    return at, np.ascontiguousarray(np.concatenate(parts, 1).astype(np.float32)), prompt_bias, np.ascontiguousarray(sample_bias)


CONST_AT, CONST_TABLE, PROMPT_BIAS, SAMPLE_BIAS = constants()
CONST_W = CONST_TABLE.shape[1]


class Steps:

    def __init__(self, sem):
        self.sem, self.base, self.n = sem, 0, 0

    def __call__(self, instruction):
        instruction.then_inc(self.sem, 1)
        self.n += 1
        return self.base + self.n

    def wait(self, eng):
        eng.wait_ge(self.sem, self.base + self.n)

    def enter(self, i, per):
        self.outer, self.per = self.base + self.n, per
        self.base, self.n = self.outer + i * per, 0

    def leave(self, count):
        assert self.n == self.per, (self.n, self.per)
        self.base, self.n = self.outer + count * self.per, 0


def layer(nc, t):
    ctx = ExitStack()
    with ctx:
        def sem(name):
            return ctx.enter_context(nc.semaphore(name))

        KW = 256
        overlays = []

        def overlay(at, *dims, kind=F32):
            n = len(overlays)
            with nc.sbuf_tensor(f"under{n}", [P, int(at * KW)], F32):
                with nc.sbuf_tensor(f"overlay{n}", [P, int(np.prod(dims))], kind) as tensor:
                    overlays.append((tensor, dims))
            return shaped(tensor[:, :], dims)

        with nc.sbuf_tensor("arena", [P, 206 * KW], F32) as arena:
            pass

        def shaped(v, dims):
            if len(dims) == 2:
                v = v.rearrange("p (a b) -> p a b", b=dims[1])
            elif len(dims) == 3:
                v = v.rearrange("p (a b c) -> p a b c", b=dims[1], c=dims[2])
            return v

        def cut(at, *dims):
            n = int(np.prod(dims))
            assert at * KW + n <= 206 * KW, (at, dims)
            return shaped(arena[:, int(at * KW):int(at * KW) + n], dims)

        def product(pe, out, lhs, rhs, start, stop):
            pe.matmul(out, lhs[0], rhs[0], start=start, stop=False)
            pe.matmul(out, lhs[0], rhs[1], start=False, stop=False)
            return pe.matmul(out, lhs[1], rhs[0], start=False, stop=stop)

        consts = cut(0, CONST_W)
        def const(name):
            at, w = CONST_AT[name]
            return consts[:, at:at + w]
        ident, ones = const("ident"), const("ones")
        small = lambda at, *dims: cut(6.25 + at / KW, *dims)
        qk = cut(10, 16, TOK)
        vz = cut(44, TILES, 2 * D)
        mixT = cut(84, 16, TOK)
        att = cut(101, QT, D)
        xbc = cut(124, XF, 3 + TOK)
        xc = xbc[:, :, 3:]
        ext = cut(149.75, XF, NB * 7)
        ctail = cut(152.5, XF, 3)
        TPAD = TILES * P
        xraw = overlay(44, DC, TOK)
        dtw_raw, oldconv = overlay(62, DC, H), cut(64, XF, NB * 3)
        dtw = overlay(62.5, DC, H, kind=F32R), overlay(63, DC, H, kind=F32R)
        ratio, ratio_r = cut(66, TILES, H), cut(66.5, TILES, H)
        xs = overlay(84, DC, TPAD, kind=F32R), overlay(104, DC, TPAD, kind=F32R)
        nothing = overlay(67, TPAD - TOK)
        wraw, ws = overlay(153, 4, DC, P), (overlay(169, 4, DC, P, kind=F32R), overlay(185, 4, DC, P, kind=F32R))
        ctmp = cut(201, 2, TOK)
        qst, kst = cut(153, 2, SEQ), cut(157, 2, SEQ)
        bst, sst, pst, ptst = cut(161, 2, SEQ), cut(165, 2, SEQ), cut(169, 2, SEQ), cut(173, 2, SEQ)
        kring = cut(177, 4, KALL)
        sbias = cut(191.25, KALL)
        vring = cut(153, 6, D)
        vring2 = cut(101, 1, D)
        vnew = cut(105, D)
        sdec, pdec = cut(109, KALL), cut(113, KALL)
        ptdec, ptnew = cut(195, KB, 64), cut(197, 64)
        ksam = cut(202, D)

        convw = small(0, XF, CW)
        convb = small(48, XF)
        dtb, alog, dskip = small(60, H), small(76, H), small(92, H)
        dt, dA = small(108, TILES, H), small(188, TILES, H)
        tmpa, tmpb = small(268, TILES, H), small(348, TILES, H)
        nmax, den, rden = small(428, 4), small(432, 4), small(436, 4)
        negA = small(440, H)
        eacs, wend, etot = small(456, H), small(472, H), small(488, H)
        wsum = small(504, H)
        stat = small(520, 8)
        dAm, decs = small(528, NB * H), small(656, NB * H)

        bank = ctx.enter_context(nc.psum_tensor("bank", [P, 8, 512], F32))

        consts_in, dtw_in = sem("consts_in"), sem("dtw_in")
        x_in = [sem(f"x_in{s}") for s in range(2)]
        x_hi, x_lo, x_pad = sem("x_hi"), sem("x_lo"), sem("x_pad")
        w_raw = [sem(f"w_raw{s}") for s in range(4)]
        w_hi, w_lo = sem("w_hi"), sem("w_lo")
        feat_ready, feat_kept = sem("feat_ready"), sem("feat_kept")
        rows_ready, rows_kept = sem("rows_ready"), sem("rows_kept")
        dt_ready, dt_made = sem("dt_ready"), sem("dt_made")
        zeroed = sem("zeroed")
        stored, vs_stored = sem("stored"), sem("vs_stored")
        dve_chain = Steps(sem("dve_chain"))
        act_chain = Steps(sem("act_chain"))
        silu_done = sem("silu_done")
        staged, bias_in = sem("staged"), [sem(f"bias_in{s}") for s in range(2)]
        scores_ready, max_ready = sem("scores_ready"), sem("max_ready")
        attT_ready, attT_kept = sem("attT_ready"), sem("attT_kept")
        stores = [0]

        def store(eng, dst, src):
            eng.dma_start(dst, src).then_inc(stored, 16)
            stores[0] += 16

        block = ctx.enter_context(nc.Block())

        copied = sem("copied")
        CHUNK = (WIN - NT) * D // 16
        PIECE = CHUNK // 16

        def copy_cache(sp, side, x):
            src, dst = (("cache_k", "o_ks"), ("cache_vall", "o_vsall"))[side]
            cutout = lambda ap, lo: ap.rearrange("b s d -> b (s d)")[:, bass.ds(x * CHUNK + lo, CHUNK)]\
                .rearrange("b (s n) -> s b n", n=PIECE)
            sp.dma_start(cutout(t[dst], 0), cutout(t[src], NT * D)).then_inc(copied, 16)

        FT = 28
        BLOCKS = FT + 16
        VG = 8

        def sp_project(sp):
            for s in range(2):
                sp.dma_start(xraw[:, 4 * s:4 * s + 4], t["xT"][:, 4 * s:4 * s + 4]).then_inc(x_in[s], 16)
            sp.dma_start(dtw_raw, t["w_dt"]).then_inc(dtw_in, 16)
            sp.dma_start(oldconv, t["state_conv"]).then_inc(dtw_in, 16)
            sp.wait_ge(w_lo, 4)
            with sp.Fori(0, BLOCKS // 4) as x:
                for s in range(4):
                    sp.wait_ge(w_lo, x * 4 + (s + 1))
                    sp.dma_start(wraw[:, s], t["w_in"][bass.ds(x * 4 + s, 1)].rearrange("s p c f -> p (s c) f"))\
                        .then_inc(w_raw[s], 16)
                copy_cache(sp, 0, x)

        def act_consts(act):
            act.dma_start(consts, t["consts"]).then_inc(consts_in, 16)
            for dst, name in ((convw, "conv_w"), (convb, "conv_b"), (dtb, "dt_bias"), (alog, "a_log"), (dskip, "d_skip")):
                act.dma_start(dst, t[name]).then_inc(consts_in, 16)

        def act_project(act):
            for c in range(DC):
                act.wait_ge(x_in[c // 4], 16)
                act.copy(xs[0][:, c, 0:TOK], xraw[:, c]).then_inc(x_hi, 1)
            act.wait_ge(dtw_in, 32)
            act.copy(dtw[0], dtw_raw).then_inc(x_hi, 1)

            def hi(x, s, free):
                act.wait_ge(w_raw[s], x * 16 + 16)
                act.wait_ge(*free)
                act.copy(ws[0][:, s], wraw[:, s]).then_inc(w_hi, 1)

            with act.Fori(0, 4) as x:
                for s in range(4):
                    hi(x, s, (feat_ready, x * 4 + (s + 1)))
            act_dt(act)
            with act.Fori(0, 4) as x:
                for s in range(4):
                    hi(x + 4, s, (feat_ready, x * 4 + (s + 17)))
                    if s < 3:
                        silu(act, x * 3 + s)
            with act.Fori(0, 3) as x:
                for s in range(4):
                    hi(x + 8, s, (rows_ready, x * 10 + (5 if s < 2 else 10)))

        def pool_project(pool):
            pool.sem_inc(w_lo, 4)
            pool.memset(nothing, 0.0).then_inc(x_pad, 1)
            pool.wait_ge(x_pad, 1)
            for k in range(2):
                pool.tensor_copy(xs[k][:, :, TOK:], nothing.unsqueeze(1).to_broadcast([P, DC, TPAD - TOK])).then_inc(x_pad, 1)
            pool.memset(xbc[:, :, 0:3], 0.0).then_inc(zeroed, 1)
            pool.memset(dt, 0.0).then_inc(zeroed, 1)
            with pool.Fori(0, BLOCKS // 4) as x:
                for s in range(4):
                    pool.wait_ge(w_hi, x * 4 + (s + 1))
                    pool.tensor_tensor(ws[1][:, s], wraw[:, s], ws[0][:, s].bitcast(F32), ALU.subtract).then_inc(w_lo, 1)

        def dve_split_x(dve):
            for c in range(DC):
                dve.wait_ge(x_hi, c + 1)
                dve.tensor_tensor(xs[1][:, c, 0:TOK], xraw[:, c], xs[0][:, c, 0:TOK].bitcast(F32), ALU.subtract).then_inc(x_lo, 1)
            dve.wait_ge(x_hi, DC + 1)
            dve.tensor_tensor(dtw[1], dtw_raw, dtw[0].bitcast(F32), ALU.subtract).then_inc(x_lo, 1)

        def pe_project(pe):
            pe.sem_inc(feat_ready, 4)
            pe.wait_ge(x_lo, DC + 1)
            pe.wait_ge(x_pad, 3)

            def tokens(c, i):
                return tuple(x[:, c, i * P:(i + 1) * P] for x in xs)

            for i in range(TILES):
                for c in range(DC):
                    mm = product(pe, bank[:, 6, i * H:(i + 1) * H], tokens(c, i), [w[:, c] for w in dtw], c == 0, c == DC - 1)
            mm.then_inc(dt_ready, 1)

            with pe.Fori(0, FT // 4) as x:
                for s in range(4):
                    j = x * 4 + s
                    pe.wait_ge(w_lo, j + 5)
                    pe.wait_ge(feat_kept, j + 1)
                    for half in range(2):
                        for c in range(DC):
                            mm = product(pe, bank[:, 2 * (s % 2) + half, 0:HALF], [w[:, s, c] for w in ws],
                                         [v[:, c, half * HALF:(half + 1) * HALF] for v in xs], c == 0, c == DC - 1)
                    mm.then_inc(feat_ready, 1)

            with pe.Fori(0, VG // 2) as x:
                for n in range(2 * TILES):
                    s, i = n // TILES, n % TILES
                    if i == 0:
                        pe.wait_ge(w_lo, x * 4 + (FT + 2 * s + 6))
                    pe.wait_ge(rows_kept, x * 10 + (n + 1))
                    for c in range(DC):
                        mm = product(pe, bank[:, 4 + n % 2, 0:2 * P], tokens(c, i), [w[:, 2 * s:2 * s + 2, c] for w in ws],
                                     c == 0, c == DC - 1)
                    mm.then_inc(rows_ready, 1)

        def dve_project(dve):
            def keep(j, s, dst):
                dve.wait_ge(feat_ready, j + 5)
                dve.tensor_copy(dst.rearrange("p o (h n) -> p (o h) n", h=2),
                                bank[:, 2 * (s % 2):2 * (s % 2) + 2, 0:HALF]).then_inc(feat_kept, 1)

            with dve.Fori(0, XF // 4) as x:
                for s in range(4):
                    keep(x * 4 + s, s, xbc[:, bass.ds(x * 4 + s, 1), 3:3 + TOK])
            dve_ext(dve)
            dve_dt(dve)
            after["conv0"] = dve_chain.base + dve_chain.n
            with dve.Fori(0, 4) as x:
                dve_chain.enter(x, 3 * 2 * CW)
                for s in range(4):
                    keep(x * 4 + (XF + s), s, qk[:, bass.ds(x * 4 + s, 1)])
                    if s < 3:
                        convolve(dve, x * 3 + s, s)
            dve_chain.leave(4)
            with dve.Fori(0, VG // 2) as x:
                for n in range(2 * TILES):
                    s, i = n // TILES, n % TILES
                    dve.wait_ge(rows_ready, x * 10 + (n + 1))
                    dve.tensor_copy(vz[0:rows(i), i, bass.ds(x * 512 + s * 256, 256)], bank[0:rows(i), 4 + n % 2, 0:2 * P]).then_inc(rows_kept, 1)

        after = {}
        def dve_dt(dve):
            step = dve_chain
            dve.wait_ge(dt_ready, 1)
            dve.wait_ge(consts_in, 96)
            dve.wait_ge(zeroed, 2)
            for i in range(TILES):
                r = rows(i)
                step(dve.tensor_tensor(dt[0:r, i], bank[0:r, 6, i * H:(i + 1) * H], dtb[0:r], ALU.add))
            step.wait(dve)
            after["abs"] = step(dve.scalar_tensor_tensor(tmpa, dt, -1.0, dt, ALU.mult, ALU.max))
            dve.wait_ge(dt_made, 1)
            after["u"] = step(dve.tensor_scalar(tmpb, tmpa, 1.0, None, ALU.add))
            step.wait(dve)
            after["ratio"] = step(dve.tensor_scalar(ratio, tmpb, 1.0, 1e-30, ALU.subtract, ALU.max))
            step.wait(dve)
            step(dve.reciprocal(ratio_r, ratio))
            step.wait(dve)
            step(dve.tensor_tensor(tmpa, tmpa, ratio_r, ALU.mult))
            step.wait(dve)
            dve.wait_ge(dt_made, 3)
            step(dve.tensor_tensor(tmpb, tmpb, tmpa, ALU.mult))
            step.wait(dve)
            step(dve.scalar_tensor_tensor(dt, dt, 0.0, tmpb, ALU.max, ALU.add))
            step.wait(dve)
            after["dA"] = step(dve.scalar_tensor_tensor(
                dA, dt, -1.0, negA.unsqueeze(1).to_broadcast([P, TILES, H]), ALU.mult, ALU.mult))

        def act_dt(act):
            act.wait_ge(dve_chain.sem, after["abs"])
            act.activation(tmpa, tmpa, ACT.Exp, scale=-1.0).then_inc(dt_made, 1)
            act.activation(negA, alog, ACT.Exp).then_inc(dt_made, 1)
            act.wait_ge(dve_chain.sem, after["ratio"])
            act.activation(tmpb, tmpb, ACT.Ln).then_inc(dt_made, 1)

        def dve_ext(dve):
            extv = ext.rearrange("p f (b w) -> p f b w", w=7)
            dve.wait_ge(feat_kept, XF + 2)
            dve.wait_ge(dtw_in, 32)
            dve_chain(dve.tensor_copy(extv[:, :, :, 0:3], oldconv.rearrange("p f (b w) -> p f b w", w=3)))
            dve_chain(dve.tensor_copy(extv[:, :, :, 3:7], xbc[:, :, 3 + SEQ:].rearrange("p f (b w) -> p f b w", w=4)))
            after["ext"] = dve_chain(dve.tensor_copy(ctail, xbc[:, :, SEQ:SEQ + 3]))
            dve_chain.wait(dve)

        def convolve(dve, f, n):
            step = dve_chain
            extv = ext.rearrange("p f (b w) -> p f b w", w=7)
            dve.wait_ge(silu_done, f + 1)
            o = bass.ds(f, 1)
            out = ctmp[:, n % 2]
            outs = out[:, SEQ:].rearrange("p (b w) -> p b w", w=NT)
            for k in range(CW):
                w = convw[:, o, k:k + 1].rearrange("p o k -> p (o k)")
                a = xbc[:, o, k:k + SEQ].rearrange("p o n -> p (o n)")
                b = extv[:, o, :, k:k + NT].rearrange("p o b w -> p (o b) w")
                if k == 0:
                    step(dve.tensor_scalar(out[:, 0:SEQ], a, w, convb[:, o], ALU.mult, ALU.add))
                    step(dve.tensor_scalar(outs, b, w, convb[:, o], ALU.mult, ALU.add))
                else:
                    dve.wait_ge(step.sem, step.base + (step.n - 1))
                    step(dve.scalar_tensor_tensor(out[:, 0:SEQ], a, w, out[:, 0:SEQ], ALU.mult, ALU.add))
                    dve.wait_ge(step.sem, step.base + (step.n - 1))
                    step(dve.scalar_tensor_tensor(outs, b, w, outs, ALU.mult, ALU.add))

        def silu(act, f):
            act.wait_ge(dve_chain.sem, f * (2 * CW) + (after["conv0"] + 2 * CW))
            n = silu_slot[0] % 3 % 2
            silu_slot[0] += 1
            act.activation(xc[:, bass.ds(f, 1)].rearrange("p o n -> p (o n)"), ctmp[:, n], ACT.Silu).then_inc(silu_done, 1)

        silu_slot = [0]

        def sp_states(sp):
            sp.wait_ge(feat_kept, FT + 2)
            store(sp, t["o_kT"], qk[:, 8:16])
            sp.wait_ge(dve_chain.sem, after["ext"])
            store(sp, t["o_conv"], ctail)
            store(sp, t["o_ext"], ext)
            sp.wait_ge(rows_kept, 4 * TILES + 2)
            store(sp, t["o_v"].rearrange("(i p) n -> p i n", p=P), vz[:, 0:QT, 0:D])
            sp.dma_start(t["o_vs"], vz[0:NS, QT, 0:D]).then_inc(vs_stored, 16)

        UNITS = H * QT
        s_free, exp_done, turned, pt_kept, pv_done, att_kept = (
            sem(n) for n in ("s_free", "exp_done", "turned", "pt_kept", "pv_done", "att_kept"))

        def units(pp):
            for n in range(16):
                yield n, n // 8, (n // 4) % 2, n % 4, pp * 16 + n

        def sp_bias(sp):
            sp.wait_ge(rows_ready, VG * TILES)
            for s in range(2):
                sp.dma_start(bst[:, s], t["prompt_bias"][s]).then_inc(bias_in[s], 16)
            with sp.Fori(1, H // 2) as k:
                for s in range(2):
                    sp.wait_ge(s_free, k * 8 + (4 * s - 4 + 2))
                    sp.dma_start(bst[:, s], t["prompt_bias"][bass.ds(k * 2 + s, 1)].rearrange("h p n -> p (h n)"))\
                        .then_inc(bias_in[s], 16)
                copy_cache(sp, 1, k - 1)

        def pool_stage(pool):
            pool.wait_ge(rows_ready, VG * TILES)

            def pair(p, s):
                for dst, lo in ((qst, 0), (kst, 8)):
                    pool.tensor_copy(dst[:, s], qk[:, bass.ds(p + lo, 1), 0:SEQ].rearrange("p o n -> p (o n)")).then_inc(staged, 1)

            pool.wait_ge(feat_kept, FT + 2)
            for s in range(2):
                pair(s, s)
            with pool.Fori(1, H // 4) as k:
                for s in range(2):
                    pool.wait_ge(scores_ready, k * 16 + (8 * s - 8))
                    pair(k * 2 + s, s)

        def pe_attend(pe):
            pe.sem_inc(turned, 2)
            pe.sem_inc(pv_done, 2)
            pe.wait_ge(feat_kept, FT + 2)
            pe.wait_ge(rows_kept, VG * TILES + 2)
            pe.wait_ge(dve_chain.sem, after["dA"])

            def scores(n, s, r, i, u):
                if i == 0 and r == 0:
                    pe.wait_ge(staged, pp * 4 + (2 * s + 2))
                pe.wait_ge(s_free, u + 1)
                k = (i + 1) * P
                pe.matmul(bank[:, n % 2, 0:k], qst[E * r:E * r + E, s, i * P:(i + 1) * P], kst[E * r:E * r + E, s, 0:k],
                          start=True, stop=True).then_inc(scores_ready, 1)

            def turn(n, s, r, i, u):
                pe.wait_ge(exp_done, u + 3)
                pe.wait_ge(pt_kept, u + 1)
                for kt in range(i + 1):
                    mm = pe.transpose(bank[:, 2 + n % 2, kt * P:(kt + 1) * P], pst[:, n % 2, kt * P:(kt + 1) * P], ident)
                mm.then_inc(turned, 1)

            def values(n, s, r, i, u):
                pe.wait_ge(pt_kept, u + 3)
                pe.wait_ge(att_kept, u + 1)
                for kt in range(i + 1):
                    mm = pe.matmul(bank[:, 4 + n % 2, 0:E], ptst[:, n % 2, kt * P:(kt + 1) * P],
                                   vz[:, kt, bass.ds(pp * (4 * E) + (2 * s + r) * E, E)], start=(kt == 0), stop=(kt == i))
                mm.then_inc(pv_done, 1)

            with pe.Fori(0, H // 4) as pp:
                us = list(units(pp))
                for n in range(16 + 2):
                    if n < 16:
                        scores(*us[n])
                    if 1 <= n <= 16:
                        turn(*us[n - 1])
                    if n >= 2:
                        values(*us[n - 2])
            pe.wait_ge(att_kept, UNITS + 2)
            for n in range(2 * QT):
                i, c0 = n // 2, 4 * (n % 2)
                if n >= 2:
                    pe.wait_ge(attT_kept, n - 1)
                for c in range(4):
                    mm = pe.transpose(bank[:, 6 + n % 2, c * P:(c + 1) * P], att[:, i, (c0 + c) * P:(c0 + c + 1) * P], ident)
                mm.then_inc(attT_ready, 1)

        def dve_attend(dve):
            dve.sem_inc(s_free, 2)
            dve.sem_inc(att_kept, 2)

            def bias(n, s, r, i, u):
                if i == 0:
                    dve.wait_ge(bias_in[r], pp * 32 + (16 * s + 16))
                dve.wait_ge(scores_ready, u + 1)
                dve.wait_ge(exp_done, u + 1)
                k = (i + 1) * P
                dve.scalar_tensor_tensor(sst[:, n % 2, 0:k], bank[:, n % 2, 0:k], E ** -0.5, bst[:, r, SEQ - k:SEQ],
                                         ALU.mult, ALU.add).then_inc(s_free, 1)
                dve.wait_ge(s_free, u + 3)
                dve.tensor_reduce(nmax[:, n % 4:n % 4 + 1], sst[:, n % 2, 0:k], AX.X, ALU.max, negate=True).then_inc(max_ready, 1)

            def norm(n, s, r, i, u):
                dve.wait_ge(exp_done, u + 3)
                dve_chain(dve.reciprocal(rden[:, n % 4:n % 4 + 1], den[:, n % 4:n % 4 + 1]))
                dve_chain.wait(dve)
                dve.wait_ge(pv_done, u + 3)
                dve.tensor_scalar(att[:, i, bass.ds(pp * (4 * E) + (2 * s + r) * E, E)], bank[:, 4 + n % 2, 0:E],
                                  rden[:, n % 4:n % 4 + 1], None, ALU.mult).then_inc(att_kept, 1)

            with dve.Fori(0, H // 4) as pp:
                dve_chain.enter(pp, 16)
                us = list(units(pp))
                for n in range(16 + 2):
                    if n < 16:
                        bias(*us[n])
                    if n >= 2:
                        norm(*us[n - 2])
            dve_chain.leave(H // 4)

        def act_attend(act):
            act.sem_inc(exp_done, 2)
            act.sem_inc(pt_kept, 2)

            def exp(n, s, r, i, u):
                act.wait_ge(max_ready, u + 1)
                act.wait_ge(turned, u + 1)
                k = (i + 1) * P
                act.activation(pst[:, n % 2, 0:k], sst[:, n % 2, 0:k], ACT.Exp, bias=nmax[:, n % 4:n % 4 + 1],
                               accum_out=den[:, n % 4:n % 4 + 1]).then_inc(exp_done, 1)

            def keep(n, s, r, i, u):
                act.wait_ge(turned, u + 3)
                act.wait_ge(pv_done, u + 1)
                k = (i + 1) * P
                act.copy(ptst[:, n % 2, 0:k], bank[:, 2 + n % 2, 0:k]).then_inc(pt_kept, 1)

            with act.Fori(0, H // 4) as pp:
                us = list(units(pp))
                for n in range(16 + 1):
                    if n < 16:
                        exp(*us[n])
                    if n >= 1:
                        keep(*us[n - 1])
            for n in range(2 * QT):
                i, c0 = n // 2, 4 * (n % 2)
                act.wait_ge(attT_ready, n + 1)
                act.copy(mixT[:, c0:c0 + 4, i * P:(i + 1) * P], bank[:, 6 + n % 2, :].rearrange("p (c n) -> p c n", c=4)).then_inc(attT_kept, 1)

        k_in = [sem(f"k_in{s}") for s in range(2)]
        v_in = [sem(f"v_in{s}") for s in range(3)]
        vnew_in, qd_ready, k_used, v_used = (sem(n) for n in ("vnew_in", "qd_ready", "k_used", "v_used"))
        d_biased, d_max, d_exp, d_scaled, d_turned, d_kept, d_pv, d_out = (
            sem(n) for n in ("d_biased", "d_max", "d_exp", "d_scaled", "d_turned", "d_kept", "d_pv", "d_out"))
        sbias_in, ks_turned, ks_kept = sem("sbias_in"), sem("ks_turned"), sem("ks_kept")
        ROWS = H * NT
        vslot = [vring[:, s] for s in range(6)] + [vring2[:, 0]]
        qflat = [cut(197.5 + 2.25 * s, 9 * 64) for s in range(2)]
        KH = KEYS // 2
        HR = ROWS // 2
        osb = cut(118, D)
        TW = HR + 4 * NT
        d_rows, d_back = sem("d_rows"), sem("d_back")

        def sp_samples(sp):
            sp.wait_ge(rows_kept, VG * TILES + 2)
            sp.dma_start(sbias[0:ROWS], t["sample_bias"]).then_inc(sbias_in, 16)

            def keys_of(b0, first):
                for c in range(0, DC, 2):
                    if not (first and c < 4):
                        sp.wait_ge(k_used, b0 * DC + (c - 2 + 2 * DC))
                    s = c // 2 % 2
                    sp.dma_start(kring[:, 2 * s:2 * s + 2, 0:KEYS], t["cache_kT"][bass.ds(b0, 1), c:c + 2].rearrange("b c p n -> p (b c) n"))\
                        .then_inc(k_in[s], 16)

            keys_of(0, True)
            sp.wait_ge(ks_kept, 1)
            sp.wait_ge(vs_stored, 16)
            for b in range(NB):
                store(sp, t["o_ks"][b, WIN - NT:], ksam[b * NT:(b + 1) * NT])
                store(sp, t["o_vsall"][b, WIN - NT:], vz[b * NT:(b + 1) * NT, QT, 0:D])
            with sp.Fori(1, NB) as b:
                keys_of(b, False)

        def pool_qdiag0(pool):
            pool.wait_ge(silu_done, XF + 1)
            for s in range(2):
                pool.memset(qflat[s], 0.0).then_inc(zeroed, 1)

        def dve_samples(dve):
            dve.wait_ge(zeroed, 4)
            dve.wait_ge(sbias_in, 16)
            dve.sem_inc(d_biased, 1)
            dve.sem_inc(d_out, 3)
            dve.sem_inc(d_rows, 1)

            def place_q(s, b):
                dve.wait_ge(k_used, b * DC + DC)
                for r in range(2):
                    dst = qflat[s].rearrange("p (c w) -> p c w", w=72)
                    dve.tensor_copy(dst[E * r:E * r + E, :, NT * r:NT * r + NT],
                                    qk[E * r:E * r + E, 0:DC, bass.ds(b * NT + SEQ, NT)]).then_inc(qd_ready, 1)

            def soft(b):
                dve.wait_ge(k_used, b * DC + 3 * DC)
                dve.wait_ge(d_exp, b + 1)
                dve_chain(dve.scalar_tensor_tensor(sdec[0:ROWS, 0:KEYS].rearrange("p (h n) -> p h n", h=2), bank[0:ROWS, 0:2, 0:KH],
                                                   E ** -0.5, sbias[0:ROWS, 0:KEYS].rearrange("p (h n) -> p h n", h=2), ALU.mult, ALU.add))
                dve.scalar_tensor_tensor(sdec[0:ROWS, KEYS:KALL], bank[0:ROWS, 2, 0:NT], E ** -0.5, sbias[0:ROWS, KEYS:KALL],
                                         ALU.mult, ALU.add).then_inc(d_biased, 1)
                dve.wait_ge(d_biased, b + 2)
                dve.tensor_reduce(nmax[0:ROWS, 0:1], sdec[0:ROWS, :], AX.X, ALU.max, negate=True).then_inc(d_max, 1)
                dve.wait_ge(d_exp, b + 2)
                dve_chain(dve.reciprocal(rden[0:ROWS, 0:1], den[0:ROWS, 0:1]))
                dve_chain.wait(dve)
                dve.tensor_scalar(pdec[0:ROWS, :], pdec[0:ROWS, :], rden[0:ROWS, 0:1], None, ALU.mult).then_inc(d_scaled, 1)

            def rows_out(b):
                dve.wait_ge(d_pv, b + 2)
                dve.wait_ge(d_back, b + 1)
                dve.tensor_copy(osb[0:HR].rearrange("p (h n) -> p h n", h=2), bank[0:HR, 6:8, :]).then_inc(d_rows, 1)

            def keep(b):
                dve.wait_ge(d_back, b + 2)
                for r in range(2):
                    src = bank[:, 3, 0:DC * TW].rearrange("p (c w) -> p c w", w=TW)
                    dve.tensor_copy(mixT[E * r:E * r + E, 0:DC, bass.ds(b * NT + SEQ, NT)],
                                    src[E * r:E * r + E, :, NT * r:NT * r + NT]).then_inc(d_out, 1)

            def between(b, s, more=True):
                soft(b)
                if more:
                    place_q(s, b + 2)
                keep(b - 1)
                rows_out(b)

            place_q(0, 0)
            place_q(1, 1)
            soft(0)
            place_q(0, 2)
            rows_out(0)
            with dve.Fori(0, NB // 2 - 2) as bb:
                dve_chain.enter(bb, 4)
                between(bb * 2 + 1, 1)
                between(bb * 2 + 2, 0)
            dve_chain.leave(NB // 2 - 2)
            between(NB - 3, 1)
            between(NB - 2, 0, False)
            between(NB - 1, 1, False)
            keep(NB - 1)

        def act_samples(act):
            act.sem_inc(d_exp, 1)
            act.sem_inc(d_kept, 1)

            def exp(b):
                act.wait_ge(d_max, b + 1)
                act.wait_ge(d_turned, b + 1)
                act.activation(pdec[0:ROWS, :], sdec[0:ROWS, :], ACT.Exp, bias=nmax[0:ROWS, 0:1], accum_out=den[0:ROWS, 0:1]).then_inc(d_exp, 1)

            def keep(b):
                act.wait_ge(d_turned, b + 2)
                act.wait_ge(d_pv, b + 1)
                act_chain(act.copy(ptdec, bank[:, 4, 0:KB * ROWS].rearrange("p (k n) -> p k n", n=ROWS)))
                act.copy(ptnew[0:NT], bank[0:NT, 5, 0:ROWS]).then_inc(d_kept, 1)

            act.wait_ge(ks_turned, 1)
            act.copy(ksam[0:NS].rearrange("p (b n) -> p b n", b=2), bank[0:NS, 6:8, :]).then_inc(ks_kept, 1)
            def values_of(b0, first):
                for n, (lo, hi, dst) in enumerate(((0, 3, vring[:, 0:3]), (3, 6, vring[:, 3:6]), (6, 7, vring2))):
                    if not first:
                        act.wait_ge(v_used, b0 * KB + (hi - KB))
                    act.dma_start(dst, t["cache_v"][bass.ds(b0, 1), lo:hi].rearrange("b k p n -> p (b k) n")).then_inc(v_in[n], 16)
                if not first:
                    act.wait_ge(d_pv, b0 + 1)
                act.dma_start(vnew[0:NT], t["o_vs"][bass.ds(b0 * NT, NT)]).then_inc(vnew_in, 16)

            act.wait_ge(vs_stored, 16)
            values_of(0, True)
            act_chain.enter(0, 1)
            exp(0)
            keep(0)
            act_chain.leave(1)
            with act.Fori(0, NB - 1) as x:
                act_chain.enter(x, 1)
                values_of(x + 1, False)
                exp(x + 1)
                keep(x + 1)
            act_chain.leave(NB - 1)

        def pe_samples(pe):
            pe.sem_inc(k_used, 2 * DC)
            pe.sem_inc(d_turned, 1)
            pe.sem_inc(d_pv, 1)
            pe.sem_inc(d_back, 1)

            def scores(b, s):
                pe.wait_ge(qd_ready, b * 2 + 2)
                pe.wait_ge(d_biased, b + 1)
                for c in range(DC):
                    if c % 2 == 0:
                        pe.wait_ge(k_in[c // 2 % 2], b * 32 + 16 * (c // 4 + 1))
                    lhsT = qflat[s][:, c * 64:c * 64 + ROWS]
                    pe.matmul(bank[0:ROWS, 2, 0:NT], lhsT, qk[:, DC + c, bass.ds(b * NT + SEQ, NT)], start=(c == 0), stop=(c == DC - 1))
                    pe.matmul(bank[0:ROWS, 0, 0:KH], lhsT, kring[:, c % 4, 0:KH], start=(c == 0), stop=(c == DC - 1))
                    pe.matmul(bank[0:ROWS, 1, 0:KH], lhsT, kring[:, c % 4, KH:KEYS], start=(c == 0), stop=(c == DC - 1)).then_inc(k_used, 1)

            def tail(b, s):
                pe.wait_ge(d_scaled, b + 1)
                pe.wait_ge(d_kept, b + 1)
                for kb in range(KB):
                    turn = pe.matmul if kb == 0 else pe.transpose
                    turn(bank[:, 4, kb * ROWS:(kb + 1) * ROWS], pdec[0:ROWS, kb * P:(kb + 1) * P], ident[0:ROWS, 0:ROWS])
                pe.transpose(bank[0:NT, 5, 0:ROWS], pdec[0:ROWS, KEYS:KALL], ident[0:ROWS, 0:ROWS]).then_inc(d_turned, 1)
                pe.wait_ge(d_kept, b + 2)
                pe.wait_ge(d_rows, b + 1)
                for kb in range(KB + 1):
                    if kb < KB and kb % 3 == 0:
                        pe.wait_ge(v_in[kb // 3], b * 16 + 16)
                    if kb == KB - 1:
                        pe.wait_ge(vnew_in, b * 16 + 16)
                    for half in range(2):
                        m, n = slice(half * HR, (half + 1) * HR), slice(half * 512, (half + 1) * 512)
                        w, v = (ptdec[:, kb, m], vslot[kb][:, n]) if kb < KB else (ptnew[0:NT, m], vnew[0:NT, n])
                        mm = pe.matmul(bank[0:HR, 6 + half, :], w, v, start=(kb == 0), stop=(kb == KB))
                    mm.then_inc(v_used, 1) if kb < KB else mm.then_inc(d_pv, 1)

            def turn_out(b):
                pe.wait_ge(d_rows, b + 2)
                pe.wait_ge(d_out, b * 2 + 3)
                for c in range(DC):
                    lo = c * TW - 2 * NT * (c % 4)
                    mm = pe.matmul(bank[:, 3, lo:lo + HR], osb[0:HR, c * P:(c + 1) * P], ident[0:HR, 0:HR], start=True, stop=True)
                mm.then_inc(d_back, 1)

            pe.wait_ge(attT_kept, 2 * QT)
            for c in range(DC):
                mm = pe.transpose(bank[0:NS, 6 + c // 4, (c % 4) * P:(c % 4 + 1) * P], qk[:, DC + c, SEQ:], ident)
            mm.then_inc(ks_turned, 1)
            pe.wait_ge(ks_kept, 1)
            scores(0, 0)
            scores(1, 1)
            tail(0, 0)
            with pe.Fori(0, NB // 2 - 1) as bb:
                for r in range(2):
                    b = bb * 2 + (r + 1)
                    scores(b + 1, r)
                    turn_out(b - 1)
                    tail(b, 1 - r)
            turn_out(NB - 2)
            tail(NB - 1, 1)
            turn_out(NB - 1)
        class Events:

            def __init__(self, sem, names):
                self.sem, self.counts, n = sem, {}, 0
                for i in range(TILES):
                    for name in names(i):
                        n += 1
                        self.counts[i, name] = n
                self.seen = 0

            def count_done(self, i, name, instruction):
                self.seen += 1
                assert self.counts[i, name] == self.seen, (i, name)
                instruction.then_inc(self.sem, 1)

            def wait(self, eng, i, name):
                eng.wait_ge(self.sem, self.counts[i, name])

        heads4 = range(4)
        seqs = range(NB)
        pe_ssd = Events(sem("pe_ssd"), lambda i:
            ["x_turned", "sums", "cb", "seg0", "seg1"] + (["out_turned"] if i else []) + (["inter"] if i < QT else []) +
            ["y0", "seg2", "y1", "seg3", "y2", "y3"] + (["state"] if i < QT else [f"state{b}" for b in seqs] + ["last_turned"]))
        act_ssd = Events(sem("act_ssd"), lambda i:
            ["x_kept", "b_kept", "eacs", "etot", "cb_kept"] + (["out_kept"] if i else []) + ["wexp", "E0", "E1", "E2", "E3", "zsilu", "sq0", "sq1", "root"] +
            (["last_kept"] if i == QT else []))
        dve_ssd = Events(sem("dve_ssd"), lambda i:
            ["wdiff", "xdt", "xw"] + (["bmask"] if i == QT else []) + ["M0", "M1", "M2", "M3"] +
            ([x for b in seqs for x in (f"hd{b}", f"hn{b}")] if i == QT else ["hd", "hn"]) +
            ["t_inter", "y_add", "xD", "y_full", "u", "var", "rstd", "n0", "n1"])
        pool_ssd = Events(sem("pool_ssd"), lambda i: (["dam", "cmask0", "cmask1"] if i == QT else []) + ["X0", "X1", "X2", "X3"])
        normg_in = sem("normg_in")
        h0_in = [sem(f"h0_in{s}") for s in range(2)]
        hn_stored = [sem(f"hn_stored{s}") for s in range(2)]

        xtok, btok = cut(10, D), cut(18, GR, N)
        xdt, xw = cut(20, D), cut(24, D)
        hT = cut(28, 2, D)
        yb, yu = cut(36, D), cut(40, D)
        esb, xsb, msb = cut(153, 2, 4, P), cut(157, 2, 4, P), cut(161, 2, 4, P)
        cbs = cut(165, GR, P)
        normg, zs = cut(166, D), cut(170, D)
        yo = cut(174, D)
        h0, hn = cut(179, 2, D), cut(187, 2, D)
        cm = cut(195, GR, NB, NS)
        bm = cut(197, NB, GR * N)
        ssq = stat[:, 0:2]
        rstd = stat[:, 2:4]

        def per_head(v, r, heads=H):
            return v.unsqueeze(2).to_broadcast([r, heads, E])

        def by_head(a, r):
            return a[0:r].rearrange("p (h e) -> p h e", e=E)

        def two_banks(b, r):
            return bank[0:r, b:b + 2, :].rearrange("p b (h e) -> p (b h) e", e=E)

        def sp_ssd(sp):
            sp.wait_ge(d_out, 3 + 2 * NB)
            sp.dma_start(normg, t["ssm_norm_g"]).then_inc(normg_in, 16)
            for b in seqs:
                if b >= 2:
                    pe_ssd.wait(sp, QT, f"state{b - 2}")
                    dve_ssd.wait(sp, QT, f"hd{b - 2}")
                sp.dma_start(h0[:, b % 2], t["state_ssm"][b]).then_inc(h0_in[b % 2], 16)
                if b == 1:
                    for x in range(11, 16):
                        copy_cache(sp, 0, x)
            dve_ssd.wait(sp, QT - 1, "hn")
            store(sp, t["o_hp"], hT[:, QT % 2])

        def act_store_states(act, b):
            dve_ssd.wait(act, QT, f"hn{b}")
            act.dma_start(t["o_hs"][b], hn[:, b % 2]).then_inc(hn_stored[b % 2], 16)

        def pool_ssd_run(pool):
            pool.wait_ge(d_out, 3 + 2 * NB)
            pool.wait_ge(dve_chain.sem, after["dA"])
            pool.memset(hT[:, 0], 0.0).then_inc(zeroed, 1)
            for i in range(TILES):
                r, sfx = rows(i), "" if i < QT else "_s"
                if i == QT:
                    pool_ssd.count_done(i, "dam", pool.tensor_tensor(
                        dAm[0:r].rearrange("p (b h) -> p b h", h=H), dA[0:r, i].unsqueeze(1).to_broadcast([r, NB, H]),
                        const("seqrow")[0:r].unsqueeze(2).to_broadcast([r, NB, H]), ALU.mult))
                    for g in range(GR):
                        pool_ssd.count_done(i, f"cmask{g}", pool.tensor_tensor(
                            cm[:, g], xc[:, 10 + g, SEQ:].unsqueeze(1).to_broadcast([P, NB, NS]),
                            const("seqcol").rearrange("p (b n) -> p b n", n=NS), ALU.mult))
                for q in heads4:
                    if q >= 2:
                        pe_ssd.wait(pool, i, f"seg{q - 2}")
                    elif i > 0:
                        pe_ssd.wait(pool, i - 1, f"seg{q + 2}")
                    pool_ssd.count_done(i, f"X{q}", pool.tensor_tensor(
                        xsb[0:r, q % 2, :, 0:r], const("tri" + sfx)[0:r, 0:r].unsqueeze(1).to_broadcast([r, 4, r]),
                        dA[0:r, i, 4 * q:4 * q + 4].unsqueeze(2).to_broadcast([r, 4, r]), ALU.mult))

        def pe_ssd_run(pe):
            pe.wait_ge(d_out, 3 + 2 * NB)
            pe.wait_ge(silu_done, XF + 1)
            for i in range(TILES):
                r, sfx, c0 = rows(i), "" if i < QT else "_s", i * P

                def seg(q):
                    pool_ssd.wait(pe, i, f"X{q}")
                    if q >= 2:
                        act_ssd.wait(pe, i, f"E{q - 2}")
                    o = bank[0:r, 4 + q % 2, 0:4 * r].rearrange("p (h n) -> p h n", n=r)
                    pe.matmul(o, ones[0:r, 0:r], xsb[0:r, q % 2, :, 0:r], start=True, stop=False)
                    pe.matmul(o, const("ntri" + sfx)[0:r, 0:r], dA[0:r, i, 4 * q:4 * q + 4].unsqueeze(2).to_broadcast([r, 4, r]),
                              start=False, stop=False)
                    pe_ssd.count_done(i, f"seg{q}", pe.matmul(o, ident[0:r, 0:r],
                                  const("hide" + sfx)[0:r, 0:r].unsqueeze(1).to_broadcast([r, 4, r]), start=False, stop=True))

                def intra(q):
                    dve_ssd.wait(pe, i, f"M{q}")
                    for k in range(4):
                        h = 4 * q + k
                        mm = pe.matmul(bank[0:r, 6 + h // 8, (h % 8) * E:(h % 8 + 1) * E], msb[0:r, q % 2, k, 0:r],
                                       xdt[0:r, h * E:(h + 1) * E], start=True, stop=True)
                    pe_ssd.count_done(i, f"y{q}", mm)

                def turn_out(n):
                    dve_ssd.wait(pe, n, "n1")
                    for c in range(8):
                        mm = pe.transpose(bank[:, c // 4, (c % 4) * P:(c % 4) * P + rows(n)], yo[0:rows(n), c * P:(c + 1) * P],
                                          ident[0:rows(n), 0:rows(n)])
                    return mm

                if i:
                    dve_ssd.wait(pe, i - 1, "y_add")
                    act_ssd.wait(pe, i - 1, "cb_kept")
                for c in range(8):
                    pe.transpose(bank[0:r, c // 4, (c % 4) * P:(c % 4 + 1) * P], xc[:, c, c0:c0 + r], ident)
                for g in range(GR):
                    mm = pe.transpose(bank[0:r, 2, g * N:(g + 1) * N], xc[:, 8 + g, c0:c0 + r], ident)
                pe_ssd.count_done(i, "x_turned", mm)

                if i == 0:
                    pe.wait_ge(dve_chain.sem, after["dA"])
                pe.matmul(bank[0:r, 3, 0:H], const("tri" + sfx)[0:r, 0:r], dA[0:r, i], start=True, stop=True)
                end = ones if i < QT else const("same_s")
                mm = pe.matmul(bank[0:r, 3, H:2 * H], end[0:r, 0:r], dA[0:r, i], start=True, stop=True)
                if i == QT:
                    pool_ssd.wait(pe, i, "dam")
                    mm = pe.matmul(bank[:, 3, 2 * H:2 * H + NB * H], ones[0:r, :], dAm[0:r], start=True, stop=True)
                pe_ssd.count_done(i, "sums", mm)
                act_ssd.wait(pe, i, "b_kept")
                for g in range(GR):
                    mm = pe.matmul(bank[0:r, 2, g * r:(g + 1) * r], xc[:, 8 + g, c0:c0 + r], xc[:, 10 + g, c0:c0 + r],
                                   start=True, stop=True)
                pe_ssd.count_done(i, "cb", mm)
                seg(0)
                seg(1)
                act_ssd.wait(pe, i, "x_kept")
                if i:
                    pe_ssd.count_done(i, "out_turned", turn_out(i - 1))
                    act_ssd.wait(pe, i, "out_kept")
                if i < QT:
                    if i == 0:
                        pe.wait_ge(zeroed, 5)
                    else:
                        dve_ssd.wait(pe, i - 1, "hn")
                    for g in range(GR):
                        mm = pe.matmul(bank[:, g, :], xc[:, 10 + g, c0:c0 + r], hT[:, i % 2, g * 512:(g + 1) * 512], start=True, stop=True)
                    pe_ssd.count_done(i, "inter", mm)
                intra(0)
                seg(2)
                intra(1)
                seg(3)
                intra(2)
                intra(3)
                if i < QT:
                    act_ssd.wait(pe, i, "E3")
                    for g in range(GR):
                        mm = pe.matmul(bank[:, 4 + g, :], btok[:, g], xw[:, g * 512:(g + 1) * 512], start=True, stop=True)
                    pe_ssd.count_done(i, "state", mm)
                else:
                    act_ssd.wait(pe, i, "E3")
                    for b in seqs:
                        pe.wait_ge(h0_in[b % 2], 16 * (b // 2 + 1))
                        if b:
                            dve_ssd.wait(pe, i, f"hn{b - 1}")
                        for g in range(GR):
                            pe.matmul(bank[0:r, g, :], cm[:, g, b], h0[:, b % 2, g * 512:(g + 1) * 512], start=(b == 0), stop=(b == NB - 1))
                            mm = pe.matmul(bank[:, 4 + g, :], bm[0:r, b, g * N:(g + 1) * N], xw[0:r, g * 512:(g + 1) * 512],
                                           start=True, stop=True)
                        pe_ssd.count_done(i, f"state{b}", mm)
                    pe_ssd.count_done(i, "last_turned", turn_out(QT))

        def act_ssd_run(act):
            act.wait_ge(d_out, 3 + 2 * NB)
            for i in range(TILES):
                r = rows(i)

                def keep_out(n, name):
                    act_ssd.count_done(i, name, act.copy(
                        mixT[:, 8:16, n * P:n * P + rows(n)].rearrange("p (b c) n -> p b c n", b=2),
                        bank[:, 0:2, :].rearrange("p b (c n) -> p b c n", n=P)[:, :, :, 0:rows(n)]))

                pe_ssd.wait(act, i, "x_turned")
                if i:
                    dve_ssd.wait(act, i - 1, "xD")
                    pe_ssd.wait(act, i - 1, "state")
                act_ssd.count_done(i, "x_kept", act.copy(xtok[0:r].rearrange("p (b n) -> p b n", b=2), bank[0:r, 0:2, :]))
                act_ssd.count_done(i, "b_kept", act.copy(btok[0:r], bank[0:r, 2, 0:GR * N].rearrange("p (g n) -> p g n", n=N)))
                pe_ssd.wait(act, i, "sums")
                act_ssd.count_done(i, "eacs", act.activation(eacs[0:r], bank[0:r, 3, 0:H], ACT.Exp))
                if i < QT:
                    act_ssd.count_done(i, "etot", act.activation(etot, bank[:, 3, H:2 * H], ACT.Exp))
                else:
                    act_ssd.count_done(i, "etot", act.activation(decs, bank[:, 3, 2 * H:2 * H + NB * H], ACT.Exp))
                pe_ssd.wait(act, i, "cb")
                act_ssd.count_done(i, "cb_kept", act.copy(cbs[0:r, :, 0:r], bank[0:r, 2, 0:GR * r].rearrange("p (g n) -> p g n", n=r)))
                if i:
                    pe_ssd.wait(act, i, "out_turned")
                    keep_out(i - 1, "out_kept")
                dve_ssd.wait(act, i, "wdiff")
                act_ssd.count_done(i, "wexp", act.activation(wend[0:r], wsum[0:r], ACT.Exp))
                for q in heads4:
                    pe_ssd.wait(act, i, f"seg{q}")
                    if q >= 2:
                        dve_ssd.wait(act, i, f"M{q - 2}")
                    act_ssd.count_done(i, f"E{q}", act.activation(
                        esb[0:r, q % 2, :, 0:r], bank[0:r, 4 + q % 2, 0:4 * r].rearrange("p (h n) -> p h n", n=r), ACT.Exp))
                act_ssd.count_done(i, "zsilu", act.activation(zs[0:r], vz[0:r, i, D:2 * D], ACT.Silu))
                if i == QT:
                    for b in seqs:
                        act_store_states(act, b)
                dve_ssd.wait(act, i, "u")
                for g in range(GR):
                    act_ssd.count_done(i, f"sq{g}", act.activation(yu[0:r, g * 512:(g + 1) * 512], yb[0:r, g * 512:(g + 1) * 512], ACT.Square,
                                                               accum_out=ssq[0:r, g:g + 1]))
                dve_ssd.wait(act, i, "var")
                act_ssd.count_done(i, "root", act.activation(rstd[0:r], rstd[0:r], ACT.Sqrt))
                if i == QT:
                    pe_ssd.wait(act, i, "last_turned")
                    keep_out(QT, "last_kept")

        def dve_ssd_run(dve):
            dve.wait_ge(normg_in, 16)
            dve.wait_ge(consts_in, 96)
            for i in range(TILES):
                r = rows(i)
                pe_ssd.wait(dve, i, "sums")
                act_ssd.wait(dve, i, "etot")
                dve_chain(dve.tensor_copy(tmpa[0:r, 0], bank[0:r, 3, 0:H]))
                dve_chain.wait(dve)
                if i:
                    act_ssd.wait(dve, i - 1, "wexp")
                dve_ssd.count_done(i, "wdiff", dve.tensor_tensor(wsum[0:r], bank[0:r, 3, H:2 * H], tmpa[0:r, 0], ALU.subtract))
                act_ssd.wait(dve, i, "x_kept")
                dve_ssd.count_done(i, "xdt", dve.tensor_tensor(by_head(xdt, r), by_head(xtok, r), per_head(dt[0:r, i], r), ALU.mult))
                act_ssd.wait(dve, i, "wexp")
                dve_ssd.wait(dve, i, "xdt")
                dve_ssd.count_done(i, "xw", dve.tensor_tensor(by_head(xw, r), by_head(xdt, r), per_head(wend[0:r], r), ALU.mult))
                if i == QT:
                    dve_ssd.count_done(i, "bmask", dve.tensor_tensor(
                        bm[0:r], btok[0:r].rearrange("p g n -> p (g n)").unsqueeze(1).to_broadcast([r, NB, GR * N]),
                        const("seqrow")[0:r].unsqueeze(2).to_broadcast([r, NB, GR * N]), ALU.mult))
                act_ssd.wait(dve, i, "cb_kept")
                for q in heads4:
                    act_ssd.wait(dve, i, f"E{q}")
                    if q >= 2:
                        pe_ssd.wait(dve, i, f"y{q - 2}")
                    elif i:
                        pe_ssd.wait(dve, i - 1, f"y{q + 2}")
                    dve_ssd.count_done(i, f"M{q}", dve.tensor_tensor(
                        msb[0:r, q % 2, :, 0:r], esb[0:r, q % 2, :, 0:r], cbs[0:r, q // 2, 0:r].unsqueeze(1).to_broadcast([r, 4, r]), ALU.mult))
                if i < QT:
                    if i == 0:
                        dve.wait_ge(zeroed, 5)
                    else:
                        dve_ssd.wait(dve, i - 1, "hn")
                        pe_ssd.wait(dve, i - 1, "inter")
                    dve_ssd.count_done(i, "hd", dve.tensor_tensor(by_head(hT[:, (i + 1) % 2], P), by_head(hT[:, i % 2], P), per_head(etot, P), ALU.mult))
                    pe_ssd.wait(dve, i, "state")
                    dve_ssd.wait(dve, i, "hd")
                    dve_ssd.count_done(i, "hn", dve.tensor_tensor(by_head(hT[:, (i + 1) % 2], P), by_head(hT[:, (i + 1) % 2], P), two_banks(4, P), ALU.add))
                else:
                    for b in seqs:
                        dve.wait_ge(h0_in[b % 2], 16 * (b // 2 + 1))
                        if b >= 2:
                            dve.wait_ge(hn_stored[b % 2], 16 * (b // 2))
                        dve_ssd.count_done(i, f"hd{b}", dve.tensor_tensor(by_head(hn[:, b % 2], P), by_head(h0[:, b % 2], P),
                                                                      per_head(decs[:, b * H:(b + 1) * H], P), ALU.mult))
                        pe_ssd.wait(dve, i, f"state{b}")
                        dve_ssd.wait(dve, i, f"hd{b}")
                        dve_ssd.count_done(i, f"hn{b}", dve.tensor_tensor(by_head(hn[:, b % 2], P), by_head(hn[:, b % 2], P), two_banks(4, P), ALU.add))
                pe_ssd.wait(dve, i, "inter" if i < QT else f"state{NB - 1}")
                if i:
                    act_ssd.wait(dve, i - 1, "sq1")
                dve_ssd.count_done(i, "t_inter", dve.tensor_tensor(by_head(yb, r), two_banks(0, r), per_head(eacs[0:r], r), ALU.mult))
                dve_ssd.wait(dve, i, "t_inter")
                pe_ssd.wait(dve, i, "y3")
                dve_ssd.count_done(i, "y_add", dve.tensor_tensor(by_head(yb, r), by_head(yb, r), two_banks(6, r), ALU.add))
                if i:
                    act_ssd.wait(dve, i - 1, "sq1")
                dve_ssd.count_done(i, "xD", dve.tensor_tensor(by_head(yu, r), by_head(xtok, r), per_head(dskip[0:r], r), ALU.mult))
                dve_ssd.wait(dve, i, "xD")
                dve_ssd.count_done(i, "y_full", dve.tensor_tensor(yb[0:r], yb[0:r], yu[0:r], ALU.add))
                dve_ssd.wait(dve, i, "y_full")
                act_ssd.wait(dve, i, "zsilu")
                dve_ssd.count_done(i, "u", dve.tensor_tensor(yb[0:r], yb[0:r], zs[0:r], ALU.mult))
                act_ssd.wait(dve, i, "sq1")
                dve_ssd.count_done(i, "var", dve.tensor_scalar(rstd[0:r], ssq[0:r], 1.0 / 512, EPS, ALU.mult, ALU.add))
                act_ssd.wait(dve, i, "root")
                dve_ssd.count_done(i, "rstd", dve.reciprocal(rstd[0:r], rstd[0:r]))
                dve_ssd.wait(dve, i, "rstd")
                if i:
                    act_ssd.wait(dve, i, "out_kept")
                for g in range(GR):
                    c = slice(g * 512, (g + 1) * 512)
                    dve_ssd.count_done(i, f"n{g}", dve.scalar_tensor_tensor(yo[0:r, c], yb[0:r, c], rstd[0:r, g:g + 1], normg[0:r, c], ALU.mult, ALU.mult))

        def sp_dump5(sp):
            for s in range(2):
                sp.wait_ge(hn_stored[s], 16 * (NB // 2))
        wout = cut(10, 16, D)
        h1 = cut(186, TILES, D)
        hh = overlay(169, DC, TOK, kind=F32R), overlay(142, DC, TOK, kind=F32R)
        xres, lng, lnb, hpre = cut(118, 2, D), cut(126, D), cut(130, D), cut(134, 2, D)
        bst6, mv = small(784, 2, 12), small(808, 2, 2)
        LN = 8
        wout_in, ln_in, xres_in = [sem(f"wout_in{g}") for g in range(4)], sem("ln_in"), [sem(f"xres_in{s}") for s in range(2)]
        mixed, ln_step, ln_root = sem("mixed"), Steps(sem("ln_step")), sem("ln_root")
        h_turned, h_hi, h_lo = sem("h_turned"), sem("h_hi"), sem("h_lo")
        lnm = {}

        def layer_norm(dve, n, i, dst, g, b, product, loaded):
            r, s, step = rows(i), n % 2, ln_step
            x, residual = hpre[0:r, s], loaded()
            step(dve.scalar_tensor_tensor(x.rearrange("p (b n) -> p b n", b=2), residual.rearrange("p (b n) -> p b n", b=2), ALPHA,
                                          product, ALU.mult, ALU.add))
            lnm["sum", n] = step.base + step.n
            step.wait(dve)
            for k in range(2):
                step(dve.bn_stats(bst6[0:r, s, 6 * k:6 * k + 6], x[:, k * 512:(k + 1) * 512]))
            step.wait(dve)
            step(dve.bn_aggr(mv[0:r, s], bst6[0:r, s]))
            step.wait(dve)
            step(dve.tensor_scalar(mv[0:r, s, 1:2], mv[0:r, s, 1:2], EPS, None, ALU.add))
            lnm["var", n] = step.base + step.n
            dve.wait_ge(ln_root, n + 1)
            step(dve.reciprocal(mv[0:r, s, 1:2], mv[0:r, s, 1:2]))
            step.wait(dve)
            step(dve.tensor_scalar(x, x, mv[0:r, s, 0:1], mv[0:r, s, 1:2], ALU.subtract, ALU.mult))
            step.wait(dve)
            step(dve.tensor_tensor(x, x, g[0:r], ALU.mult))
            step.wait(dve)
            step(dve.tensor_tensor(dst, x, b[0:r], ALU.add))
            lnm["out", n] = step.base + step.n

        def act_root(act, n, i):
            act.wait_ge(ln_step.sem, lnm["var", n])
            act.activation(mv[0:rows(i), n % 2, 1:2], mv[0:rows(i), n % 2, 1:2], ACT.Sqrt).then_inc(ln_root, 1)

        def sp_out(sp):
            act_ssd.wait(sp, QT, "last_kept")
            for g in range(4):
                sp.dma_start(wout[:, 4 * g:4 * g + 4], t["w_out"][:, 4 * g:4 * g + 4]).then_inc(wout_in[g], 16)
            sp.dma_start(lng, t["ln1_g"]).then_inc(ln_in, 16)
            sp.dma_start(lnb, t["ln1_b"]).then_inc(ln_in, 16)
            for i in range(TILES):
                if i >= 2:
                    sp.wait_ge(ln_step.sem, lnm["sum", i - 2])
                sp.dma_start(xres[0:rows(i), i % 2], t["x"][i * P:i * P + rows(i)]).then_inc(xres_in[i % 2], 16)
                copy_cache(sp, 1, 7 + i)

        def pe_out(pe):
            act_ssd.wait(pe, QT, "last_kept")
            for i in range(TILES):
                if i >= 2:
                    pe.wait_ge(ln_step.sem, lnm["sum", i - 2])
                for half in range(2):
                    for c in range(16):
                        if i == 0 and half == 0 and c % 4 == 0:
                            pe.wait_ge(wout_in[c // 4], 16)
                        mm = pe.matmul(bank[0:rows(i), 2 * (i % 2) + half, :], mixT[:, c, i * P:i * P + rows(i)],
                                       wout[:, c, half * 512:(half + 1) * 512], start=(c == 0), stop=(c == 15))
                mm.then_inc(mixed, 1)
                if i:
                    turn_h(pe, i - 1)
            turn_h(pe, QT)

        def turn_h(pe, i):
            pe.wait_ge(ln_step.sem, lnm["out", i])
            if i:
                pe.wait_ge(h_lo, 2 * i)
            for c in range(DC):
                mm = pe.transpose(bank[:, 4 + c // 4, (c % 4) * P:(c % 4) * P + rows(i)], h1[0:rows(i), i, c * P:(c + 1) * P],
                                  ident[0:rows(i), 0:rows(i)])
                if c % 4 == 3:
                    mm.then_inc(h_turned, 1)

        def turned_h(i, k):
            return bank[:, 4 + k, :].rearrange("p (c n) -> p c n", n=P)[:, :, 0:rows(i)]

        def low_h(dve, i):
            for k in range(2):
                dve.wait_ge(h_hi, 2 * i + k + 1)
                hi, lo = (x[:, 4 * k:4 * k + 4, i * P:i * P + rows(i)] for x in hh)
                dve.tensor_tensor(lo, turned_h(i, k), hi.bitcast(F32), ALU.subtract).then_inc(h_lo, 1)

        def dve_out(dve):
            dve.wait_ge(ln_in, 32)
            act_ssd.wait(dve, QT, "last_kept")
            for i in range(TILES):
                def loaded(i=i):
                    dve.wait_ge(xres_in[i % 2], 16 * (i // 2 + 1))
                    dve.wait_ge(mixed, i + 1)
                    return xres[0:rows(i), i % 2]
                layer_norm(dve, i, i, h1[0:rows(i), i], lng, lnb, bank[0:rows(i), 2 * (i % 2):2 * (i % 2) + 2, :], loaded)
                if i:
                    low_h(dve, i - 1)
            low_h(dve, QT)

        def act_out(act):
            for i in range(TILES):
                act_root(act, i, i)
                for k in range(2):
                    act.wait_ge(h_turned, 2 * i + k + 1)
                    act.copy(hh[0][:, 4 * k:4 * k + 4, i * P:i * P + rows(i)], turned_h(i, k)).then_inc(h_hi, 1)

        QF = 2 * PH
        qT, skT = cut(66, 2, TOK), cut(74, 2, P)
        uraw = [overlay(at, DC, P) for at in (75, 79, 159, 163)]
        us = overlay(84, 4, DC, P, kind=F32R), overlay(50, 4, DC, P, kind=F32R)
        u_in, u_hi, u_lo = [sem(f"u_in{s}") for s in range(4)], sem("u_hi"), sem("u_lo")
        sall = cut(10, TILES, QF, PK)
        skT_in = sem("skT_in")
        q_ready, q_kept, s_ready, s_kept = (sem(n) for n in ("q_ready", "q_kept", "s_ready", "s_kept"))
        sall_zeroed = sem("sall_zeroed")

        def sp_query(sp):
            sp.dma_start(skT, t["peer_keys"]).then_inc(skT_in, 16)
            for s in range(4):
                sp.dma_start(uraw[s], t["peer_wq"][s]).then_inc(u_in[s], 16)
            for s in range(4):
                copy_cache(sp, 1, 12 + s)
            with sp.Fori(1, QF // 4) as k:
                for s in range(4):
                    sp.wait_ge(u_lo, k * 4 + (s - 3))
                    sp.dma_start(uraw[s], t["peer_wq"][bass.ds(k * 4 + s, 1)].rearrange("f p c n -> p (f c) n")).then_inc(u_in[s], 16)

        def hi_of(act, s, q):
            act.wait_ge(u_in[s], q * 16 + 16)
            act.copy(us[0][:, s], uraw[s]).then_inc(u_hi, 1)

        def pool_query(pool):
            pool.sem_inc(v_lo, 4)
            pool.wait_ge(mixed, TILES)
            pool.memset(sall[:, QT], 0.0).then_inc(sall_zeroed, 1)
            with pool.Fori(0, (QF + PK) // 4) as x:
                for s in range(4):
                    pool.wait_ge(u_hi, x * 4 + (s + 1))
                    pool.tensor_tensor(us[1][:, s], uraw[s], us[0][:, s].bitcast(F32), ALU.subtract).then_inc(u_lo, 1)

        def pe_query(pe):
            pe.wait_ge(h_lo, 2 * TILES)
            pe.wait_ge(skT_in, 16)
            pe.wait_ge(ln_step.sem, lnm["out", QT])
            pe.sem_inc(s_ready, 2)

            def query(f, s):
                pe.wait_ge(u_lo, f + 1)
                pe.wait_ge(q_kept, f + 1)
                for half in range(2):
                    for c in range(DC):
                        mm = product(pe, bank[:, 2 * (s % 2) + half, 0:HALF], [w[:, s, c] for w in us],
                                     [h[:, c, half * HALF:(half + 1) * HALF] for h in hh], c == 0, c == DC - 1)
                mm.then_inc(q_ready, 1)

            def score(f, s):
                pe.wait_ge(q_kept, f + 3)
                pe.wait_ge(s_kept, f * 2 + 2)
                for i in range(TILES):
                    mm = pe.matmul(bank[0:rows(i), 4 + 2 * (s % 2) + i // QT, (i % QT) * P:(i % QT + 1) * P],
                                   qT[:, s % 2, i * P:i * P + rows(i)], skT[:, s % 2], start=True, stop=True)
                mm.then_inc(s_ready, 1)

            with pe.Fori(0, QF // 4) as k:
                for s in range(5):
                    if s < 4:
                        query(k * 4 + s, s)
                    if s:
                        score(k * 4 + (s - 1), s - 1)

        def act_query(act):
            act.sem_inc(q_kept, 2)
            act.wait_ge(mixed, TILES)
            for s in range(4):
                hi_of(act, s, 0)
            with act.Fori(0, QF // 4) as k:
                for s in range(4):
                    f = k * 4 + s
                    act.wait_ge(q_ready, f + 1)
                    act.wait_ge(s_ready, f + 1)
                    act.copy(qT[:, s % 2].rearrange("p (h n) -> p h n", h=2), bank[:, 2 * (s % 2):2 * (s % 2) + 2, 0:HALF]).then_inc(q_kept, 1)
                    hi_of(act, s, k + 1)

        def dve_query(dve):
            dve.sem_inc(s_kept, 4)
            dve.wait_ge(sall_zeroed, 1)
            with dve.Fori(0, QF // 4) as k:
                for s in range(4):
                    f = k * 4 + s
                    dve.wait_ge(s_ready, f + 3)
                    dve.tensor_copy(sall[:, 0:QT, bass.ds(f, 1)].rearrange("p i o n -> p i (o n)"),
                                    bank[:, 4 + 2 * (s % 2), :].rearrange("p (i n) -> p i n", n=P)).then_inc(s_kept, 1)
                    dve.tensor_copy(sall[0:NS, QT, bass.ds(f, 1)].rearrange("p o n -> p (o n)"), bank[0:NS, 5 + 2 * (s % 2), 0:P]).then_inc(s_kept, 1)

        K8 = 8
        sc, sv = cut(100, QF, PK), cut(108, QF, TOPK)
        su = cut(109, QF, TOPK).bitcast(U32)
        si = cut(110, QF, TOPK)
        cand = cut(111, PH, TOPK, TOPK)
        cv, cu, ca = cut(119, PH, TOPK), cut(119.5, PH, TOPK).bitcast(U32), cut(120, PH, TOPK).bitcast(U32)
        caf = cut(120.5, 2, PH, TOPK)
        cb_ = cut(121.5, PH, TOPK).bitcast(U32)
        hot = cut(122, PH, TOPK, TOPK)
        chosen = cut(130, 3, PH * TOPK)
        hsum, hrec = cut(131.5, PH), cut(131.6, PH)
        slotT = cut(133, 3, TILES * P)
        TOP = 12 * QF // 2
        picked, gate_exp, ch_turned, ch_kept = sem("picked"), sem("gate_exp"), sem("ch_turned"), sem("ch_kept")
        topk = Steps(sem("topk"))
        PER_TILE = 1 + 5 * QF + 2 + 5 * PH + 5 + 2 * 3 + 3
        cv2 = cut(132, PH, TOPK)

        def dve_topk(dve):
            step = topk
            dve.wait_ge(s_kept, 2 * QF + 4)
            NEGBIG = -3.0e38
            fences = []
            with dve.Fori(0, TILES) as i:
                step.enter(i, PER_TILE)
                step(dve.tensor_copy(sc, sall[:, bass.ds(i, 1)].rearrange("p o f n -> p (o f) n")))
                step.wait(dve)

                def fence():
                    step.wait(dve)
                    fences.append(0)
                    dve.memset(small(900 + len(fences), 1), 0.0)

                def top16(values, width, out_v, out_i, n):
                    for k in range(2):
                        fence()
                        for f in range(n):
                            step(dve.max(out_v(f, k), values(f)))
                        fence()
                        for f in range(n):
                            step(dve.max_index(out_i(f, k), out_v(f, k), values(f)))
                        if k == 0:
                            fence()
                            for f in range(n):
                                step(dve.match_replace(values(f), out_v(f, k), values(f), NEGBIG))

                top16(lambda f: sc[:, f], PK, lambda f, k: sv[:, f, K8 * k:K8 * k + K8], lambda f, k: su[:, f, K8 * k:K8 * k + K8], QF)
                step.wait(dve)
                step(dve.tensor_copy(si, su))
                v = sv.rearrange("p (h s) k -> p h s k", s=2)
                step(dve.tensor_tensor(cand, v[:, :, 0].unsqueeze(3).to_broadcast([P, PH, TOPK, TOPK]),
                                       v[:, :, 1].unsqueeze(2).to_broadcast([P, PH, TOPK, TOPK]), ALU.add))
                step.wait(dve)
                flat = cand.rearrange("p h a b -> p h (a b)")
                top16(lambda f: flat[:, f], TOPK * TOPK, lambda f, k: cv[:, f, K8 * k:K8 * k + K8],
                      lambda f, k: cu[:, f, K8 * k:K8 * k + K8], PH)
                step.wait(dve)
                step(dve.tensor_scalar(ca, cu, 4, None, ALU.logical_shift_right))
                step(dve.tensor_scalar(cb_, cu, 15, None, ALU.bitwise_and))
                step.wait(dve)
                step(dve.tensor_copy(caf[:, 0], ca))
                step(dve.tensor_copy(caf[:, 1], cb_))
                step(dve.tensor_tensor(cv2, cv, cv[:, :, 0:1].to_broadcast([P, PH, TOPK]), ALU.subtract))
                after["shifted"] = step.outer + step.n
                step.wait(dve)
                dve.wait_ge(ch_turned, i + 1)
                iv = si.rearrange("p (h s) k -> p h s k", s=2)
                for side in range(2):
                    step(dve.tensor_tensor(hot, caf[:, side].unsqueeze(3).to_broadcast([P, PH, TOPK, TOPK]),
                                           const("iota")[:, 0:TOPK].unsqueeze(1).unsqueeze(1).to_broadcast([P, PH, TOPK, TOPK]), ALU.is_equal))
                    step.wait(dve)
                    step(dve.tensor_tensor(hot, hot, iv[:, :, side].unsqueeze(2).to_broadcast([P, PH, TOPK, TOPK]), ALU.mult))
                    step.wait(dve)
                    step(dve.tensor_reduce(chosen[:, side].rearrange("p (h k) -> p h k", k=TOPK), hot, AX.X, ALU.add))
                    step.wait(dve)
                dve.wait_ge(gate_exp, i + 1)
                step(dve.tensor_reduce(hsum, cv2, AX.X, ALU.add))
                step.wait(dve)
                step(dve.reciprocal(hrec, hsum))
                step.wait(dve)
                step(dve.tensor_tensor(chosen[:, 2].rearrange("p (h k) -> p h k", k=TOPK), cv2,
                                       hrec.unsqueeze(2).to_broadcast([P, PH, TOPK]), ALU.mult))
                step.wait(dve)
            step.leave(TILES)
        AHEAD = 12
        EARLY, SLABS = AHEAD * TILES, TOK // SLAB
        assert EARLY + SLABS * GRP == PK
        slab = [cut(10, PK, SLAB), cut(26, PK, SLAB)]
        aring = cut(66, 4, TOK)
        hot_a, hot_b = cut(100, 2, 4, P), cut(104, 2, 4, P)
        a_stored = [sem(f"a_stored{s}") for s in range(4)]
        u_done, gelu_done = sem("u_done"), sem("gelu_done")
        hot_ready, g_done, g_kept = (sem(n) for n in ("hot_ready", "g_done", "g_kept"))
        slab_stored = [sem(f"slab_stored{s}") for s in range(2)]
        GS = SLAB // 4
        GROUPS = PK // GRP

        def sp_up(sp):
            for s in range(4):
                sp.sem_inc(a_stored[s], 16)
            for s in range(2):
                sp.sem_inc(slab_stored[s], 16)

            def fetch(a, s):
                sp.wait_ge(u_lo, a + (QF - 3))
                sp.dma_start(uraw[s], t["peer_u"][bass.ds(a, 1)].rearrange("a p c n -> p (a c) n")).then_inc(u_in[s], 16)

            def keep(a, s, g):
                sp.wait_ge(gelu_done, a + 3)
                sp.dma_start(t["act"][bass.ds(g, 1), :, s].rearrange("g p n -> p (g n)"), aring[:, s]).then_inc(a_stored[s], 16)

            for s in range(4):
                fetch(s, s)
            with sp.Fori(0, EARLY // 4) as x:
                for s in range(4):
                    fetch(x * 4 + (s + 4), s)
                    keep(x * 4 + s, s, x)

            def keep_slab(n, s):
                sp.wait_ge(g_kept, n * GS + (GS + 2))
                sp.dma_start(t["gate"][bass.ds(n, 1)].rearrange("s p a n -> p (s a) n"), slab[s]).then_inc(slab_stored[s], 16)

            def last_rows(n, more=True):
                for s in range(4):
                    if more:
                        fetch(n * 4 + (EARLY + s + 4), s)
                    keep(n * 4 + (EARLY + s), s, n + EARLY // 4)

            last_rows(0)
            sp_first_group(sp)
            with sp.Fori(0, (SLABS - 3) // 2) as x:
                for s in range(2):
                    keep_slab(x * 2 + s, s)
                    last_rows(x * 2 + (s + 1))
            for n in range(SLABS - 3, SLABS):
                keep_slab(n, n % 2)
                if n < SLABS - 1:
                    last_rows(n + 1, n + 1 < SLABS - 1)

        def act_up(act):
            act.wait_ge(s_ready, QF + 2)
            act.sem_inc(ch_kept, 1)
            act.sem_inc(gelu_done, 2)
            act.sem_inc(g_kept, 2)

            def gelu(a, s, q):
                act.wait_ge(u_done, a + 1)
                act.wait_ge(a_stored[s], q * 16 + 16)
                act.activation(aring[:, s].rearrange("p (h n) -> p h n", h=2), bank[:, 2 * (s % 2):2 * (s % 2) + 2, 0:HALF],
                               ACT.Gelu).then_inc(gelu_done, 1)

            with act.Fori(0, TILES) as i:
                for n in range(AHEAD):
                    a, q = i * AHEAD + n, i * (AHEAD // 4) + n // 4
                    gelu(a, n % 4, q)
                    hi_of(act, n % 4, q + (QF // 4 + 1))
                    if n == AHEAD - 3:
                        act.wait_ge(topk.sem, i * PER_TILE + after["shifted"])
                        act.activation(cv2, cv2, ACT.Exp).then_inc(gate_exp, 1)
                act.wait_ge(ch_turned, i + 2)
                act.copy(slotT[:, :, bass.ds(i * P, P)], bank[:, 6, 0:3 * P].rearrange("p (j n) -> p j n", j=3)).then_inc(ch_kept, 1)

            def last_rows(n, sl, more=True):
                for s in range(4):
                    a, q = n * 4 + (EARLY + s), n + EARLY // 4
                    gelu(a, s, q)
                    if more:
                        hi_of(act, s, q + (QF // 4 + 1))
                    for par in range(2):
                        act.wait_ge(g_done, n * GS + (2 * s + par + 3))
                        act.copy(slab[sl][:, :, 8 * s + 4 * par:8 * s + 4 * par + 4].rearrange("p a n -> p n a"),
                                 bank[:, 4 + par, :].rearrange("p (n a) -> p n a", a=P)).then_inc(g_kept, 1)

            with act.Fori(0, (SLABS - 1) // 2) as x:
                for sl in range(2):
                    act.wait_ge(slab_stored[sl], x * 16 + 16)
                    last_rows(x * 2 + sl, sl)
            act.wait_ge(slab_stored[(SLABS - 1) % 2], 16 * (SLABS // 2 + 1))
            last_rows(SLABS - 1, (SLABS - 1) % 2, False)


        def pe_up(pe):
            pe.sem_inc(ch_turned, 1)
            pe.sem_inc(g_done, 2)
            pe.wait_ge(q_kept, QF + 2)
            pe.wait_ge(s_kept, 2 * QF + 4)

            def up(a, s):
                pe.wait_ge(u_lo, a + (QF + 1))
                pe.wait_ge(gelu_done, a + 1)
                for half in range(2):
                    for c in range(DC):
                        mm = product(pe, bank[:, 2 * (s % 2) + half, 0:HALF], [w[:, s, c] for w in us],
                                     [h[:, c, half * HALF:(half + 1) * HALF] for h in hh], c == 0, c == DC - 1)
                mm.then_inc(u_done, 1)

            with pe.Fori(0, TILES) as i:
                for n in range(AHEAD):
                    up(i * AHEAD + n, n % 4)
                pe.wait_ge(topk.sem, i * PER_TILE + PER_TILE)
                pe.wait_ge(ch_kept, i + 1)
                for j in range(3):
                    mm = pe.transpose(bank[:, 6, j * P:(j + 1) * P], chosen[:, j], ident)
                mm.then_inc(ch_turned, 1)
            pe.wait_ge(ch_kept, TILES + 1)
            with pe.Fori(0, SLABS) as n:
                for s in range(4):
                    up(n * 4 + (EARLY + s), s)
                    for par in range(2):
                        w = n * GS + (2 * s + par)
                        pe.wait_ge(hot_ready, w + 1)
                        pe.wait_ge(g_kept, w + 1)
                        for j in range(4):
                            mm = pe.matmul(bank[:, 4 + par, j * P:(j + 1) * P], hot_b[:, par, j], hot_a[:, par, j], start=True, stop=True)
                        mm.then_inc(g_done, 1)

        def dve_onehots(dve):
            dve.sem_inc(weighted, 8)
            dve.wait_ge(ch_kept, TILES + 1)
            with dve.Fori(0, TOK // 8) as x:
                for par in range(2):
                    w = x * 2 + par
                    dve.wait_ge(g_done, w + 1)
                    for j in range(4):
                        at = lambda row: slotT[:, row, bass.ds(w * 4 + j, 1)]
                        dve.tensor_scalar(hot_a[:, par, j], const("iota"), at(0), None, ALU.is_equal)
                        last = dve.tensor_scalar(hot_b[:, par, j], const("iota"), at(1), at(2), ALU.is_equal, ALU.mult)
                    last.then_inc(hot_ready, 1)

        acc = cut(10, DC, TOK)
        ga = overlay(27, 8, TOK, kind=F32R), overlay(44, 8, TOK, kind=F32R)
        agrp = [cut(at, GRP, TOK) for at in (124, 93)]
        ggrp = [cut(at, GRP * TOK) for at in (164.5, 173)]
        vraw, vs = overlay(108, 4, D), (overlay(61, 8, D, kind=F32R), overlay(132.5, 8, D, kind=F32R))
        prod = overlay(181.5, 2, TOK)
        a_in, gate_in = [sem(f"a_in{s}") for s in range(2)], [sem(f"gate_in{s}") for s in range(2)]
        vraw_in = [sem(f"vraw_in{s}") for s in range(4)]
        v_hi, v_lo, ga_hi, ga_lo, weighted, vp_done, added, acc_zeroed = (
            sem(n) for n in ("v_hi", "v_lo", "ga_hi", "ga_lo", "weighted", "vp_done", "added", "acc_zeroed"))

        def sp_rows(sp, x, par, k):
            a = x * 8 + (par * GRP + k)
            sp.wait_ge(v_lo, a + 1)
            sp.dma_start(vraw[:, k], t["peer_v"][bass.ds(a, 1)].rearrange("a p n -> p (a n)")).then_inc(vraw_in[k], 16)

        def sp_gelus(sp, x, par):
            g = x * 2 + par
            sp.wait_ge(weighted, g * GRP + 4)
            sp.dma_start(agrp[par], t["act"][bass.ds(g, 1)].rearrange("g p k n -> p (g k) n")).then_inc(a_in[par], 16)

        def sp_gates(sp, x, par):
            g = x * 2 + par
            sp.dma_start(ggrp[par].rearrange("p (s a n) -> p s (a n)", a=GRP, n=SLAB),
                         t["gate"].rearrange("s p a n -> p s (a n)")[:, :, bass.ds(g * (GRP * SLAB), GRP * SLAB)])\
                .then_inc(gate_in[par], 16)

        def sp_first_group(sp):
            sp.wait_ge(ch_kept, TILES + 1)
            for s in range(4):
                sp.wait_ge(a_stored[s], 32)
            sp_gelus(sp, 0, 0)
            for k in range(GRP):
                sp_rows(sp, 0, 0, k)

        def sp_values(sp):
            for s in range(2):
                sp.wait_ge(slab_stored[s], 16 * (1 + (SLABS + 1 - s) // 2))
            for s in range(4):
                sp.wait_ge(a_stored[s], 16 * (GROUPS + 1))
            sp_gates(sp, 0, 0)

            def group(x, par):
                sp_gelus(sp, x, par)
                sp_gates(sp, x, par)
                for k in range(GRP):
                    sp_rows(sp, x, par, k)

            group(0, 1)
            with sp.Fori(1, GROUPS // 2) as x:
                for par in range(2):
                    group(x, par)
            sp.wait_ge(copied, 16 * 32)

        def pool_values_lo(pool):
            pool.wait_ge(u_done, PK)
            with pool.Fori(0, PK // 8) as x:
                for j in range(8):
                    pool.wait_ge(v_hi, x * 8 + (j + 1))
                    pool.tensor_tensor(vs[1][:, j], vraw[:, j % GRP], vs[0][:, j].bitcast(F32), ALU.subtract).then_inc(v_lo, 1)

        def act_values(act):
            for s in range(4):
                act.wait_ge(a_stored[s], 16 * (GROUPS + 1))
            with act.Fori(0, GROUPS // 2) as x:
                for j in range(8):
                    par, k = j // GRP, j % GRP
                    if k == 0:
                        act.wait_ge(vp_done, x * (2 * DC) + (par * DC + DC))
                    act.wait_ge(vraw_in[k], x * 32 + (16 * par + 16))
                    act.copy(vs[0][:, j], vraw[:, k]).then_inc(v_hi, 1)
                    act.wait_ge(weighted, x * 8 + (j + 9))
                    act.copy(ga[0][:, j], prod[:, j % 2]).then_inc(ga_hi, 1)

        def pe_values(pe):
            pe.sem_inc(vp_done, 2 * DC)
            pe.wait_ge(gelu_done, PK + 2)
            pe.wait_ge(g_kept, SLABS * GS + 2)
            with pe.Fori(0, GROUPS // 2) as x:
                for par in range(2):
                    g = x * 2 + par
                    pe.wait_ge(ga_lo, g * GRP + (GRP + 2))
                    pe.wait_ge(v_lo, g * GRP + (GRP + 4))
                    for c in range(DC):
                        pe.wait_ge(added, g * DC + (c + 5))
                        for half in range(2):
                            for k in range(GRP):
                                j = par * GRP + k
                                mm = product(pe, bank[:, 2 * (c % 4) + half, 0:HALF], [v[:, j, c * P:(c + 1) * P] for v in vs],
                                             [w[:, j, half * HALF:(half + 1) * HALF] for w in ga], k == 0, k == GRP - 1)
                        mm.then_inc(vp_done, 1)

        def dve_values(dve):
            dve.sem_inc(added, 8)
            dve.sem_inc(ga_lo, 2)
            dve.wait_ge(slab_stored[0], 16 * (2 + SLABS // 2))
            dve.wait_ge(slab_stored[1], 16 * (1 + SLABS // 2))
            dve.wait_ge(u_done, PK)
            dve.memset(acc, 0.0).then_inc(acc_zeroed, 1)
            dve.wait_ge(acc_zeroed, 1)

            def weigh(g2, par, g):
                def times(k):
                    if k == 0:
                        dve.wait_ge(a_in[par], g2 * 16 + 16)
                        dve.wait_ge(gate_in[par], g2 * 16 + 16)
                    dve.wait_ge(ga_lo, g * GRP + (k + 1))
                    dve.tensor_tensor(prod[:, k % 2].rearrange("p (s n) -> p s n", n=SLAB),
                                      agrp[par][:, k].rearrange("p (s n) -> p s n", n=SLAB),
                                      ggrp[par].rearrange("p (s a n) -> p s a n", a=GRP, n=SLAB)[:, :, k], ALU.mult).then_inc(weighted, 1)

                def low(k):
                    dve.wait_ge(ga_hi, g * GRP + (k + 1))
                    j = par * GRP + k
                    dve.tensor_tensor(ga[1][:, j], prod[:, k % 2], ga[0][:, j].bitcast(F32), ALU.subtract).then_inc(ga_lo, 1)

                times(0)
                for k in range(1, GRP):
                    times(k)
                    low(k - 1)
                low(GRP - 1)

            def add(g2, par, g):
                for c in range(DC):
                    dve.wait_ge(vp_done, g * DC + (c + 17))
                    dve.wait_ge(added, g * DC + (c + 1))
                    v = acc[:, c].rearrange("p (h n) -> p h n", h=2)
                    dve.tensor_tensor(v, v, bank[:, 2 * (c % 4):2 * (c % 4) + 2, 0:HALF], ALU.add).then_inc(added, 1)

            weigh(0, 0, 0)
            with dve.Fori(0, GROUPS // 2 - 1) as x:
                weigh(x, 1, x * 2 + 1)
                add(x, 0, x * 2)
                weigh(x + 1, 0, x * 2 + 2)
                add(x, 1, x * 2 + 1)
            x = GROUPS // 2 - 1
            weigh(x, 1, 2 * x + 1)
            add(x, 0, 2 * x)
            add(x, 1, 2 * x + 1)

        ln2_in, o_turned, y_stored = sem("ln2_in"), sem("o_turned"), [sem(f"y_stored{s}") for s in range(2)]

        def sp_final(sp):
            sp.wait_ge(vp_done, (GROUPS + 2) * DC)
            sp.dma_start(lng, t["ln2_g"]).then_inc(ln2_in, 16)
            sp.dma_start(lnb, t["ln2_b"]).then_inc(ln2_in, 16)
            for i in range(TILES):
                sp.wait_ge(ln_step.sem, lnm["out", TILES + i])
                s = (TILES + i) % 2
                sp.dma_start(t["o_y"][i * P:i * P + rows(i)], xres[0:rows(i), s]).then_inc(y_stored[s], 16)
            sp.wait_ge(y_stored[1], 48)
            sp.wait_ge(y_stored[0], 32)

        def pe_final(pe):
            pe.wait_ge(added, GROUPS * DC + 8)
            for i in range(TILES):
                if i >= 2:
                    pe.wait_ge(ln_step.sem, lnm["sum", TILES + i - 2])
                for c in range(DC):
                    mm = pe.transpose(bank[0:rows(i), 2 * (i % 2) + c // 4, (c % 4) * P:(c % 4 + 1) * P], acc[:, c, i * P:i * P + rows(i)], ident)
                mm.then_inc(o_turned, 1)

        def dve_final(dve):
            dve.wait_ge(ln2_in, 32)
            for i in range(TILES):
                def loaded(i=i):
                    dve.wait_ge(o_turned, i + 1)
                    if i >= 2:
                        dve.wait_ge(y_stored[(TILES + i) % 2], 16 * (i // 2))
                    return h1[0:rows(i), i]
                layer_norm(dve, TILES + i, i, xres[0:rows(i), (TILES + i) % 2], lng, lnb, bank[0:rows(i), 2 * (i % 2):2 * (i % 2) + 2, :], loaded)

        def act_final(act):
            for i in range(TILES):
                act_root(act, TILES + i, i)
        @block.vector
        def _(dve):
            dve.sem_inc(feat_kept, 2)
            dve.sem_inc(rows_kept, 2)
            dve_split_x(dve)
            dve_project(dve)
            dve_attend(dve)
            dve_samples(dve)
            dve_ssd_run(dve)
            dve_out(dve)
            dve_query(dve)
            dve_topk(dve)
            dve_onehots(dve)
            dve_values(dve)
            dve_final(dve)

        @block.scalar
        def _(act):
            act.sem_inc(silu_done, 1)
            act_consts(act)
            act_project(act)
            act_attend(act)
            act_samples(act)
            act_ssd_run(act)
            act_out(act)
            act_query(act)
            act_up(act)
            act_values(act)
            act_final(act)

        @block.gpsimd
        def _(pool):
            pool_project(pool)
            pool_stage(pool)
            pool_qdiag0(pool)
            pool_ssd_run(pool)
            pool_query(pool)
            pool_values_lo(pool)

        @block.tensor
        def _(pe):
            pe_project(pe)
            pe_attend(pe)
            pe_samples(pe)
            pe_ssd_run(pe)
            pe_out(pe)
            pe_query(pe)
            pe_up(pe)
            pe_values(pe)
            pe_final(pe)

        @block.sync
        def _(sp):
            sp_project(sp)
            sp_states(sp)
            sp_bias(sp)
            sp_samples(sp)
            sp_ssd(sp)
            sp_dump5(sp)
            sp_out(sp)
            sp_query(sp)
            sp_up(sp)
            sp_values(sp)
            sp_final(sp)
            sp.wait_ge(stored, stores[0])


def lay_out(a):
    f = {k: np.asarray(v) for k, v in a.items()}
    tok = np.concatenate([f["x_prompt"].reshape(SEQ, D), f["x_sample"].reshape(NS, D)], 0)
    w = f["w_in"][0]
    blocks = lambda m: m.reshape(DC, P, m.shape[1] // P, P).transpose(2, 1, 0, 3)
    qkv_z = np.concatenate([w[:, 4 * D:4 * D + XF * P], w[:, 0:2 * D], w[:, 2 * D:4 * D]], 1)
    across = lambda v: np.broadcast_to(v[None, :], (P, v.shape[0]))
    perseq = lambda m, n: m.transpose(2, 0, 1).reshape(n, P, -1).transpose(1, 0, 2)
    ins = {
        "consts": CONST_TABLE,
        "x": tok,
        "xT": tok.T.reshape(DC, P, TOK).transpose(1, 0, 2),
        "w_in": blocks(qkv_z),
        "w_dt": w[:, -H:].reshape(DC, P, H).transpose(1, 0, 2),
        "state_conv": perseq(f["state_conv"][0], XF),
        "conv_w": f["conv_w"][0].reshape(XF, P, CW).transpose(1, 0, 2),
        "conv_b": f["conv_b"][0].reshape(XF, P).T,
        "dt_bias": across(f["dt_bias"][0]), "a_log": across(f["a_log"][0]), "d_skip": across(f["d_skip"][0]),
        "prompt_bias": PROMPT_BIAS, "sample_bias": SAMPLE_BIAS,
        "cache_kT": f["cache_k"][0][:, sample_positions()].transpose(0, 2, 3, 1).reshape(NB, DC, P, KEYS),
        "cache_v": f["cache_v"][0][:, sample_positions()].reshape(NB, KB, P, D),
        "ssm_norm_g": across(f["ssm_norm_g"][0]),
        "state_ssm": f["state_ssm"][0].transpose(0, 3, 1, 2).reshape(NB, N, D),
        "w_out": f["w_out"][0].reshape(16, P, D).transpose(1, 0, 2),
        "ln1_g": across(f["ln1_g"][0]), "ln1_b": across(f["ln1_b"][0]),
        "peer_wq": blocks(f["peer_wq"][0]), "peer_keys": f["peer_keys"][0].transpose(2, 0, 1),
        "peer_u": f["peer_u"][0].reshape(PK, PK, DC, P).transpose(0, 3, 2, 1),
        "peer_v": f["peer_v"][0].reshape(PK, PK, D),
        "ln2_g": across(f["ln2_g"][0]), "ln2_b": across(f["ln2_b"][0]),
        "cache_k": f["cache_k"][0].reshape(NB, WIN, D), "cache_vall": f["cache_v"][0].reshape(NB, WIN, D),
    }
    return {k: np.ascontiguousarray(v) for k, v in ins.items()}


OUTS = {
    "o_kT": (P, 8, TOK), "o_conv": (P, XF, 3), "o_ext": (P, XF, NB * 7), "o_v": (SEQ, D), "o_vs": (NS, D),
    "o_hp": (N, D), "o_hs": (NB, N, D),
    "o_ks": (NB, WIN, D), "o_vsall": (NB, WIN, D), "o_y": (TOK, D),
}


def kernel(**inputs):
    import concourse.bacc as bacc
    from concourse.bass_utils import run_bass_kernel_spmd as run

    nc = bacc.Bacc("TRN2", target_bir_lowering=False, num_devices=1)
    ins = lay_out(inputs)
    t = {k: nc.dram_tensor(k, v.shape, F32, kind="ExternalInput").ap() for k, v in ins.items()}
    t.update({k: nc.dram_tensor(k, s, F32, kind="ExternalOutput").ap() for k, s in OUTS.items()})
    t["gate"] = nc.dram_tensor("gate", (TOK // SLAB, P, PK, SLAB), F32, kind="Internal").ap()
    t["act"] = nc.dram_tensor("act", (PK // GRP, P, GRP, TOK), F32, kind="Internal").ap()
    layer(nc, t)
    r = run(nc, [ins], core_ids=[0]).results[0]
    kT = r["o_kT"].transpose(2, 1, 0).reshape(TOK, H, E)
    k_prompt = kT[:SEQ][None, None]
    v_prompt = r["o_v"].reshape(1, 1, SEQ, H, E)
    conv_prompt = r["o_conv"].transpose(2, 1, 0).reshape(1, 1, 3, XF * P)
    ext = r["o_ext"].reshape(P, XF, NB, 7).transpose(2, 3, 1, 0).reshape(NB, 7, XF * P)
    conv_sample = ext[None, :, 4:]
    h_prompt = r["o_hp"].reshape(N, H, E).transpose(1, 2, 0)[None, None]
    h_sample = r["o_hs"].reshape(NB, N, H, E).transpose(0, 2, 3, 1)[None]
    y = r["o_y"]
    return (y[:SEQ].reshape(1, SEQ, D), y[SEQ:].reshape(NB, NT, D), k_prompt, v_prompt, conv_prompt, h_prompt,
            r["o_ks"].reshape(1, NB, WIN, H, E), r["o_vsall"].reshape(1, NB, WIN, H, E), conv_sample, h_sample)
```
